# Optimizing a Trainium2 kernel written in Bass

```python
import math
import jax, jax.numpy as jnp
from jax import lax
import numpy as np
import jax
import jax.numpy as jnp

D_MODEL = 1024
BATCH = 1
SEQ = 1024
DEPTH = 1

PLE_DIM = 256
D_RG = D_MODEL // 2
RG_BLOCKS = 8
RG_BLOCK = D_RG // RG_BLOCKS
CONV_WIDTH = 4
RG_C = 8.0
D_HG = D_MODEL // 2
HG_HEAD_DIM = 128
HG_HEADS = D_HG // HG_HEAD_DIM
HG_CHUNK = 64
D_MIX = D_RG + D_HG
D_IN = 2 * D_RG + 4 * D_HG
EPS = 1e-6


def rms_norm(x, w):
    xf = x.astype(jnp.float32)
    y = xf * lax.rsqrt(jnp.mean(xf * xf, axis=-1, keepdims=True) + EPS)
    return (y * w.astype(jnp.float32)).astype(x.dtype)

def causal_depthwise_conv(x, w, b):
    T = x.shape[1]
    xp = jnp.pad(x, ((0, 0), (CONV_WIDTH - 1, 0), (0, 0)))
    y = b
    for j in range(CONV_WIDTH):
        y = y + xp[:, j:j + T] * w[j]
    return y

def rg_lru(x, wa, ba, wx, bx, lam):
    B, T, _ = x.shape
    xf = x.astype(jnp.float32)
    xb = xf.reshape(B, T, RG_BLOCKS, RG_BLOCK)
    r = jax.nn.sigmoid(jnp.einsum('btgi,gij->btgj', xb, wa.astype(jnp.float32)).reshape(B, T, D_RG) + ba)
    i = jax.nn.sigmoid(jnp.einsum('btgi,gij->btgj', xb, wx.astype(jnp.float32)).reshape(B, T, D_RG) + bx)
    log_a = -RG_C * r * jax.nn.softplus(-lam.astype(jnp.float32))
    a = jnp.exp(log_a)
    mult = jnp.sqrt(-jnp.expm1(2.0 * log_a))
    mult = jnp.where(jnp.arange(T)[None, :, None] == 0, 1.0, mult)
    u = mult * (i * xf)

    def combine(left, right):
        a_l, b_l = left
        a_r, b_r = right
        return a_l * a_r, a_r * b_l + b_r

    _, h = lax.associative_scan(combine, (a, u), axis=1)
    return h.astype(x.dtype)

def gla_chunked(q, k, logf, v):
    B, T, H, K = q.shape
    V = v.shape[-1]
    C = HG_CHUNK
    N = T // C

    def chunks(t):
        return t.reshape(B, N, C, H, t.shape[-1]).transpose(0, 3, 1, 2, 4)

    q, k, logf, v = chunks(q), chunks(k), chunks(logf), chunks(v)
    b = jnp.cumsum(logf, axis=3)
    b_last = b[:, :, :, -1:, :]
    qe = q * jnp.exp(b)
    ke = k * jnp.exp(-b)
    scores = jnp.einsum('bhnck,bhnsk->bhncs', qe, ke)
    causal = jnp.tril(jnp.ones((C, C), dtype=bool))
    scores = jnp.where(causal, scores, 0.0)
    o_intra = jnp.einsum('bhncs,bhnsv->bhncv', scores, v)

    kd = k * jnp.exp(b_last - b)
    dS = jnp.einsum('bhnsk,bhnsv->bhnkv', kd, v)
    decay = jnp.exp(b_last[:, :, :, 0, :])

    def step(S, inp):
        d, ds = inp
        return d[..., None] * S + ds, S

    S0 = jnp.zeros((B, H, K, V), jnp.float32)
    _, S_prev = lax.scan(step, S0, (jnp.moveaxis(decay, 2, 0), jnp.moveaxis(dS, 2, 0)))
    o_inter = jnp.einsum('bhnck,nbhkv->bhncv', qe, S_prev)
    o = o_intra + o_inter
    return o.transpose(0, 2, 3, 1, 4).reshape(B, T, H, V)

def hgrn2_branch(q, fz, iv, g, lb, norm_w):
    B, T, _ = q.shape
    qf, fzf, ivf, gf = (t.astype(jnp.float32) for t in (q, fz, iv, g))
    lb = lb.astype(jnp.float32)
    f = lb + (1.0 - lb) * jax.nn.sigmoid(fzf)
    logf = jnp.log(f)
    k = (1.0 - lb) * jax.nn.sigmoid(-fzf)
    qs = jax.nn.silu(qf) * (HG_HEAD_DIM ** -0.5)
    heads = lambda t: t.reshape(B, T, HG_HEADS, HG_HEAD_DIM)
    o = gla_chunked(heads(qs), heads(k), heads(logf), heads(ivf))
    o = o * lax.rsqrt(jnp.mean(o * o, axis=-1, keepdims=True) + EPS) * norm_w.astype(jnp.float32)
    o = o.reshape(B, T, D_HG) * jax.nn.silu(gf)
    return o.astype(q.dtype)

def first_inputs(seed: int = 0) -> dict:
    key = jax.random.key(seed)
    ks = jax.random.split(key, 20)
    f32 = jnp.float32
    nrm = lambda k, shape, scale: scale * jax.random.normal(k, shape, f32)
    u = jax.random.uniform(ks[10], (DEPTH, D_RG), f32, minval=0.9, maxval=0.999)
    s = u ** (1.0 / RG_C)
    rg_lambda = jnp.log(s) - jnp.log1p(-s)
    return {
        "x": jax.random.normal(ks[0], (BATCH, SEQ, D_MODEL), f32),
        "p": jax.random.normal(ks[1], (DEPTH, BATCH, SEQ, PLE_DIM), f32),
        "norm_mix_w": 1.0 + nrm(ks[2], (DEPTH, D_MODEL), 0.1),
        "w_in": nrm(ks[3], (DEPTH, D_MODEL, D_IN), D_MODEL ** -0.5),
        "conv_w": nrm(ks[4], (DEPTH, CONV_WIDTH, D_RG), CONV_WIDTH ** -0.5),
        "conv_b": nrm(ks[5], (DEPTH, D_RG), 0.01),
        "rg_wa": nrm(ks[6], (DEPTH, RG_BLOCKS, RG_BLOCK, RG_BLOCK), RG_BLOCK ** -0.5),
        "rg_ba": nrm(ks[7], (DEPTH, D_RG), 0.1),
        "rg_wx": nrm(ks[8], (DEPTH, RG_BLOCKS, RG_BLOCK, RG_BLOCK), RG_BLOCK ** -0.5),
        "rg_bx": nrm(ks[9], (DEPTH, D_RG), 0.1),
        "rg_lambda": rg_lambda,
        "hg_lb": nrm(ks[11], (DEPTH + 1, D_HG), 0.1),
        "hg_norm_w": 1.0 + nrm(ks[12], (DEPTH, HG_HEAD_DIM), 0.1),
        "w_out": nrm(ks[13], (DEPTH, D_MIX, D_MODEL), D_MIX ** -0.5),
        "ple_norm_w": 1.0 + nrm(ks[14], (DEPTH, D_MODEL), 0.1),
        "w_ple_gate": nrm(ks[15], (DEPTH, D_MODEL, D_MODEL), D_MODEL ** -0.5),
        "b_ple_gate": nrm(ks[16], (DEPTH, D_MODEL), 0.1),
        "w_ple_proj": nrm(ks[17], (DEPTH, PLE_DIM, D_MODEL), PLE_DIM ** -0.5),
        "final_norm_w": 1.0 + nrm(ks[18], (D_MODEL,), 0.1),
    }

def first_block(x, p, norm_mix_w, w_in, conv_w, conv_b, rg_wa, rg_ba, rg_wx, rg_bx,
              rg_lambda, hg_lb, hg_norm_w, w_out, ple_norm_w, w_ple_gate, b_ple_gate,
              w_ple_proj, final_norm_w):
    lb_all = jnp.cumsum(jax.nn.softmax(hg_lb.astype(jnp.float32), axis=0), axis=0)
    split_at = [D_RG, 2 * D_RG, 2 * D_RG + D_HG, 2 * D_RG + 2 * D_HG, 2 * D_RG + 3 * D_HG]
    h = x
    for l in range(DEPTH):
        u = rms_norm(h, norm_mix_w[l])
        proj = u @ w_in[l]
        xa, ga, qb, fb, ib, gb = jnp.split(proj, split_at, axis=-1)
        xa = causal_depthwise_conv(xa, conv_w[l], conv_b[l])
        ya = rg_lru(xa, rg_wa[l], rg_ba[l], rg_wx[l], rg_bx[l], rg_lambda[l]) * jax.nn.silu(ga)
        yb = hgrn2_branch(qb, fb, ib, gb, lb_all[l], hg_norm_w[l])
        h = h + jnp.concatenate([ya, yb], axis=-1) @ w_out[l]
        gate = jax.nn.sigmoid(rms_norm(h, ple_norm_w[l]) @ w_ple_gate[l] + b_ple_gate[l])
        h = h + gate * (p[l] @ w_ple_proj[l])
    return rms_norm(h, final_norm_w)


GLA_HEADS = 4
GLA_DK = D_MODEL // 16
GLA_DV = D_MODEL // 8
GLA_RANK = 16
GLA_GATE_NORM = 16.0
ML_HEADS = 4
ML_DK = D_MODEL // 16
ML_DV = D_MODEL // 8
ML_CONV = 4
S5_GROUP = 16
S5_WIDTH = D_MODEL // 2
S5_GROUPS = S5_WIDTH // S5_GROUP
S5_STATE = 64
S5_DT_MIN = 0.001
S5_DT_MAX = 0.1
CHUNK = 64
FFN_HIDDEN = ((8 * D_MODEL + 767) // 768) * 256
N_BRANCH = 3
RMS_EPS = 1e-6

IN_SIZES = (
    GLA_HEADS * GLA_DK,
    GLA_HEADS * GLA_DK,
    GLA_HEADS * GLA_DV,
    GLA_RANK,
    GLA_HEADS * GLA_DV,
    ML_HEADS * ML_DK,
    ML_HEADS * ML_DK,
    ML_HEADS * ML_DV,
    ML_HEADS,
    ML_HEADS,
    ML_HEADS * ML_DV,
    S5_WIDTH,
    N_BRANCH * D_MODEL,
)
IN_DIM = sum(IN_SIZES)


def rms_norm_2(x, w):
    xf = x.astype(jnp.float32)
    y = xf * lax.rsqrt(jnp.mean(xf * xf, axis=-1, keepdims=True) + RMS_EPS)
    return (y * w.astype(jnp.float32)).astype(x.dtype)

def _split(z, sizes):
    out, start = [], 0
    for s in sizes:
        out.append(z[..., start:start + s])
        start += s
    return out

def _heads(a, n):
    return a.reshape(a.shape[0], a.shape[1], n, -1)

def _to_chunks(a):
    b, t, h, d = a.shape
    return a.reshape(b, t // CHUNK, CHUNK, h, d).transpose(1, 0, 3, 2, 4)

def _from_chunks(a):
    n, b, h, l, d = a.shape
    return a.transpose(1, 0, 3, 2, 4).reshape(b, n * l, h, d)

def gla_attention(q, k, v, g):
    out_dtype = v.dtype
    f32 = jnp.float32
    bsz, _, heads, dk = q.shape
    dv = v.shape[-1]
    qc, kc, vc, gc = (_to_chunks(a.astype(f32)) for a in (q * dk ** -0.5, k, v, g))
    causal = jnp.tril(jnp.ones((CHUNK, CHUNK), dtype=bool))

    def step(state, inp):
        qi, ki, vi, gi = inp
        cum = jnp.cumsum(gi, axis=2)
        o_inter = jnp.einsum('bhld,bhdv->bhlv', qi * jnp.exp(cum), state)
        rel = cum[:, :, :, None, :] - cum[:, :, None, :, :]
        decay = jnp.exp(jnp.where(causal[:, :, None], rel, -jnp.inf))
        scores = jnp.einsum('bhid,bhjd,bhijd->bhij', qi, ki, decay)
        o = o_inter + jnp.einsum('bhij,bhjv->bhiv', scores, vi)
        last = cum[:, :, -1:, :]
        state = (jnp.exp(last[:, :, 0, :])[..., None] * state
                 + jnp.einsum('bhjd,bhjv->bhdv', ki * jnp.exp(last - cum), vi))
        return state, o

    s0 = jnp.zeros((bsz, heads, dk, dv), f32)
    _, o = lax.scan(step, s0, (qc, kc, vc, gc))
    return _from_chunks(o).astype(out_dtype)

def mlstm_memory(q, k, v, i_pre, f_pre):
    out_dtype = v.dtype
    f32 = jnp.float32
    bsz, _, heads, dk = q.shape
    dv = v.shape[-1]
    log_f = jax.nn.log_sigmoid(f_pre.astype(f32))
    qc, kc, vc = (_to_chunks(a.astype(f32)) for a in (q, k * dk ** -0.5, v))
    ic, fc = (_to_chunks(a.astype(f32)[..., None])[..., 0] for a in (i_pre, log_f))
    causal = jnp.tril(jnp.ones((CHUNK, CHUNK), dtype=bool))

    def step(carry, inp):
        mem, norm, m_prev = carry
        qi, ki, vi, ii, lfi = inp
        b = jnp.cumsum(lfi, axis=-1)
        a_inter = b + m_prev[..., None]
        d_intra = jnp.where(causal, b[..., :, None] - b[..., None, :] + ii[..., None, :], -jnp.inf)
        m_t = jnp.maximum(a_inter, jnp.max(d_intra, axis=-1))
        w_inter = jnp.exp(a_inter - m_t)
        scores = jnp.einsum('bhtd,bhsd->bhts', qi, ki) * jnp.exp(d_intra - m_t[..., None])
        num = (w_inter[..., None] * jnp.einsum('bhtd,bhdv->bhtv', qi, mem)
               + jnp.einsum('bhts,bhsv->bhtv', scores, vi))
        den = w_inter * jnp.einsum('bhtd,bhd->bht', qi, norm) + jnp.sum(scores, axis=-1)
        h = num / jnp.maximum(jnp.abs(den), jnp.exp(-m_t))[..., None]
        m_new = m_t[..., -1]
        carry_decay = jnp.exp(b[..., -1] + m_prev - m_new)
        w_key = jnp.exp(b[..., -1:] - b + ii - m_new[..., None])
        mem = carry_decay[..., None, None] * mem + jnp.einsum('bhs,bhsd,bhsv->bhdv', w_key, ki, vi)
        norm = carry_decay[..., None] * norm + jnp.einsum('bhs,bhsd->bhd', w_key, ki)
        return (mem, norm, m_new), h

    carry0 = (jnp.zeros((bsz, heads, dk, dv), f32),
              jnp.zeros((bsz, heads, dk), f32),
              jnp.zeros((bsz, heads), f32))
    _, h = lax.scan(step, carry0, (qc, kc, vc, ic, fc))
    return _from_chunks(h).astype(out_dtype)

def _complex_linear_combine(earlier, later):
    a1r, a1i, b1r, b1i = earlier
    a2r, a2i, b2r, b2i = later
    return (a2r * a1r - a2i * a1i,
            a2r * a1i + a2i * a1r,
            a2r * b1r - a2i * b1i + b2r,
            a2r * b1i + a2i * b1r + b2i)

def s5_ssm(u, lam_re, lam_im, log_step, b_re, b_im, c_re, c_im, d_skip):
    out_dtype = u.dtype
    f32 = jnp.float32
    bsz, t, _ = u.shape
    uf = u.astype(f32).reshape(bsz, t, S5_GROUPS, S5_GROUP)
    lam_re = jnp.minimum(lam_re.astype(f32), -1e-4)
    lam_im = lam_im.astype(f32)
    dt = jnp.exp(log_step.astype(f32))[:, None]
    mag = jnp.exp(lam_re * dt)
    abar_re = mag * jnp.cos(lam_im * dt)
    abar_im = mag * jnp.sin(lam_im * dt)
    inv = 1.0 / (lam_re * lam_re + lam_im * lam_im)
    z_re = ((abar_re - 1.0) * lam_re + abar_im * lam_im) * inv
    z_im = (abar_im * lam_re - (abar_re - 1.0) * lam_im) * inv
    b_re = b_re.astype(f32)
    b_im = b_im.astype(f32)
    bbar_re = z_re[..., None] * b_re - z_im[..., None] * b_im
    bbar_im = z_re[..., None] * b_im + z_im[..., None] * b_re
    bu_re = jnp.einsum('gpc,btgc->btgp', bbar_re, uf)
    bu_im = jnp.einsum('gpc,btgc->btgp', bbar_im, uf)
    a_re = jnp.broadcast_to(abar_re, (1, t) + abar_re.shape)
    a_im = jnp.broadcast_to(abar_im, (1, t) + abar_im.shape)
    _, _, x_re, x_im = lax.associative_scan(_complex_linear_combine, (a_re, a_im, bu_re, bu_im), axis=1)
    y = (jnp.einsum('gcp,btgp->btgc', c_re.astype(f32), x_re)
         - jnp.einsum('gcp,btgp->btgc', c_im.astype(f32), x_im))
    y = y.reshape(bsz, t, S5_WIDTH) + d_skip.astype(f32) * u.astype(f32)
    return y.astype(out_dtype)

def causal_dwconv(u, w, b):
    k = w.shape[0]
    y = lax.conv_general_dilated(u, w[:, None, :], window_strides=(1,), padding=[(k - 1, 0)],
                                 dimension_numbers=('NWC', 'WIO', 'NWC'),
                                 feature_group_count=u.shape[-1])
    return y + b

def hybrid_mixer(h, w_in, gla_a2, gla_a_b, gla_norm_w, ml_conv_w, ml_conv_b, ml_i_b, ml_f_b,
                 s5_lam_re, s5_lam_im, s5_log_step, s5_b_re, s5_b_im, s5_c_re, s5_c_im, s5_d,
                 s5_glu_w, s5_glu_b, proj_gla, proj_ml, proj_s5, branch_gate_b, w_out):
    bsz, t, _ = h.shape
    z = h @ w_in
    gq, gk, gv, ga, gr, mq, mk, mv, mi, mf, mo, su, zg = _split(z, IN_SIZES)

    g_log = jax.nn.log_sigmoid((ga @ gla_a2 + gla_a_b).astype(jnp.float32)) / GLA_GATE_NORM
    o_gla = gla_attention(_heads(gq, GLA_HEADS), _heads(gk, GLA_HEADS), _heads(gv, GLA_HEADS),
                          _heads(g_log, GLA_HEADS))
    o_gla = rms_norm_2(o_gla, gla_norm_w.reshape(GLA_HEADS, GLA_DV)).reshape(bsz, t, -1)
    y_gla = o_gla * jax.nn.silu(gr)

    qk = jax.nn.silu(causal_dwconv(jnp.concatenate([mq, mk], axis=-1), ml_conv_w, ml_conv_b))
    mq = qk[..., :ML_HEADS * ML_DK]
    mk = qk[..., ML_HEADS * ML_DK:]
    h_ml = mlstm_memory(_heads(mq, ML_HEADS), _heads(mk, ML_HEADS), _heads(mv, ML_HEADS),
                        mi + ml_i_b, mf + ml_f_b)
    y_ml = jax.nn.sigmoid(mo) * h_ml.reshape(bsz, t, -1)

    y_s5 = jax.nn.gelu(s5_ssm(su, s5_lam_re, s5_lam_im, s5_log_step, s5_b_re, s5_b_im,
                              s5_c_re, s5_c_im, s5_d))
    y_s5 = y_s5 * jax.nn.sigmoid(y_s5 @ s5_glu_w + s5_glu_b)

    gates = jax.nn.sigmoid(zg + branch_gate_b).reshape(bsz, t, N_BRANCH, D_MODEL)
    merged = (gates[:, :, 0] * (y_gla @ proj_gla)
              + gates[:, :, 1] * (y_ml @ proj_ml)
              + gates[:, :, 2] * (y_s5 @ proj_s5))
    return merged @ w_out

def swiglu_ffn(h, w_in, w_out):
    gate, up = jnp.split(h @ w_in, 2, axis=-1)
    return (jax.nn.silu(gate) * up) @ w_out

def second_inputs(seed: int = 0) -> dict:
    key = jax.random.key(seed)
    keys = list(jax.random.split(key, 48))

    def normal(shape, scale):
        return scale * jax.random.normal(keys.pop(), shape, jnp.float32)

    def uniform(shape):
        return jax.random.uniform(keys.pop(), shape, jnp.float32)

    def gain(shape):
        return 1.0 + normal(shape, 0.05)

    L, D = DEPTH, D_MODEL
    glw = GLA_HEADS * GLA_DV
    mlw = ML_HEADS * ML_DV
    n_idx = jnp.arange(S5_STATE, dtype=jnp.float32)
    log_lo, log_hi = math.log(S5_DT_MIN), math.log(S5_DT_MAX)
    return {
        'x': normal((BATCH, SEQ, D), 1.0),
        'c': normal((BATCH, D), 1.0),
        'ada_w': normal((L, D, 6 * D), 0.1 * D ** -0.5),
        'ada_b': normal((L, 6 * D), 0.01),
        'pre1_w': gain((L, D)),
        'post1_w': gain((L, D)),
        'pre2_w': gain((L, D)),
        'post2_w': gain((L, D)),
        'w_in': normal((L, D, IN_DIM), D ** -0.5),
        'gla_a2': normal((L, GLA_RANK, GLA_HEADS * GLA_DK), GLA_RANK ** -0.5),
        'gla_a_b': normal((L, GLA_HEADS * GLA_DK), 0.1),
        'gla_norm_w': gain((L, glw)),
        'ml_conv_w': normal((L, ML_CONV, 2 * ML_HEADS * ML_DK), ML_CONV ** -0.5),
        'ml_conv_b': normal((L, 2 * ML_HEADS * ML_DK), 0.01),
        'ml_i_b': normal((L, ML_HEADS), 0.1),
        'ml_f_b': 3.0 + 3.0 * uniform((L, ML_HEADS)),
        's5_lam_re': -0.5 + normal((L, S5_GROUPS, S5_STATE), 0.01),
        's5_lam_im': math.pi * n_idx + normal((L, S5_GROUPS, S5_STATE), 0.01),
        's5_log_step': log_lo + (log_hi - log_lo) * uniform((L, S5_GROUPS)),
        's5_b_re': normal((L, S5_GROUPS, S5_STATE, S5_GROUP), (2 * S5_GROUP) ** -0.5),
        's5_b_im': normal((L, S5_GROUPS, S5_STATE, S5_GROUP), (2 * S5_GROUP) ** -0.5),
        's5_c_re': normal((L, S5_GROUPS, S5_GROUP, S5_STATE), S5_STATE ** -0.5),
        's5_c_im': normal((L, S5_GROUPS, S5_GROUP, S5_STATE), S5_STATE ** -0.5),
        's5_d': normal((L, S5_WIDTH), 1.0),
        's5_glu_w': normal((L, S5_WIDTH, S5_WIDTH), S5_WIDTH ** -0.5),
        's5_glu_b': normal((L, S5_WIDTH), 0.01),
        'proj_gla': normal((L, glw, D), glw ** -0.5),
        'proj_ml': normal((L, mlw, D), mlw ** -0.5),
        'proj_s5': normal((L, S5_WIDTH, D), S5_WIDTH ** -0.5),
        'branch_gate_b': normal((L, N_BRANCH * D), 0.01),
        'w_out': normal((L, D, D), D ** -0.5),
        'ffn_w_in': normal((L, D, 2 * FFN_HIDDEN), D ** -0.5),
        'ffn_w_out': normal((L, FFN_HIDDEN, D), FFN_HIDDEN ** -0.5),
    }

def second_block(x, c, ada_w, ada_b, pre1_w, post1_w, pre2_w, post2_w, w_in, gla_a2, gla_a_b,
              gla_norm_w, ml_conv_w, ml_conv_b, ml_i_b, ml_f_b, s5_lam_re, s5_lam_im, s5_log_step,
              s5_b_re, s5_b_im, s5_c_re, s5_c_im, s5_d, s5_glu_w, s5_glu_b, proj_gla, proj_ml,
              proj_s5, branch_gate_b, w_out, ffn_w_in, ffn_w_out):
    c_act = jax.nn.silu(c)
    for l in range(DEPTH):
        mod = c_act @ ada_w[l] + ada_b[l]
        sh1, sc1, gt1, sh2, sc2, gt2 = [m[:, None, :] for m in jnp.split(mod, 6, axis=-1)]

        h = rms_norm_2(x, pre1_w[l]) * (1.0 + sc1) + sh1
        y = hybrid_mixer(h, w_in[l], gla_a2[l], gla_a_b[l], gla_norm_w[l], ml_conv_w[l], ml_conv_b[l],
                         ml_i_b[l], ml_f_b[l], s5_lam_re[l], s5_lam_im[l], s5_log_step[l],
                         s5_b_re[l], s5_b_im[l], s5_c_re[l], s5_c_im[l], s5_d[l], s5_glu_w[l],
                         s5_glu_b[l], proj_gla[l], proj_ml[l], proj_s5[l], branch_gate_b[l], w_out[l])
        x = x + (1.0 + gt1) * rms_norm_2(y, post1_w[l])

        h = rms_norm_2(x, pre2_w[l]) * (1.0 + sc2) + sh2
        y = swiglu_ffn(h, ffn_w_in[l], ffn_w_out[l])
        x = x + (1.0 + gt2) * rms_norm_2(y, post2_w[l])
    return x


def setup_inputs(seed=0):
    out = dict(first_inputs(seed))
    for name, value in second_inputs(seed + 1).items():
        if name != "x":
            out[name + "_2"] = value
    return out


def reference(
    x, p, norm_mix_w, w_in, conv_w, conv_b, rg_wa, rg_ba, rg_wx, rg_bx, rg_lambda, hg_lb,
    hg_norm_w, w_out, ple_norm_w, w_ple_gate, b_ple_gate, w_ple_proj, final_norm_w, c_2,
    ada_w_2, ada_b_2, pre1_w_2, post1_w_2, pre2_w_2, post2_w_2, w_in_2, gla_a2_2, gla_a_b_2,
    gla_norm_w_2, ml_conv_w_2, ml_conv_b_2, ml_i_b_2, ml_f_b_2, s5_lam_re_2, s5_lam_im_2,
    s5_log_step_2, s5_b_re_2, s5_b_im_2, s5_c_re_2, s5_c_im_2, s5_d_2, s5_glu_w_2, s5_glu_b_2,
    proj_gla_2, proj_ml_2, proj_s5_2, branch_gate_b_2, w_out_2, ffn_w_in_2, ffn_w_out_2,
):
    x = first_block(
        x, p, norm_mix_w, w_in, conv_w, conv_b, rg_wa, rg_ba, rg_wx, rg_bx, rg_lambda, hg_lb,
        hg_norm_w, w_out, ple_norm_w, w_ple_gate, b_ple_gate, w_ple_proj, final_norm_w,
    )
    return second_block(
        x, c_2, ada_w_2, ada_b_2, pre1_w_2, post1_w_2, pre2_w_2, post2_w_2, w_in_2, gla_a2_2,
        gla_a_b_2, gla_norm_w_2, ml_conv_w_2, ml_conv_b_2, ml_i_b_2, ml_f_b_2, s5_lam_re_2,
        s5_lam_im_2, s5_log_step_2, s5_b_re_2, s5_b_im_2, s5_c_re_2, s5_c_im_2, s5_d_2,
        s5_glu_w_2, s5_glu_b_2, proj_gla_2, proj_ml_2, proj_s5_2, branch_gate_b_2, w_out_2,
        ffn_w_in_2, ffn_w_out_2,
    )


_drawn_inputs = setup_inputs


def setup_inputs(seed=0):
    import zlib

    import numpy as np

    out = dict(_drawn_inputs(seed))
    spreads = {}
    factors = {'rg_ba': 5.196,
     'rg_bx': 4.227,
     'hg_lb': 6.891,
     'ml_conv_b_2': 6.219,
     'ml_i_b_2': 8.0,
     's5_lam_re_2': 200.0,
     's5_glu_b_2': 35.106,
     'branch_gate_b_2': 8.0,
     's5_lam_im_2': 35.84,
     's5_log_step_2': 37.832,
     's5_b_re_2': 49.328,
     's5_b_im_2': 49.328,
     's5_c_re_2': 48.128,
     's5_c_im_2': 49.16}
    for name, (base, spread) in spreads.items():
        noise = np.random.default_rng([zlib.crc32(name.encode()), seed]).standard_normal(out[name].shape)
        drawn = base * np.exp(spread * noise) if base else spread * noise
        out[name] = jnp.asarray(drawn.astype(out[name].dtype))
    for name, factor in factors.items():
        out[name] = (out[name] * factor).astype(out[name].dtype)
    return out
```

```python
import concourse.bass as bass
from concourse import mybir

F32 = mybir.dt.float32
F32R = mybir.dt.float32r
ALU = mybir.AluOpType
ACT = mybir.ActivationFunctionType
ds = bass.ds

P = 128
D = 1024
T = 1024
KB = D // P
EPS = 1e-6
SBUF_BASE = 16512
BLOCK = T * 4
CH = 64
NCH = T // CH
TT = T // P
PI = 3.1415925
TURN_INV = 0.15915494309189535
ROUND = 1.5 * 2 ** 23
TURN = (6.28125, 0.0019350051879882812, 3.019916050e-07)

VEC_SPEC = [
    ("norm_mix_w", 8), ("conv_w", 16), ("conv_b", 4), ("rg_ba", 4), ("rg_bx", 4), ("rg_lambda", 4),
    ("hg_lb", 8), ("hg_norm_w", 1), ("ple_norm_w", 8), ("b_ple_gate", 8), ("final_norm_w", 8),
    ("ada_b", 48), ("pre1_w", 8), ("post1_w", 8), ("pre2_w", 8), ("post2_w", 8), ("gla_a_b", 2),
    ("gla_norm_w", 4), ("ml_conv_w", 16), ("ml_conv_b", 4), ("ml_if_b", 1), ("s5_d", 4), ("glu_b", 4),
    ("branch_b", 24),
]
VEC_MADE = [
    ("zero", 8), ("eps", 1), ("one", 1), ("rg_s8", 4), ("neg_rg_s8", 4), ("lb", 4), ("one_minus_lb", 4), ("tmp", 24), ("pre1_g", 8),
    ("post1_g", 8), ("pre2_g", 8), ("post2_g", 8),
]


def columns(spec, at=0):
    found = {}
    for name, n in spec:
        found[name] = at
        at += n
    return found, at


VEC, N_VEC = columns(VEC_SPEC)
VEC_ON_CHIP, N_VEC_ALL = columns(VEC_MADE, N_VEC)
VEC.update(VEC_ON_CHIP)

STREAM = [
    ("rg_w", 8, (8, 8)), ("hg_w", 16, (8, 8)), ("out1_w", 8, (8, 8)), ("ple_w", 8, (2, 2)),
    ("gate_w", 8, (8, 8)), ("misc_w", 2, (4, 4)), ("gla_w", 12, (8, 8)), ("ml_w", 12, (8, 8)),
    ("s5_w", 4, (8, 8)), ("glu_w", 4, (4, 4)), ("mix0", 48, (8, 4)), ("mix1", 48, (8, 4)),
    ("out2_w", 8, (8, 8)), ("up0", 44, (8, 8)), ("down0", 24, (8, 8)), ("up1", 44, (8, 8)),
    ("down1", 24, (8, 8)),
]
SOURCE = {"mix0": ("zg_w", "proj_w"), "mix1": ("zg_w", "proj_w"), "up0": ("up_w",) * 2,
          "up1": ("up_w",) * 2, "down0": ("down_w",) * 2, "down1": ("down_w",) * 2}
TILE0, N_TILES = columns([(name, n) for name, n, _ in STREAM])
UNIT0, N_UNITS = columns([
    ("rg_w", 8), ("hg_w", 16), ("out1_w", 8), ("ple_w", 8), ("gate_w", 8), ("misc_w", 2), ("gla_w", 12),
    ("ml_w", 12), ("s5_w", 4), ("glu_w", 4), ("mix0", 24), ("mix1", 24), ("out2_w", 8), ("up0", 22),
    ("down0", 4), ("up1", 22), ("down1", 4)])


def program(nc, dram, out, debug=None):
    def sb(name, blocks, shape, dt=F32):
        return nc.alloc_sbuf_tensor_at(name, [P, *shape], dt, offset=SBUF_BASE + int(blocks * BLOCK))

    def sem(name):
        return nc.alloc_semaphore(name)

    H = sb("H", 0, [8, T])
    UH = sb("UH", 8, [8, T], F32R)
    UL = sb("UL", 16, [8, T], F32R)
    WRAW = sb("WRAW", 24, [2, T])
    WH = sb("WH", 26, [2, T], F32R)
    WL = sb("WL", 28, [2, T], F32R)
    WK = sb("WK", 30, [20, T])
    ADA = sb("ADA", 47, [3, T])
    consts = [SBUF_BASE + 50 * BLOCK]

    def const(name, shape):
        t = nc.alloc_sbuf_tensor_at(name, [P, *shape], F32, offset=consts[0])
        n = 4
        for k in shape:
            n *= k
        consts[0] += n
        return t

    ONES = const("ONES", [P])
    IDENT = const("IDENT", [P])
    NEGMASK = const("NEGMASK", [P])
    MASK = const("MASK", [CH])
    RESET = const("RESET", [T])
    C_ROW = WK[:, 16, :]
    ML_AT = 768
    A2W = WK[0:16, 19, 768:1024]
    SEL = WK[:, 19, 0:768]
    YH = sb("YH", 30, [12, 512], F32R)
    YL = sb("YL", 36, [12, 512], F32R)
    RESP = 768
    GH = sb("GH", 30, [4, T], F32R)
    GLO = sb("GLO", 34, [4, T], F32R)
    HH = sb("HH", 30, [22, 512], F32R)
    HL1 = sb("HL1", 0, [16, 512], F32R)
    HL2 = sb("HL2", 41, [6, 512], F32R)
    YF = [sb("YF0", 44, [8, 512]), sb("YF1", 16, [8, 512])]
    XR = sb("XR", 8, [8, T])
    h_save = nc.dram_tensor("h_save", [D, T], F32, kind="Internal").ap()
    TOUCH = const("TOUCH", [8])
    MOD = const("MOD", [48])
    CONST_V = const("CONST_V", [N_VEC_ALL])
    PH = sb("PH", 45, [2, T], F32R)
    PL = sb("PL", 47, [2, T], F32R)
    PG = nc.alloc_psum_tensor("PG", [P, 4, 512], F32)
    PX = nc.alloc_psum_tensor("PX", [P, 4, 512], F32)

    def vec(name, j=0):
        return CONST_V[:, VEC[name] + j:VEC[name] + j + 1]

    def vec_at(name, i):
        return CONST_V[:, ds(i + VEC[name], 1)]

    def vecs(name, n):
        return CONST_V[:, VEC[name]:VEC[name] + n]

    def wk(s, n=1):
        return WK[:, s:s + n, :].rearrange("p a t -> p (a t)")

    vec_loaded = sem("vec_loaded")
    x_loaded = sem("x_loaded")
    c_loaded = sem("c_loaded")
    bd_loaded = sem("bd_loaded")
    w_loaded = [sem(f"w_loaded{r}") for r in range(2)]
    ada_loaded = [sem(f"ada_loaded{r}") for r in range(3)]
    w_split = sem("w_split")
    tile_done = sem("tile_done")
    slot_free = [sem(f"slot_free{s}") for s in range(2)]
    ada_done = sem("ada_done")
    consts_made = sem("consts_made")
    pre_dve = sem("pre_dve")
    pre_act = sem("pre_act")
    norm_sq = sem("norm_sq")
    norm_acc = sem("norm_acc")
    norm_ms = sem("norm_ms")
    norm_rs = sem("norm_rs")
    norm_t = sem("norm_t")
    norm_hi = sem("norm_hi")
    norm_lo = sem("norm_lo")
    rg_w_copied = sem("rg_w_copied")
    rg_conv = sem("rg_conv")
    rg_gates = sem("rg_gates")
    rg_sig = sem("rg_sig")
    rg_decay = sem("rg_decay")
    rg_q = sem("rg_q")
    rg_mult = sem("rg_mult")
    rg_done = sem("rg_done")
    out_saved = sem("out_saved")
    debug_saved = sem("debug_saved")
    la_names = (
        "sig", "logf", "gaps", "exps", "kd", "keys", "turned", "turned_copied", "scores", "attn", "ds", "state",
        "o", "sq", "ms", "rs", "y", "free")
    hg = {n: sem(f"hg_{n}") for n in la_names}
    gl = {n: sem(f"gla_{n}") for n in la_names}
    sp_hi = sem("sp_hi")
    sp_lo = sem("sp_lo")
    ple_hi = sem("ple_hi")
    ple_ready = sem("ple_ready")
    rg_ogate = sem("rg_ogate")
    gate_added = sem("gate_added")
    gate_sig = sem("gate_sig")
    h_reloaded = sem("h_reloaded")
    p_loaded = sem("p_loaded")
    h_saved = sem("h_saved")
    small_loaded = sem("small_loaded")
    gains_made = sem("gains_made")
    misc_out = sem("misc_out")
    gla_a2 = sem("gla_a2")
    gla_x = sem("gla_x")
    gla_ln = sem("gla_ln")
    gla_copied = sem("gla_copied")
    gla_done = sem("gla_done")
    m = {n: sem(f"ml_{n}") for n in (
        "rows", "ln", "gates", "exps", "turned_rows", "tok", "conv_in", "conv", "silu", "in", "free", "spread",
        "spread_used", "kw", "turned", "turned_copied", "ds", "state", "decay_in", "scores", "e", "p", "num", "h",
        "ht", "y")}
    s5 = {n: sem(f"s5_{n}") for n in (
        "loaded", "dt", "angle", "trig", "g", "resp", "resp_copied", "kt", "kt_copied", "gt", "gt_copied", "tok",
        "tok_copied", "u", "u_copied", "v", "x", "y", "y_copied", "back", "pre_gelu")}
    glu_hi = sem("glu_hi")
    glu_lo = sem("glu_lo")
    glu_sig = sem("glu_sig")
    glu_y = sem("glu_y")
    mix_hi = sem("mix_hi")
    mix_lo = sem("mix_lo")
    mix_sig = sem("mix_sig")
    m_ready = sem("m_ready")
    x_reloaded = sem("x_reloaded")
    ffn_silu = sem("ffn_silu")
    ffn_t = sem("ffn_t")
    ffn_hi = sem("ffn_hi")
    ffn_lo = sem("ffn_lo")

    def S5P(k):
        return WK[:, 14, 16 * k:16 * k + 16]

    def slot(s):
        return PG[:, 2 * s:2 * s + 2, :].rearrange("p b t -> p (b t)")

    def aux(b, n=2):
        return PX[:, b:b + n, :].rearrange("p b t -> p (b t)")

    block = nc.Block()
    with block:
        @block.sync
        def _(sp):
            def weight_pair(name, pair):
                _, n, kbs = next(s for s in STREAM if s[0] == name)
                t0 = TILE0[name]
                sources = SOURCE.get(name)
                for j in range(2):
                    if t0 or not isinstance(pair, int) or pair:
                        sp.wait_ge(w_split, pair * 2 + (t0 + j - 1))
                    if sources and sources[0] != sources[1]:
                        src = dram[sources[j]][ds(pair, 1)]
                    else:
                        src = dram[sources[0] if sources else name][ds(pair * 2 + j, 1)]
                    sp.dma_start(WRAW[:, j, 0:kbs[j] * P], src.rearrange("a p c -> (a p) c")
                                 ).then_inc(w_loaded[j], 16)

            def ada_tiles(first, n):
                for j in range(n):
                    if not isinstance(first, int) or first + j >= 3:
                        sp.wait_ge(ada_done, first + (j - 3 + 1))
                    sp.dma_start(ADA[:, j % 3, :], dram["ada_w"][ds(first + j, 1)].rearrange("a p c -> (a p) c")
                                 ).then_inc(ada_loaded[j % 3], 16)

            sp.dma_start(CONST_V[:, 0:N_VEC], dram["vec"]).then_inc(vec_loaded, 16)
            sp.dma_start(C_ROW, dram["c_row"]).then_inc(c_loaded, 16)
            for j in range(KB):
                sp.dma_start(H[:, j, :], dram["x"][j * P:(j + 1) * P, :]).then_inc(x_loaded, 16)
            sp.dma_start(WK[:, 14, :], dram["rg_bd"]).then_inc(bd_loaded, 16)
            weight_pair("rg_w", 0)
            ada_tiles(0, 3)
            with sp.Fori(1, 4) as i:
                weight_pair("rg_w", i)
                ada_tiles(i * 3, 3)
            with sp.Fori(0, 4) as i:
                weight_pair("hg_w", i * 2)
                weight_pair("hg_w", i * 2 + 1)
                ada_tiles(i * 9 + 12, 9)
            weight_pair("out1_w", 0)
            sp.wait_ge(sp_lo, 8)
            for j in range(KB):
                sp.dma_start(H[:, j, :], dram["x"][j * P:(j + 1) * P, :]).then_inc(h_reloaded, 16)
            with sp.Fori(1, 4) as i:
                weight_pair("out1_w", i)
            for j in range(2):
                if j:
                    sp.wait_ge(ple_ready, 1)
                sp.dma_start(WK[:, 19, :], dram["p"][j * P:(j + 1) * P, :]).then_inc(p_loaded, 16)
            with sp.Fori(0, 4) as i:
                weight_pair("ple_w", i)
            with sp.Fori(0, 4) as i:
                weight_pair("gate_w", i)

            weight_pair("misc_w", 0)
            sp.wait_ge(norm_lo, 8 * 3)
            sp.dma_start(A2W, dram["gla_a2"]).then_inc(small_loaded, 16)
            sp.dma_start(SEL, dram["sel"]).then_inc(small_loaded, 16)
            for j in range(KB):
                sp.dma_start(h_save[j * P:(j + 1) * P, :], H[:, j, :]).then_inc(h_saved, 16)
            with sp.Fori(0, 6) as i:
                weight_pair("gla_w", i)
            with sp.Fori(0, 3) as i:
                weight_pair("ml_w", i)
            sp.wait_ge(m["gates"], 1)
            sp.dma_start(WK[:, 15, :], dram["s5_bc"]).then_inc(s5["loaded"], 16)
            sp.dma_start(WK[:, 14, 0:48], dram["s5_lam"]).then_inc(s5["loaded"], 16)
            with sp.Fori(3, 6) as i:
                weight_pair("ml_w", i)
            weight_pair("s5_w", 0)
            weight_pair("s5_w", 1)
            weight_pair("glu_w", 0)
            weight_pair("glu_w", 1)
            for name in ("mix0", "mix1"):
                with sp.Fori(0, 24) as i:
                    weight_pair(name, i)
            weight_pair("out2_w", 0)
            sp.wait_ge(sp_lo, 16)
            for j in range(KB):
                sp.dma_start(H[:, j, :], h_save[j * P:(j + 1) * P, :]).then_inc(h_reloaded, 16)
            with sp.Fori(1, 4) as i:
                weight_pair("out2_w", i)
            weight_pair("up0", 0)
            sp.wait_ge(norm_lo, 8 * 5)
            for j in range(KB):
                sp.dma_start(h_save[j * P:(j + 1) * P, :], H[:, j, :]).then_inc(h_saved, 16)
            with sp.Fori(1, 22) as i:
                weight_pair("up0", i)
            with sp.Fori(0, 12) as i:
                weight_pair("down0", i)
            with sp.Fori(0, 22) as i:
                weight_pair("up1", i)
            weight_pair("down1", 0)
            sp.wait_ge(tile_done, TILE0["down1"])
            for j in range(KB):
                sp.dma_start(XR[:, j, :], h_save[j * P:(j + 1) * P, :]).then_inc(x_reloaded, 16)
            with sp.Fori(1, 12) as i:
                weight_pair("down1", i)
            for j in range(KB):
                sp.wait_ge(norm_lo, 8 * 6 + j + 1)
                sp.dma_start(out[j * P:(j + 1) * P, :], XR[:, j, :]).then_inc(out_saved, 16)
            sp.wait_ge(out_saved, 16 * KB)

        @block.gpsimd
        def _(pool):
            pool.memset(ONES[:], 1.0)
            pool.memset(IDENT[:], 0.0)
            pool.memset(NEGMASK[:], 0.0)
            pool.memset(MASK[:], 1.0)
            pool.memset(RESET[:], 1.0)
            pool.drain()
            pool.affine_select(out=IDENT[:], in_=IDENT[:], compare_op=ALU.not_equal, fill=1.0, base=0,
                               pattern=[[-1, P]], channel_multiplier=1)
            pool.affine_select(out=NEGMASK[:], in_=NEGMASK[:], compare_op=ALU.is_ge, fill=-1e30, base=0,
                               pattern=[[1, P]], channel_multiplier=-1)
            for c in range(2):
                pool.drain()
                m = MASK[CH * c:CH * c + CH, :]
                pool.affine_select(out=m, in_=m, compare_op=ALU.is_ge, fill=0.0, base=0,
                                   pattern=[[1, CH]], channel_multiplier=-1)
            pool.drain()
            pool.memset(TOUCH[:], 0.0)
            pool.memset(RESET[:].rearrange("p (n c) -> p n c", c=CH)[:, :, 0:1], 0.0)
            pool.drain().then_inc(consts_made, 1)

            def split_tile(t, r, n, first=False):
                pool.wait_ge(w_loaded[r], (t // 2) * 16 + 16 if isinstance(t, int) else t * 8 + (16 - 8 * r))
                if not first:
                    pool.wait_ge(tile_done, t - 1)
                pool.tensor_tensor(TOUCH[:, 0:2], TOUCH[:, 2:4], TOUCH[:, 4:6], ALU.add)
                pool.tensor_scalar(WH[:, r, 0:n], WRAW[:, r, 0:n], 1.0, 0.0, ALU.mult, ALU.add)
                pool.drain()
                pool.tensor_tensor(WL[:, r, 0:n], WRAW[:, r, 0:n], WH[:, r, 0:n].bitcast(F32),
                                   ALU.subtract).then_inc(w_split, 1)

            for name, n, kbs in STREAM:
                t0 = TILE0[name]
                start = 0
                if t0 == 0:
                    split_tile(0, 0, kbs[0] * P, first=True)
                    split_tile(1, 1, kbs[1] * P, first=True)
                    start = 1
                with pool.Fori(start, n // 2) as i:
                    for r in range(2):
                        split_tile(i * 2 + (t0 + r), r, kbs[r] * P)

        @block.tensor
        def _(pe):
            def norm_sum(n, wb=0):
                pe.wait_ge(norm_acc, 7 * (n + 1))
                for half in range(2):
                    mm = pe.matmul(PX[:, half, :], ONES[:], WK[:, wb + 3, 512 * half:512 * half + 512],
                                   start=True, stop=True)
                mm.then_inc(norm_ms, 1)

            def product(t, r, s, kbs, xh, xl, first=True, last=True):
                pe.wait_ge(w_split, t + 1)
                for half in range(2):
                    tok = slice(512 * half, 512 * half + 512)
                    for k in range(kbs):
                        for n, (w, x) in enumerate(((WH, xh), (WH, xl), (WL, xh))):
                            mm = pe.matmul(PG[:, 2 * s + half, :], w[:, r, P * k:P * k + P], x[:, k, tok],
                                           start=first and k == 0 and n == 0,
                                           stop=last and k == kbs - 1 and n == 2)
                mm.then_inc(tile_done, 1)

            def first_products(t, kbs, xh, xl, ready, count, u):
                for r in range(2):
                    pe.wait_ge(w_split, t + r + 1)
                    if u:
                        pe.wait_ge(slot_free[r], u)
                for k in range(kbs):
                    pe.wait_ge(ready, count + k + 1)
                    for r in range(2):
                        for half in range(2):
                            tok = slice(512 * half, 512 * half + 512)
                            for n, (w, x) in enumerate(((WH, xh), (WH, xl), (WL, xh))):
                                mm = pe.matmul(PG[:, 2 * r + half, :], w[:, r, P * k:P * k + P], x[:, k, tok],
                                               start=k == 0 and n == 0, stop=k == kbs - 1 and n == 2)
                        if k == kbs - 1:
                            mm.then_inc(tile_done, 1)

            def next_units(t, u):
                def part(n, half):
                    if half == 0:
                        pe.wait_ge(w_split, t + n + 1)
                        pe.wait_ge(slot_free[n], u)
                    tok = slice(512 * half, 512 * half + 512)
                    for k in range(KB):
                        for m_, (w, x) in enumerate(((WH, UH), (WH, UL), (WL, UH))):
                            mm = pe.matmul(PG[:, 2 * n + half, :], w[:, n, P * k:P * k + P], x[:, k, tok],
                                           start=k == 0 and m_ == 0, stop=k == KB - 1 and m_ == 2)
                    if half == 1:
                        mm.then_inc(tile_done, 1)
                return [(n, half) for n in range(2) for half in range(2)], part

            pe.wait_ge(consts_made, 1)
            norm_sum(0)

            def rg_block(i, i0):
                t = TILE0["rg_w"] + i * 2
                if i0:
                    first_products(t, KB, UH, UL, norm_lo, 0, 0)
                else:
                    for n in range(2):
                        pe.wait_ge(slot_free[n], i)
                        product(t + n, n, n, KB, UH, UL)
                pe.wait_ge(rg_conv, i + 1)
                if not i0:
                    pe.wait_ge(rg_sig, i * 2)
                for g in range(2):
                    for half in range(2):
                        mm = pe.matmul(PX[:, 2 * g + half, :], WK[:, 15, P * g:P * g + P],
                                       WK[:, 2, 512 * half:512 * half + 512], start=True, stop=True)
                mm.then_inc(rg_gates, 1)

            rg_block(0, True)
            with pe.Fori(1, 4) as i:
                rg_block(i, False)

            def la_core(la, i, nh, dk, kdt, vt, att, qe0, ke, qe1, S, v, kd, sqo, n_turn, following=None):
                parts, part = following or ([], None)
                parts = list(parts)

                def fill(n=1):
                    for _ in range(n):
                        if parts:
                            part(*parts.pop(0))
                pe.wait_ge(la["kd"], i + 1)
                for n, src in enumerate([*v, kd]):
                    b = 2 * (n % 2)
                    if n >= 2:
                        pe.wait_ge(la["turned_copied"], i * n_turn + n - 1)
                    for t in range(TT):
                        mm = pe.transpose(PX[:, b + t // 4, P * (t % 4):P * (t % 4) + P],
                                          WK[:, src, P * t:P * t + P], IDENT[:])
                    mm.then_inc(la["turned"], 1)
                fill()
                pe.wait_ge(la["turned_copied"], i * n_turn + n_turn)
                pe.wait_ge(la["keys"], i + 1)
                for hh in range(nh):
                    rows = slice(dk * hh, dk * hh + dk)
                    for t in range(TT):
                        for c in range(2):
                            at = P * t + CH * c
                            mm = pe.matmul(PX[CH * c:CH * c + 32, hh, CH * t:CH * t + CH],
                                           WK[rows, ke, at:at + 32], WK[rows, qe0, at:at + CH],
                                           start=True, stop=True)
                            q = 32 * (2 * t + c)
                            mm = pe.matmul(PX[CH * c + 32:CH * c + CH, hh, CH * t + 32:CH * t + CH],
                                           WK[rows, ke, at + 32:at + CH], WK[rows, qe1, q:q + 32],
                                           start=True, stop=True)
                mm.then_inc(la["scores"], 1)
                for g in range(2):
                    if g:
                        pe.wait_ge(la["state"], i * 2 + 1)
                    for t in range(4 * g, 4 * g + 4):
                        for c in range(2):
                            for hh in range(nh):
                                tok = slice(CH * c, CH * c + CH)
                                mm = pe.matmul(PX[dk * hh:dk * hh + dk, 2 + c, P * (t % 4):P * (t % 4) + P],
                                               WK[tok, kdt, P * t + dk * hh:P * t + dk * hh + dk],
                                               WK[tok, vt[hh], P * t:P * t + P], start=True, stop=True)
                    mm.then_inc(la["ds"], 1)
                fill()
                pe.wait_ge(la["attn"], i + 1)
                pe.wait_ge(la["state"], i * 2 + 2)
                for hh in range(nh):
                    if hh:
                        fill()
                        pe.wait_ge(la["y"], i * nh + hh)
                    for t in range(TT):
                        o = PX[:, t // 4, P * (t % 4):P * (t % 4) + P]
                        pe.matmul(o, WK[:, vt[hh], P * t:P * t + P], WK[:, att[hh], P * t:P * t + P],
                                  start=True, stop=False)
                        for c in range(2):
                            rows = slice(dk * hh, dk * hh + dk)
                            mm = pe.matmul(o[:, CH * c:CH * c + CH], WK[rows, S:S + 2, :].rearrange(
                                "p a t -> p (a t)")[:, P * (2 * t + c):P * (2 * t + c) + P],
                                WK[rows, qe0, P * t + CH * c:P * t + CH * c + CH], start=False, stop=c == 1)
                    mm.then_inc(la["o"], 1)
                    fill(2 if nh == 1 else 1)
                    pe.wait_ge(la["sq"], i * nh + hh + 1)
                    for half in range(2):
                        mm = pe.matmul(PX[:, 2 + half, :], ONES[:], WK[:, sqo, 512 * half:512 * half + 512],
                                       start=True, stop=True)
                    mm.then_inc(la["ms"], 1)

            def hg_head(i, last):
                t = TILE0["hg_w"] + i * 4
                for n in range(2, 4):
                    pe.wait_ge(slot_free[n % 2], i * 2 + (UNIT0["hg_w"] // 2 + n // 2))
                    product(t + n, n % 2, n % 2, KB, UH, UL)
                la_core(hg, i, 1, 128, 12, [11], [13], 8, 10, 6, 14, [4], 7, 4, 2,
                        None if last else next_units(t + 4, i * 2 + (UNIT0["hg_w"] // 2 + 2)))

            for n in range(2):
                pe.wait_ge(slot_free[n], UNIT0["hg_w"] // 2)
                product(TILE0["hg_w"] + n, n, n, KB, UH, UL)
            with pe.Fori(0, 3) as i:
                hg_head(i, False)
            hg_head(3, True)

            first_products(TILE0["out1_w"], KB, UH, UL, sp_lo, 0, UNIT0["out1_w"] // 2)
            with pe.Fori(1, 4) as i:
                for n in range(2):
                    pe.wait_ge(slot_free[n], UNIT0["out1_w"] // 2 + i)
                    product(TILE0["out1_w"] + i * 2 + n, n, n, KB, UH, UL)
            pe.wait_ge(ple_ready, 2)
            with pe.Fori(0, 4) as i:
                for n in range(2):
                    pe.wait_ge(slot_free[n], UNIT0["ple_w"] // 2 + i)
                    product(TILE0["ple_w"] + i * 2 + n, n, n, 2, PH, PL)
            norm_sum(1)
            first_products(TILE0["gate_w"], KB, UH, UL, norm_lo, 8, UNIT0["gate_w"] // 2)
            with pe.Fori(1, 4) as i:
                for n in range(2):
                    pe.wait_ge(slot_free[n], UNIT0["gate_w"] // 2 + i)
                    product(TILE0["gate_w"] + i * 2 + n, n, n, KB, UH, UL)
            norm_sum(2)

            def partial(t, r, bank, kbs, x, first=True, last=True, w0=0):
                pe.wait_ge(w_split, t + 1)
                for k in range(kbs):
                    xh, xl = x(k)
                    for n, (w, v) in enumerate(((WH, xh), (WH, xl), (WL, xh))):
                        mm = pe.matmul(PG[:, bank, :], w[:, r, P * k:P * k + P], v,
                                       start=first and k == 0 and n == 0, stop=last and k == kbs - 1 and n == 2)
                return mm

            def u_half(h):
                return lambda k: (UH[:, k, 512 * h:512 * h + 512], UL[:, k, 512 * h:512 * h + 512])

            norm_sum(3)
            for h in range(2):
                pe.wait_ge(slot_free[h], UNIT0["misc_w"] // 2)
            for k in range(KB):
                if k % 4 == 0:
                    pe.wait_ge(w_split, TILE0["misc_w"] + k // 4 + 1)
                pe.wait_ge(norm_lo, 24 + k + 1)
                for h in range(2):
                    tok = slice(512 * h, 512 * h + 512)
                    for n, (w, x) in enumerate(((WH, UH), (WH, UL), (WL, UH))):
                        mm = pe.matmul(PG[:, 2 * h, :], w[:, k // 4, P * (k % 4):P * (k % 4) + P], x[:, k, tok],
                                       start=k == 0 and n == 0, stop=k == KB - 1 and n == 2)
                if k % 4 == 3:
                    mm.then_inc(tile_done, 1)
            pe.wait_ge(misc_out, 1)
            pe.wait_ge(small_loaded, 32)
            for b in range(2):
                for half in range(2):
                    mm = pe.matmul(PX[:, 2 * b + half, :], A2W[:, P * b:P * b + P],
                                   WK[0:16, 15, 512 * half:512 * half + 512], start=True, stop=True)
            mm.then_inc(gla_a2, 1)

            for i in range(2):
                u = UNIT0["gla_w"] // 2 + 3 * i
                t = TILE0["gla_w"] + 6 * i
                for n in range(0 if i == 0 else 2, 6):
                    pe.wait_ge(slot_free[n % 2], u + n // 2)
                    product(t + n, n % 2, n % 2, KB, UH, UL)
                la_core(gl, i, 2, 64, 10, [5, 6], [14, 16], 11, 13, 9, 17, [5, 6], 10, 4, 3, next_units(t + 6, u + 3))

            for b in range(2):
                for n in range(2, 6):
                    pe.wait_ge(slot_free[n % 2], UNIT0["ml_w"] // 2 + 3 * b + n // 2)
                    product(TILE0["ml_w"] + 6 * b + n, n % 2, n % 2, KB, UH, UL)
                if not b:
                    pe.wait_ge(m["exps"], 1)
                    for n, s_ in enumerate((12, 11)):
                        for t in range(TT):
                            mm = pe.transpose(PX[:, 0, 32 * n + 4 * t:32 * n + 4 * t + 4],
                                              WK[0:4, s_, P * t:P * t + P], IDENT[0:4, 0:4])
                    mm.then_inc(m["turned_rows"], 1)
                    pe.wait_ge(m["tok"], 1)
                if b:
                    pe.wait_ge(m["y"], 2 * b)
                for g in range(2):
                    rows = slice(32 + 32 * g, 36 + 32 * g)
                    for half in range(2):
                        mm = pe.matmul(PX[:, 2 * g + half, :], SEL[rows, 512 + P * b:512 + P * b + P],
                                       WK[rows, 13, 512 * half:512 * half + 512], start=True, stop=True)
                mm.then_inc(m["spread"], 1)
                pe.wait_ge(m["kw"], b + 1)
                for n, src in enumerate((4, 5, 9)):
                    bk = 2 * (n % 2)
                    if n >= 2:
                        pe.wait_ge(m["turned_copied"], 3 * b + n - 1)
                    for t in range(TT):
                        mm = pe.transpose(PX[:, bk + t // 4, P * (t % 4):P * (t % 4) + P],
                                          WK[:, src, P * t:P * t + P], IDENT[:])
                    mm.then_inc(m["turned"], 1)
                parts, part = next_units(TILE0["ml_w"] + 6 * b + 6, UNIT0["ml_w"] // 2 + 3 * b + 3)
                part(*parts[0])
                pe.wait_ge(m["turned_copied"], 3 * b + 3)
                for t in range(TT):
                    for hh in range(2):
                        kw = WK[:, 9, P * t + 64 * hh:P * t + 64 * hh + 64]
                        pe.matmul(PX[64 * hh:64 * hh + 64, 2 + t // 4, P * (t % 4):P * (t % 4) + P], kw,
                                  WK[:, 4 + hh, P * t:P * t + P], start=True, stop=True)
                        mm = pe.matmul(PX[64 * hh:64 * hh + 64, 0, t:t + 1], kw, ONES[:, 0:1],
                                       start=True, stop=True)
                mm.then_inc(m["ds"], 1)
                pe.wait_ge(m["state"], b + 1)
                for hh in range(2):
                    head = 2 * b + hh
                    rows = slice(64 * hh, 64 * hh + 64)
                    if hh:
                        pe.wait_ge(m["y"], head)
                    for half in range(2):
                        pe.matmul(PX[:, half, :], SEL[0:4, P * head:P * head + P],
                                  WK[0:4, 13, 512 * half:512 * half + 512], start=True, stop=False)
                        pe.matmul(PX[:, half, :].rearrange("p (t c) -> p t c", c=P), IDENT[:],
                                  NEGMASK[:, None, :].to_broadcast([P, 4, P]), start=False, stop=True)
                    for t in range(TT):
                        mm = pe.matmul(PX[:, 2 + t // 4, P * (t % 4):P * (t % 4) + P],
                                       WK[rows, 3, P * t:P * t + P], WK[rows, 2, P * t:P * t + P],
                                       start=True, stop=True)
                    mm.then_inc(m["scores"], 1)
                    if hh:
                        part(*parts[3])
                    else:
                        part(*parts[1])
                    pe.wait_ge(m["p"], head + 1)
                    for t in range(TT):
                        qw = WK[rows, 8, P * t:P * t + P]
                        o = PX[:, t // 4, P * (t % 4):P * (t % 4) + P]
                        pe.matmul(o, WK[:, 11, P * t:P * t + P], WK[:, 4 + hh, P * t:P * t + P],
                                  start=True, stop=False)
                        pe.matmul(o, qw, WK[rows, 10, P * t:P * t + P], start=False, stop=True)
                        d_ = PX[:, 2, t:t + 1]
                        pe.matmul(d_, WK[:, 11, P * t:P * t + P], ONES[:, 0:1], start=True, stop=False)
                        mm = pe.matmul(d_, qw, WK[rows, 19, ML_AT + 72 + t:ML_AT + 73 + t], start=False, stop=True)
                    mm.then_inc(m["num"], 1)
                    if not hh:
                        part(*parts[2])
                    pe.wait_ge(m["h"], head + 1)
                    for t in range(TT):
                        mm = pe.transpose(PX[:, 2 + t // 4, P * (t % 4):P * (t % 4) + P],
                                          WK[:, 12, P * t:P * t + P], IDENT[:])
                    mm.then_inc(m["ht"], 1)

            for n in range(2, 4):
                pe.wait_ge(slot_free[n % 2], UNIT0["s5_w"] // 2 + n // 2)
                product(TILE0["s5_w"] + n, n % 2, n % 2, KB, UH, UL)

            def s5_block(i, first):
                pe.wait_ge(s5["g"], i + 1)
                if not first:
                    pe.wait_ge(s5["pre_gelu"], i)
                for l in range(8):
                    mm = pe.transpose(PX[:, l // 4, P * (l % 4):P * (l % 4) + P],
                                      WK[:, 12, :].rearrange("p (n l) -> p l n", l=8)[:, l, :], IDENT[:])
                mm.then_inc(s5["tok"], 1)
                for j in range(4):
                    for ri in range(2):
                        mm = pe.matmul(PX[32 * j:32 * j + 32, 2, 0:240],
                                       WK[:, 13, P * ri + 32 * j:P * ri + 32 * j + 32],
                                       WK[:, ri, 240 * j:240 * j + 240], start=ri == 0, stop=ri == 1)
                mm.then_inc(s5["resp"], 1)
                pe.wait_ge(s5["tok_copied"], i + 1)
                for g in range(8):
                    mm = pe.transpose(PX[:, g // 4, P * (g % 4):P * (g % 4) + P],
                                      WK[:, 5, P * g:P * g + P], IDENT[:])
                mm.then_inc(s5["u"], 1)
                pe.wait_ge(s5["resp_copied"], i + 1)
                for j in range(4):
                    for ri in range(2):
                        n = 2 * j + ri
                        mm = pe.transpose(PX[:, 2 + n // 4, P * (n % 4):P * (n % 4) + P],
                                          WK[:, ri, 240 * j:240 * j + P], IDENT[:])
                mm.then_inc(s5["gt"], 1)
                pe.wait_ge(s5["u_copied"], i + 1)
                pe.wait_ge(s5["gt_copied"], i + 1)
                for g in range(8):
                    j, rows = g // 2, slice(64 * (g % 2), 64 * (g % 2) + 64)
                    for ri in range(2):
                        n = 2 * j + ri
                        mm = pe.matmul(PX[rows, ri, P * j:P * j + P],
                                       WK[:, 4, P * n + 64 * (g % 2):P * n + 64 * (g % 2) + 64],
                                       WK[:, 6, P * g:P * g + P], start=True, stop=True)
                mm.then_inc(s5["v"], 1)
                for l in range(8):
                    mm = pe.transpose(PX[:, 2 + l // 4, P * (l % 4):P * (l % 4) + P],
                                      WK[:, 13, RESP + 16 * (7 - l):RESP + 16 * (7 - l) + P], IDENT[:])
                mm.then_inc(s5["kt"], 1)
                pe.wait_ge(s5["kt_copied"], i + 1)
                pe.wait_ge(s5["x"], i + 1)
                for g in range(8):
                    j, rows = g // 2, slice(64 * (g % 2), 64 * (g % 2) + 64)
                    o = PX[:, 2 + g % 2, P * j:P * j + P]
                    pe.matmul(o, WK[:, 6, P * g:P * g + P], WK[:, 3, P * g:P * g + P], start=True, stop=False)
                    for ri in range(2):
                        mm = pe.matmul(o, WK[rows, 8, 512 * ri + P * j:512 * ri + P * j + P],
                                       WK[rows, 2, 512 * ri + P * j:512 * ri + P * j + P],
                                       start=False, stop=ri == 1)
                mm.then_inc(s5["y"], 1)
                pe.wait_ge(s5["y_copied"], i + 1)
                for l in range(8):
                    mm = pe.transpose(PX[:, l // 4, P * (l % 4):P * (l % 4) + P],
                                      WK[:, 5, P * l:P * l + P], IDENT[:])
                mm.then_inc(s5["back"], 1)

            s5_block(0, True)
            with pe.Fori(1, 4) as i:
                s5_block(i, False)
            pe.wait_ge(glu_lo, 4)
            for n in range(4):
                pe.wait_ge(slot_free[n % 2], UNIT0["glu_w"] // 2 + n // 2)
                product(TILE0["glu_w"] + n, n % 2, n % 2, 4, GH, GLO)

            for hf, name in enumerate(("mix0", "mix1")):
                with pe.Fori(0, 4) as i:
                    for n in range(6):
                        s_ = n % 2
                        t = i * 12 + (TILE0[name] + 2 * n)
                        pe.wait_ge(slot_free[s_], i * 3 + (UNIT0[name] // 2 + n // 2))
                        partial(t, 0, 2 * s_, 8, u_half(hf)).then_inc(tile_done, 1)
                        pe.wait_ge(mix_lo, 12 * hf + 4 * (n % 3) + 4)
                        partial(t + 1, 1, 2 * s_ + 1, 4, lambda k: (
                            YH[:, 4 * (n % 3) + k, :], YL[:, 4 * (n % 3) + k, :])).then_inc(tile_done, 1)
            first_products(TILE0["out2_w"], KB, UH, UL, sp_lo, 8, UNIT0["out2_w"] // 2)
            with pe.Fori(1, 4) as i:
                for n in range(2):
                    pe.wait_ge(slot_free[n], UNIT0["out2_w"] // 2 + i)
                    product(TILE0["out2_w"] + i * 2 + n, n, n, KB, UH, UL)
            norm_sum(4, 8)
            norm_sum(5)
            pe.wait_ge(norm_lo, 48)
            def hl(k):
                return HL1[:, k, :] if k < 16 else HL2[:, k - 16, :]

            for hf in range(2):
                up, down = f"up{hf}", f"down{hf}"
                with pe.Fori(0, 11) as i:
                    for n in range(2):
                        t = i * 4 + (TILE0[up] + 2 * n)
                        pe.wait_ge(slot_free[n], i + UNIT0[up] // 2)
                        for g in range(2):
                            partial(t + g, g, 2 * n + g, 8, u_half(hf)).then_inc(tile_done, 1)
                with pe.Fori(0, 2) as i:
                    for n in range(2):
                        pe.wait_ge(slot_free[n], i + UNIT0[down] // 2)
                        for b in range(2):
                            for q in range(3):
                                o = 6 * n + 3 * b + q
                                pe.wait_ge(ffn_lo, 22 * hf + min(8 * q + 8, 22))
                                partial(i * 12 + (TILE0[down] + o), o % 2, 2 * n + b, (8, 8, 6)[q],
                                        lambda k: (HH[:, 8 * q + k, :], hl(8 * q + k)),
                                        q == 0, q == 2).then_inc(tile_done, 1)
            norm_sum(6)

        @block.scalar
        def _(act):
            def norm_squares(n, src, wb=0, made=None):
                for j in range(KB):
                    if made is not None:
                        act.wait_ge(norm_lo, made + j + 1)
                    if j >= 3:
                        act.wait_ge(norm_acc, 7 * n + max(1, j - 3))
                    for tok, x in src(j):
                        ins = act.activation(WK[:, wb + j % 3, tok], x, ACT.Square)
                    ins.then_inc(norm_sq, 1)
                act.wait_ge(norm_ms, n + 1)
                act.activation(WK[:, wb + 4, :], aux(0), ACT.Ln, bias=vec("eps"), scale=1.0 / D)
                act.drain()
                act.activation(WK[:, wb + 4, :], WK[:, wb + 4, :], ACT.Exp, scale=-0.5).then_inc(norm_rs, 1)

            def whole(x):
                return lambda j: [(slice(0, T), x[:, j, :])]

            def norm_split(m, shift=None):
                for j in range(KB):
                    act.wait_ge(norm_t, 8 * m + j + 1)
                    act.activation(UH[:, j, :], WK[:, 5 + j % 2, :], ACT.Identity,
                                   bias=0.0 if shift is None else shift(j)).then_inc(norm_hi, 1)

            act.wait_ge(vec_loaded, 16)
            act.wait_ge(c_loaded, 16)
            act.activation(C_ROW, C_ROW, ACT.Silu).then_inc(pre_act, 1)
            act.wait_ge(pre_dve, 1)
            tmp = VEC["tmp"]
            act.activation(CONST_V[:, tmp + 12:tmp + 24], CONST_V[:, tmp:tmp + 12], ACT.Exp).then_inc(pre_act, 1)
            act.wait_ge(x_loaded, 16 * KB)
            norm_squares(0, whole(H))
            norm_split(0)

            XP = wk(0, 2)
            with act.Fori(0, 4) as i:
                t = TILE0["rg_w"] + i * 2
                act.wait_ge(tile_done, t + 1)
                act.wait_ge(pre_dve, i + 2)
                act.activation(XP[:, 3:3 + T], slot(0), ACT.Copy).then_inc(slot_free[0], 1)
                act.wait_ge(tile_done, t + 2)
                act.activation(WK[:, 5, :], slot(1), ACT.Sigmoid).then_inc(rg_ogate, 1)
                act.wait_ge(rg_gates, i + 1)
                act.activation(WK[:, 3, :], aux(0), ACT.Sigmoid, bias=vec_at("rg_ba", i)).then_inc(rg_sig, 1)
                act.activation(WK[:, 4, :], aux(2), ACT.Sigmoid, bias=vec_at("rg_bx", i)).then_inc(rg_sig, 1)
                act.drain()
                act.activation(WK[:, 6, :], WK[:, 3, :], ACT.Tanh, scale=vec_at("rg_s8", i))
                act.activation(WK[:, 7, :], WK[:, 3, :], ACT.Exp, scale=vec_at("neg_rg_s8", i))
                act.drain()
                act.activation(WK[:, 8, :], WK[:, 7, :], ACT.Square).then_inc(rg_decay, 1)
                act.wait_ge(rg_q, i + 1)
                act.activation(WK[:, 8, :], WK[:, 8, :], ACT.Sqrt).then_inc(rg_mult, 1)

            def halves(s, lo, n=1):
                v = WK[:, s, :].rearrange("p (n c) -> p n c", c=CH)
                return v[:, :, 0:32] if lo else v[:, :, 32:CH]

            def half_row(s, k):
                return WK[:, s, 512 * k:512 * k + 512].rearrange("p (n c) -> p n c", c=32)

            def la_exps(la, i, b, bm, eb, ek, ed):
                act.wait_ge(la["gaps"], i + 1)
                act.activation(WK[:, ed, :], WK[:, ed, :], ACT.Exp)
                act.activation(WK[:, eb, :], WK[:, b, :], ACT.Exp)
                act.activation(half_row(bm, 1), half_row(bm, 0), ACT.Exp)
                act.activation(halves(ek, True), halves(b, True), ACT.Exp, scale=-1.0)
                act.activation(halves(ek, False), half_row(bm, 0), ACT.Exp, scale=-1.0).then_inc(la["exps"], 1)

            def la_rest(la, i, nh, n_turn, dst, sqo, rs, dv=P):
                for n, s in enumerate(dst):
                    act.wait_ge(la["turned"], i * n_turn + n + 1)
                    act.activation(WK[:, s, :], aux(2 * (n % 2)), ACT.Copy).then_inc(la["turned_copied"], 1)
                for hh in range(nh):
                    act.wait_ge(la["o"], i * nh + hh + 1)
                    act.activation(WK[:, sqo, :], aux(0), ACT.Square).then_inc(la["sq"], 1)
                    act.wait_ge(la["ms"], i * nh + hh + 1)
                    act.activation(WK[:, rs, :], aux(2), ACT.Ln, bias=vec("eps"), scale=1.0 / dv)
                    act.drain()
                    act.activation(WK[:, rs, :], WK[:, rs, :], ACT.Exp, scale=-0.5).then_inc(la["rs"], 1)

            act.wait_ge(rg_done, 4)
            with act.Fori(0, 4) as i:
                t = TILE0["hg_w"] + i * 4
                act.wait_ge(hg["free"], i + 1)
                act.wait_ge(tile_done, t + 1)
                act.activation(WK[:, 0, :], slot(0), ACT.Sigmoid)
                act.activation(WK[:, 2, :], slot(0), ACT.Sigmoid, scale=-1.0).then_inc(slot_free[0], 1)
                act.wait_ge(tile_done, t + 2)
                act.activation(WK[:, 3, :], slot(1), ACT.Sigmoid).then_inc(hg["sig"], 1)
                act.drain()
                act.activation(WK[:, 0, :], WK[:, 0, :], ACT.Ln, bias=vec_at("lb", i),
                               scale=vec_at("one_minus_lb", i)).then_inc(hg["logf"], 1)
                act.wait_ge(tile_done, t + 3)
                act.activation(WK[:, 4, :], slot(0), ACT.Copy).then_inc(slot_free[0], 1)
                act.wait_ge(tile_done, t + 4)
                act.activation(WK[:, 5, :], slot(1), ACT.Sigmoid).then_inc(hg["sig"], 1)
                la_exps(hg, i, 1, 0, 9, 10, 7)
                la_rest(hg, i, 1, 2, [11, 12], 4, 1)

            act.wait_ge(hg["y"], 4)
            for j in range(KB):
                act.activation(UH[:, j, :], H[:, j, :], ACT.Copy).then_inc(sp_hi, 1)
            for j in range(2):
                act.wait_ge(p_loaded, 16 * (j + 1))
                act.activation(PH[:, j, :], WK[:, 19, :], ACT.Copy).then_inc(ple_hi, 1)
            with act.Fori(0, 4) as i:
                for n in range(2):
                    act.wait_ge(tile_done, i * 2 + (TILE0["ple_w"] + n + 1))
                    act.activation(WK[:, ds(i * 2 + (7 + n), 1), :].rearrange("p a t -> p (a t)"), slot(n),
                                   ACT.Copy).then_inc(slot_free[n], 1)
            norm_squares(1, whole(H))
            norm_split(1)
            def gate(i, n, first):
                act.wait_ge(tile_done, i * 2 + (TILE0["gate_w"] + n + 1))
                if not first:
                    act.wait_ge(gate_added, i * 2 + (n - 1))
                act.activation(WK[:, n, :], slot(n), ACT.Sigmoid, bias=vec_at("b_ple_gate", i * 2 + n)
                               ).then_inc(slot_free[n], 1)
            gate(0, 0, True)
            gate(0, 1, True)
            with act.Fori(1, 4) as i:
                for n in range(2):
                    gate(i, n, False)
            act.wait_ge(gate_added, 8)
            norm_squares(2, whole(H))

            act.wait_ge(gains_made, 1)
            norm_squares(3, whole(H), made=16)
            norm_split(2, lambda j: MOD[:, j:j + 1])
            act.wait_ge(tile_done, TILE0["misc_w"] + 2)
            for half in range(2):
                act.activation(WK[:, 15, 512 * half:512 * half + 512], PG[:, 2 * half, :],
                               ACT.Copy).then_inc(slot_free[half], 1)
            act.drain().then_inc(misc_out, 1)
            act.wait_ge(gla_x, 1)
            for b in range(2):
                act.activation(WK[:, 2 + b, :], WK[:, 2 + b, :], ACT.Exp)
            act.drain()
            for b in range(2):
                act.activation(WK[:, 2 + b, :], WK[:, 2 + b, :], ACT.Ln, bias=vec("one")).then_inc(gla_ln, 1)

            with act.Fori(0, 2) as i:
                t = TILE0["gla_w"] + i * 6
                act.wait_ge(gl["free"], i + 1)
                la_exps(gl, i, 2, 9, 12, 13, 10)
                act.wait_ge(tile_done, t + 1)
                act.activation(WK[:, 4, :], slot(0), ACT.Copy).then_inc(slot_free[0], 1)
                for n in range(2):
                    act.wait_ge(tile_done, t + 3 + n)
                    act.activation(WK[:, 5 + n, :], slot(n), ACT.Copy).then_inc(slot_free[n], 1)
                for n in range(2):
                    act.wait_ge(tile_done, t + 5 + n)
                    act.activation(WK[:, 7 + n, :], slot(n), ACT.Silu).then_inc(slot_free[n], 1)
                la_rest(gl, i, 2, 3, [5, 6, 10], 4, 2)

            act.wait_ge(m["rows"], 1)
            act.activation(WK[0:4, 2, :], WK[0:4, 2, :], ACT.Exp)
            act.drain()
            act.activation(WK[0:4, 2, :], WK[0:4, 2, :], ACT.Ln, bias=CONST_V[0:4, VEC["one"]:VEC["one"] + 1]
                           ).then_inc(m["ln"], 1)
            act.wait_ge(m["gates"], 1)
            act.activation(WK[32:36, 13, :], WK[0:4, 9, :], ACT.Exp)
            act.activation(WK[64:68, 13, :], WK[0:4, 16, :], ACT.Exp)
            act.activation(WK[0:4, 11, :], WK[0:4, 3, :], ACT.Exp, scale=-1.0).then_inc(m["exps"], 1)
            XQ, XK = wk(0, 2), wk(17, 2)
            for b in range(2):
                t = TILE0["ml_w"] + 6 * b
                if b:
                    act.wait_ge(s5["loaded"], 32)
                    act.activation(S5P(3), S5P(2), ACT.Exp).then_inc(s5["dt"], 1)
                    act.wait_ge(s5["angle"], 1)
                    act.activation(S5P(6), S5P(4), ACT.Exp)
                    act.activation(S5P(7), S5P(4), ACT.Exp, scale=8.0)
                    act.activation(S5P(10), S5P(9), ACT.Sin)
                    act.activation(S5P(11), S5P(9), ACT.Sin, scale=0.5)
                    act.drain().then_inc(s5["trig"], 1)
                for n, x in enumerate((XQ, XK)):
                    act.wait_ge(tile_done, t + 1 + n)
                    if b:
                        act.wait_ge(m["conv"], 2 * b)
                    act.activation(x[:, 3:3 + T], slot(n), ACT.Copy).then_inc(slot_free[n], 1)
                for n in range(2):
                    act.wait_ge(tile_done, t + 3 + n)
                    act.activation(WK[:, 4 + n, :], slot(n), ACT.Copy).then_inc(slot_free[n], 1)
                for n in range(2):
                    act.wait_ge(m["conv"], 2 * b + n + 1)
                    act.activation(WK[:, 2 + n, :], WK[:, 2 + n, :], ACT.Silu).then_inc(m["silu"], 1)
                for n in range(2):
                    act.wait_ge(tile_done, t + 5 + n)
                    act.activation(WK[:, 6 + n, :], slot(n), ACT.Sigmoid).then_inc(slot_free[n], 1)
                for n, s_ in enumerate((4, 5, 9)):
                    act.wait_ge(m["turned"], 3 * b + n + 1)
                    act.activation(WK[:, s_, :], aux(2 * (n % 2)), ACT.Copy).then_inc(m["turned_copied"], 1)
                for hh in range(2):
                    head = 2 * b + hh
                    act.wait_ge(m["scores"], head + 1)
                    for t in range(TT):
                        ins = act.activation(WK[:, 11, P * t:P * t + P], PX[:, t // 4, P * (t % 4):P * (t % 4) + P],
                                             ACT.Exp, bias=WK[:, 19, ML_AT + 4 * t + head:ML_AT + 4 * t + head + 1])
                    ins.then_inc(m["e"], 1)

            for n in range(4):
                act.wait_ge(tile_done, TILE0["s5_w"] + n + 1)
                act.activation(WK[:, 16 + n, :], slot(n % 2), ACT.Copy).then_inc(slot_free[n % 2], 1)
            with act.Fori(0, 4) as i:
                act.wait_ge(s5["tok"], i + 1)
                act.activation(WK[:, 5, :].rearrange("p (g l c) -> p l g c", g=8, l=8),
                               aux(0).rearrange("p (l g c) -> p l g c", g=8, l=8), ACT.Copy
                               ).then_inc(s5["tok_copied"], 1)
                act.wait_ge(s5["resp"], i + 1)
                act.activation(WK[:, 13, RESP:RESP + 240], PX[:, 2, 0:240], ACT.Copy).then_inc(s5["resp_copied"], 1)
                act.wait_ge(s5["u"], i + 1)
                act.activation(WK[:, 6, :], aux(0), ACT.Copy).then_inc(s5["u_copied"], 1)
                act.wait_ge(s5["gt"], i + 1)
                act.activation(WK[:, 4, :], aux(2), ACT.Copy).then_inc(s5["gt_copied"], 1)
                act.wait_ge(s5["kt"], i + 1)
                act.activation(WK[:, 3, :].rearrange("p (g l c) -> p l g c", g=8, l=8),
                               aux(2).rearrange("p (l g c) -> p l g c", g=8, l=8), ACT.Copy
                               ).then_inc(s5["kt_copied"], 1)
                act.wait_ge(s5["y"], i + 1)
                for b in range(2):
                    ins = act.activation(WK[:, 5, :].rearrange("p (l j g c) -> p g j l c", g=2, j=4, l=8)[:, b],
                                         PX[:, 2 + b, :].rearrange("p (j l c) -> p j l c", j=4, l=8), ACT.Copy)
                ins.then_inc(s5["y_copied"], 1)
                act.wait_ge(s5["pre_gelu"], i + 1)
                y = WK[:, ds(i + 16, 1), :].rearrange("p a t -> p (a t)")
                act.activation(y, y, ACT.Gelu_apprx_tanh)
            act.drain()
            for j in range(4):
                act.activation(GH[:, j, :], WK[:, 16 + j, :], ACT.Copy).then_inc(glu_hi, 1)
            for n in range(4):
                act.wait_ge(tile_done, TILE0["glu_w"] + n + 1)
                act.activation(WK[:, 8 + n, :], slot(n % 2), ACT.Sigmoid, bias=vec("glu_b", n)
                               ).then_inc(slot_free[n % 2], 1)

            for hf in range(2):
                tok = slice(512 * hf, 512 * hf + 512)
                if hf:
                    act.wait_ge(tile_done, TILE0["mix1"])
                for k in range(12):
                    if k == 8 and not hf:
                        act.wait_ge(glu_y, 4)
                    raw = H[:, k, tok] if k < 8 else WK[:, 8 + k, tok]
                    act.activation(YH[:, k, :], raw, ACT.Copy).then_inc(mix_hi, 1)
                with act.Fori(0, 4) as i:
                    for n in range(6):
                        s_ = n % 2
                        act.wait_ge(tile_done, i * 12 + (TILE0[f"mix{hf}"] + 2 * n + 1))
                        act.activation(WK[:, 13, 512 * s_:512 * s_ + 512], PG[:, 2 * s_, :], ACT.Sigmoid,
                                       bias=vec_at("branch_b", i * 2 + (8 * (n % 3) + n // 3))).then_inc(mix_sig, 1)

            act.wait_ge(m_ready, 16)
            for j in range(KB):
                act.activation(UH[:, j, :], H[:, j, :], ACT.Copy).then_inc(sp_hi, 1)
            with act.Fori(0, 4) as i:
                for n in range(2):
                    act.wait_ge(tile_done, i * 2 + (TILE0["out2_w"] + n + 1))
                    act.activation(WK[:, ds(i * 2 + n, 1), :].rearrange("p a t -> p (a t)"), slot(n),
                                   ACT.Copy).then_inc(slot_free[n], 1)
            act.drain()
            norm_squares(4, whole(WK), wb=8)
            norm_squares(5, whole(H), made=32)
            norm_split(3, lambda j: MOD[:, 24 + j:25 + j])

            for hf in range(2):
                with act.Fori(0, 11) as i:
                    for n in range(2):
                        act.wait_ge(tile_done, i * 4 + (TILE0[f"up{hf}"] + 2 * n + 1))
                        act.activation(WK[:, 18, 512 * n:512 * n + 512], PG[:, 2 * n, :], ACT.Silu
                                       ).then_inc(ffn_silu, 1)
                        act.wait_ge(ffn_t, i * 2 + (22 * hf + n + 1))
                        act.activation(HH[:, ds(i * 2 + n, 1), :].rearrange("p a t -> p (a t)"),
                                       WK[:, 19, 512 * n:512 * n + 512], ACT.Copy).then_inc(ffn_hi, 1)
                with act.Fori(0, 2) as i:
                    for n in range(2):
                        act.wait_ge(tile_done, i * 12 + (TILE0[f"down{hf}"] + 6 * n + 6))
                        act.activation(YF[hf][:, ds(i * 4 + 2 * n, 2), :], PG[:, 2 * n:2 * n + 2, :], ACT.Copy
                                       ).then_inc(slot_free[n], 1)
            act.drain()
            norm_squares(6, lambda j: [(slice(512 * h, 512 * h + 512), YF[h][:, j, :]) for h in range(2)])

        @block.vector
        def _(dve):
            def norm_sum_blocks(n, wb=0):
                for j in range(1, KB):
                    dve.wait_ge(norm_sq, 8 * n + j + 1)
                    a = WK[:, wb, :] if j == 1 else WK[:, wb + 3, :]
                    dve.tensor_tensor(WK[:, wb + 3, :], a, WK[:, wb + j % 3, :], ALU.add).then_inc(norm_acc, 1)
                    dve.drain()

            def norm_residual(n, pieces, gain, res, wb):
                dve.wait_ge(norm_rs, n + 1)
                for j in range(KB):
                    for tok, x in pieces(j):
                        dve.scalar_tensor_tensor(WK[:, wb + 5 + j % 2, tok], x, gain(j), WK[:, wb + 4, tok],
                                                 ALU.mult, ALU.mult)
                    dve.drain()
                    dve.tensor_tensor(res[:, j, :], res[:, j, :], WK[:, wb + 5 + j % 2, :], ALU.add).then_inc(norm_lo, 1)
                    dve.drain()

            def norm_split(n, m, src, gain, shift=None, wb=0):
                dve.wait_ge(norm_rs, n + 1)

                def low(j):
                    dve.wait_ge(norm_hi, 8 * m + j + 1)
                    dve.scalar_tensor_tensor(UL[:, j, :], WK[:, 5 + j % 2, :],
                                             vec("zero") if shift is None else shift(j),
                                             UH[:, j, :].bitcast(F32), ALU.add, ALU.subtract).then_inc(norm_lo, 1)
                for j in range(KB):
                    if j >= 2:
                        dve.drain()
                    dve.scalar_tensor_tensor(WK[:, 5 + j % 2, :], src[:, j, :], gain(j), WK[:, 4, :],
                                             ALU.mult, ALU.mult).then_inc(norm_t, 1)
                    if j:
                        low(j - 1)
                low(KB - 1)

            def horner(q, c, z2):
                dve.drain()
                dve.scalar_tensor_tensor(q, q, c, z2, ALU.add, ALU.mult)

            dve.memset(vecs("zero", 8), 0.0)
            dve.memset(vecs("eps", 1), EPS)
            dve.memset(vecs("one", 1), 1.0)
            dve.wait_ge(vec_loaded, 16)
            tmp = VEC["tmp"]
            q = [CONST_V[:, tmp + 4 * j:tmp + 4 * j + 4] for j in range(6)]
            lb0, lb1 = CONST_V[:, VEC["hg_lb"]:VEC["hg_lb"] + 4], CONST_V[:, VEC["hg_lb"] + 4:VEC["hg_lb"] + 8]
            lam = vecs("rg_lambda", 4)
            dve.tensor_tensor(q[3], lb0, lb1, ALU.max)
            dve.drain()
            dve.tensor_tensor(q[0], lb0, q[3], ALU.subtract)
            dve.tensor_tensor(q[1], lb1, q[3], ALU.subtract)
            dve.scalar_tensor_tensor(q[2], lam, -1.0, lam, ALU.mult, ALU.min)
            dve.drain().then_inc(pre_dve, 1)
            dve.wait_ge(pre_act, 2)
            dve.tensor_tensor(q[0], q[3], q[4], ALU.add)
            dve.drain()
            dve.reciprocal(q[0], q[0])
            dve.drain()
            dve.tensor_tensor(vecs("lb", 4), q[3], q[0], ALU.mult)
            dve.drain()
            dve.tensor_scalar(vecs("one_minus_lb", 4), vecs("lb", 4), -1.0, 1.0, ALU.mult, ALU.add)
            dve.tensor_scalar(q[1], q[5], 2.0, None, ALU.add)
            dve.drain()
            dve.reciprocal(q[1], q[1])
            dve.drain()
            dve.tensor_tensor(q[2], q[5], q[1], ALU.mult)
            dve.drain()
            dve.tensor_tensor(q[0], q[2], q[2], ALU.mult)
            dve.drain()
            dve.tensor_scalar(q[1], q[0], 1.0 / 15, None, ALU.mult)
            for k in (13, 11, 9, 7, 5, 3):
                horner(q[1], 1.0 / k, q[0])
            dve.drain()
            dve.scalar_tensor_tensor(q[2], q[1], 1.0, q[2], ALU.add, ALU.mult)
            dve.tensor_scalar(q[3], lam, -1.0, 0.0, ALU.mult, ALU.max)
            dve.drain()
            dve.scalar_tensor_tensor(q[1], q[2], 2.0, q[3], ALU.mult, ALU.add)
            dve.drain()
            dve.tensor_scalar(vecs("rg_s8", 4), q[1], 8.0, None, ALU.mult)
            dve.tensor_scalar(vecs("neg_rg_s8", 4), q[1], -8.0, None, ALU.mult)
            dve.drain()
            norm_sum_blocks(0)
            norm_split(0, 0, H, lambda j: vec("norm_mix_w", j))

            XP = wk(0, 2)
            XC = WK[:, 2, :]
            bd = wk(14)
            dve.drain()
            dve.memset(XP[:, 0:3], 0.0).then_inc(pre_dve, 1)
            dve.wait_ge(bd_loaded, 16)

            def rg_conv_block(i, first):
                if not first:
                    dve.wait_ge(rg_gates, i)
                dve.tensor_copy(WK[:, 15, 0:2 * P], bd[:, ds(i * (2 * P), 2 * P)])
                dve.wait_ge(slot_free[0], i + 1)
                dve.tensor_scalar(XC, XP[:, 3:3 + T], vec_at("conv_w", i + 12), vec_at("conv_b", i),
                                  ALU.mult, ALU.add)
                for k in range(3):
                    dve.drain()
                    dve.scalar_tensor_tensor(XC, XP[:, k:k + T], vec_at("conv_w", i + 4 * k), XC,
                                             ALU.mult, ALU.add)
                dve.drain().then_inc(rg_conv, 1)

            def ada(i, first_rg, n):
                for j in range(n):
                    q = j % 3
                    dve.wait_ge(ada_loaded[q], (i * 16 if first_rg else i * 48 + 64) + 16 * (j // 3 + 1))
                    dve.scalar_tensor_tensor(ADA[:, q, :], ADA[:, q, :], 1.0, C_ROW, ALU.mult, ALU.mult,
                                             accum_out=MOD[:, ds((i * 3 if first_rg else i * 9 + 12) + j, 1)]).then_inc(ada_done, 1)

            def rg_rest(i):
                dve.wait_ge(rg_ogate, i + 1)
                dve.tensor_tensor(WK[:, 5, :], slot(1), WK[:, 5, :], ALU.mult).then_inc(slot_free[1], 1)
                ada(i, True, 3)
                dve.wait_ge(rg_sig, i * 2 + 2)
                dve.tensor_tensor(WK[:, 9, :], WK[:, 4, :], XC, ALU.mult)
                dve.wait_ge(rg_decay, i + 1)
                dve.scalar_tensor_tensor(WK[:, 8, :], WK[:, 8, :], 1.0, WK[:, 6, :], ALU.add,
                                         ALU.mult).then_inc(rg_q, 1)
                dve.wait_ge(rg_mult, i + 1)
                dve.memset(WK[:, 8, 0:1], 1.0)
                dve.drain()
                dve.tensor_tensor(WK[:, 9, :], WK[:, 9, :], WK[:, 8, :], ALU.mult)
                dve.drain()
                dve.tensor_tensor_scan(WK[:, 10, :], WK[:, 7, :], WK[:, 9, :], 0.0, ALU.mult, ALU.add)
                dve.drain()
                dve.tensor_tensor(H[:, ds(i, 1), :].rearrange("p a t -> p (a t)"), WK[:, 10, :], WK[:, 5, :],
                                  ALU.mult).then_inc(rg_done, 1)
                dve.drain().then_inc(pre_dve, 1)

            rg_conv_block(0, True)
            rg_rest(0)
            with dve.Fori(1, 4) as i:
                rg_conv_block(i, False)
                rg_rest(i)

            def chunks(s, w=CH):
                return WK[:, s, :].rearrange("p (n c) -> p n c", c=w)

            def half_row(s, k):
                return WK[:, s, 512 * k:512 * k + 512].rearrange("p (n c) -> p n c", c=32)

            def la_gaps(la, b, bm, bd_, logf):
                dve.tensor_tensor_scan(WK[:, b, :], RESET[:], logf, 0.0, ALU.mult, ALU.add)
                dve.drain()
                B = chunks(b)
                dve.tensor_tensor(half_row(bm, 0), B[:, :, 32:CH], B[:, :, 31:32].to_broadcast([P, NCH, 32]),
                                  ALU.subtract)
                dve.tensor_tensor(chunks(bd_), B[:, :, CH - 1:CH].to_broadcast([P, NCH, CH]), B,
                                  ALU.subtract).then_inc(la["gaps"], 1)

            def la_core(la, i, nh, dk, att, S, eb, n_done):
                for hh in range(nh):
                    if hh == 0:
                        dve.wait_ge(la["scores"], i + 1)
                    for c in range(2):
                        rows = slice(CH * c, CH * c + CH)
                        out_ = WK[rows, att[hh], :].rearrange("p (t c) -> p t c", c=P)[:, :, CH * c:CH * c + CH]
                        ins = dve.tensor_tensor(out_, PX[rows, hh, :].rearrange("p (t c) -> p t c", c=CH),
                                                MASK[rows, None, :].to_broadcast([CH, TT, CH]), ALU.mult)
                ins.then_inc(la["attn"], 1)
                st = WK[:, S:S + 2, :].rearrange("p a t -> p (a t)")
                for n in range(NCH):
                    if n % 8 == 0:
                        dve.wait_ge(la["ds"], i * 2 + (n // 8 + 1))
                    if n < NCH - 1:
                        ins = dve.scalar_tensor_tensor(
                            st[:, P * (n + 1):P * (n + 2)], st[:, P * n:P * (n + 1)],
                            WK[:, eb, CH * n + CH - 1:CH * n + CH],
                            PX[:, 2 + n % 2, P * (n // 2 % 4):P * (n // 2 % 4) + P], ALU.mult, ALU.add)
                    if n % 8 == 7:
                        dve.drain().then_inc(la["state"], 1)
                    else:
                        dve.drain()

            dve.drain()
            dve.memset(WK[:, 14, 0:P], 0.0)
            dve.memset(WK[:, 13, :], 0.0)
            dve.drain().then_inc(hg["free"], 1)
            with dve.Fori(0, 4) as i:
                ada(i, False, 9)
                dve.wait_ge(hg["sig"], i * 2 + 1)
                dve.scalar_tensor_tensor(WK[:, 3, :], slot(1), 128 ** -0.5, WK[:, 3, :], ALU.mult,
                                         ALU.mult).then_inc(slot_free[1], 1)
                dve.wait_ge(hg["logf"], i + 1)
                la_gaps(hg, 1, 0, 7, WK[:, 0, :])
                dve.wait_ge(hg["sig"], i * 2 + 2)
                dve.tensor_tensor(WK[:, 5, :], slot(1), WK[:, 5, :], ALU.mult).then_inc(slot_free[1], 1)
                dve.wait_ge(hg["exps"], i + 1)
                k = vec_at("one_minus_lb", i)
                dve.scalar_tensor_tensor(WK[:, 7, :], WK[:, 2, :], k, WK[:, 7, :], ALU.mult,
                                         ALU.mult).then_inc(hg["kd"], 1)
                dve.tensor_tensor(WK[:, 8, :], WK[:, 3, :], WK[:, 9, :], ALU.mult)
                dve.tensor_tensor(half_row(6, 0), chunks(3)[:, :, 32:CH], half_row(0, 1), ALU.mult)
                dve.scalar_tensor_tensor(WK[:, 10, :], WK[:, 2, :], k, WK[:, 10, :], ALU.mult,
                                         ALU.mult).then_inc(hg["keys"], 1)
                la_core(hg, i, 1, 128, [13], 14, 9, 1)
                dve.wait_ge(hg["rs"], i + 1)
                dve.scalar_tensor_tensor(WK[:, 0, :], aux(0), vec("hg_norm_w"), WK[:, 1, :], ALU.mult, ALU.mult)
                dve.drain()
                dve.tensor_tensor(H[:, ds(i + 4, 1), :].rearrange("p a t -> p (a t)"), WK[:, 0, :],
                                  WK[:, 5, :], ALU.mult).then_inc(hg["y"], 1)
                dve.drain().then_inc(hg["free"], 1)

            for j in range(KB):
                dve.wait_ge(sp_hi, j + 1)
                dve.tensor_tensor(UL[:, j, :], H[:, j, :], UH[:, j, :].bitcast(F32),
                                  ALU.subtract).then_inc(sp_lo, 1)
            dve.wait_ge(h_reloaded, 16 * KB)

            def h_at(j):
                return H[:, ds(j, 1), :].rearrange("p a t -> p (a t)")

            with dve.Fori(0, 4) as i:
                for n in range(2):
                    dve.wait_ge(tile_done, i * 2 + (TILE0["out1_w"] + n + 1))
                    h = h_at(i * 2 + n)
                    dve.tensor_tensor(h, h, slot(n), ALU.add).then_inc(slot_free[n], 1)
            for j in range(2):
                dve.wait_ge(ple_hi, j + 1)
                dve.tensor_tensor(PL[:, j, :], WK[:, 19, :], PH[:, j, :].bitcast(F32),
                                  ALU.subtract).then_inc(ple_ready, 1)
            norm_sum_blocks(1)
            norm_split(1, 1, H, lambda j: vec("ple_norm_w", j))
            with dve.Fori(0, 4) as i:
                for n in range(2):
                    dve.wait_ge(slot_free[n], i + (UNIT0["gate_w"] // 2 + 1))
                    dve.tensor_tensor(WK[:, n, :], WK[:, n, :],
                                      WK[:, ds(i * 2 + (7 + n), 1), :].rearrange("p a t -> p (a t)"), ALU.mult)
                    dve.drain()
                    h = h_at(i * 2 + n)
                    dve.tensor_tensor(h, h, WK[:, n, :], ALU.add).then_inc(gate_added, 1)
            dve.tensor_tensor(MOD[:], MOD[:], vecs("ada_b", 48), ALU.add)
            dve.drain()
            for g, at, w in (("pre1", 8, "pre1"), ("post1", 16, "post1"), ("pre2", 32, "pre2"), ("post2", 40, "post2")):
                dve.scalar_tensor_tensor(vecs(g + "_g", 8), MOD[:, at:at + 8], 1.0, vecs(w + "_w", 8),
                                         ALU.add, ALU.mult)
            dve.drain().then_inc(gains_made, 1)
            norm_sum_blocks(2)
            dve.wait_ge(norm_rs, 3)
            for j in range(KB):
                dve.scalar_tensor_tensor(H[:, j, :], H[:, j, :], vec("final_norm_w", j), WK[:, 4, :],
                                         ALU.mult, ALU.mult).then_inc(norm_lo, 1)

            norm_sum_blocks(3)
            norm_split(3, 2, H, lambda j: vec("pre1_g", j), lambda j: MOD[:, j:j + 1])
            dve.wait_ge(gla_a2, 1)
            for b in range(2):
                dve.tensor_scalar(WK[:, b, :], aux(2 * b), vec("gla_a_b", b), None, ALU.add)
            dve.drain()
            for b in range(2):
                dve.scalar_tensor_tensor(WK[:, 2 + b, :], WK[:, b, :], -1.0, WK[:, b, :], ALU.mult, ALU.min)
            dve.drain().then_inc(gla_x, 1)
            dve.memset(WK[:, 14, :], 0.0)
            dve.memset(WK[:, 16, :], 0.0)
            dve.memset(WK[:, 17, 0:P], 0.0)
            for b in range(2):
                dve.wait_ge(gla_ln, b + 1)
                dve.scalar_tensor_tensor(WK[:, b, :], WK[:, b, :], 0.0, WK[:, 2 + b, :], ALU.min, ALU.subtract)
            dve.drain()
            for b in range(2):
                dve.tensor_scalar(WK[:, b, :], WK[:, b, :], 1.0 / 16, None, ALU.mult)
            dve.wait_ge(h_saved, 16 * KB)
            dve.drain().then_inc(gl["free"], 1)
            with dve.Fori(0, 2) as i:
                dve.wait_ge(gl["free"], i + 1)
                la_gaps(gl, 2, 9, 10, WK[:, ds(i, 1), :].rearrange("p a t -> p (a t)"))
                dve.wait_ge(tile_done, i * 6 + (TILE0["gla_w"] + 2))
                dve.tensor_scalar(WK[:, 3, :], slot(1), 0.125, None, ALU.mult).then_inc(slot_free[1], 1)
                dve.drain()
                dve.wait_ge(gl["exps"], i + 1)
                dve.tensor_tensor(WK[:, 11, :], WK[:, 3, :], WK[:, 12, :], ALU.mult)
                dve.tensor_tensor(half_row(9, 0), chunks(3)[:, :, 32:CH], half_row(9, 1), ALU.mult)
                dve.wait_ge(slot_free[1], i * 3 + (UNIT0["gla_w"] // 2 + 2))
                dve.tensor_tensor(WK[:, 10, :], WK[:, 4, :], WK[:, 10, :], ALU.mult).then_inc(gl["kd"], 1)
                dve.tensor_tensor(WK[:, 13, :], WK[:, 4, :], WK[:, 13, :], ALU.mult).then_inc(gl["keys"], 1)
                la_core(gl, i, 2, 64, [14, 16], 17, 12, 2)
                for hh in range(2):
                    dve.wait_ge(gl["rs"], i * 2 + hh + 1)
                    dve.scalar_tensor_tensor(WK[:, 3, :], aux(0), vec_at("gla_norm_w", i * 2 + hh), WK[:, 2, :],
                                             ALU.mult, ALU.mult)
                    dve.drain()
                    dve.tensor_tensor(h_at(i * 2 + hh), WK[:, 3, :], WK[:, 7 + hh, :], ALU.mult
                                      ).then_inc(gl["y"], 1)
                    dve.drain()
                dve.drain().then_inc(gl["free"], 1)

            def row(s):
                return WK[0:4, s, :]

            def tiles(s):
                return row(s).rearrange("p (t c) -> p t c", c=P)

            ip, x, ln, M, Bc, reset, A, mprev, ib = 0, 1, 2, 3, 4, 5, 6, 8, 12
            bias = VEC["ml_if_b"]
            dve.tensor_scalar(row(ip), WK[32:36, 15, :], CONST_V[32:36, bias:bias + 1], None, ALU.add)
            dve.tensor_scalar(row(x), WK[64:68, 15, :], CONST_V[64:68, bias:bias + 1], None, ALU.add)
            dve.drain()
            dve.scalar_tensor_tensor(row(ln), row(x), -1.0, row(x), ALU.mult, ALU.min)
            dve.drain().then_inc(m["rows"], 1)
            dve.memset(row(reset), 1.0)
            dve.memset(row(mprev)[:, 0:TT], 0.0)
            dve.drain()
            dve.memset(tiles(reset)[:, :, 0:1], 0.0)
            dve.wait_ge(m["ln"], 1)
            dve.scalar_tensor_tensor(row(x), row(x), 0.0, row(ln), ALU.min, ALU.subtract)
            dve.drain()
            dve.tensor_tensor_scan(row(M), row(x), row(ip), 0.0, ALU.add, ALU.max)
            dve.tensor_tensor_scan(row(Bc), row(reset), row(x), 0.0, ALU.mult, ALU.add)
            dve.drain()
            dve.tensor_tensor(row(A), row(Bc), row(M), ALU.subtract)
            dve.tensor_tensor(row(ib), row(ip), row(Bc), ALU.subtract)
            dve.tensor_copy(row(mprev)[:, 1:TT], tiles(M)[:, 0:TT - 1, P - 1])
            dve.drain()
            dve.tensor_tensor(tiles(9), tiles(A), row(mprev)[:, 0:TT, None].to_broadcast([4, TT, P]), ALU.add)
            dve.tensor_tensor(tiles(16), tiles(ib), tiles(A)[:, :, P - 1:P].to_broadcast([4, TT, P]), ALU.add)
            dve.tensor_copy(row(13), row(A))
            dve.drain()
            XQ, XK = wk(0, 2), wk(17, 2)
            dve.memset(XQ[:, 0:3], 0.0)
            dve.memset(XK[:, 0:3], 0.0)
            dve.drain().then_inc(m["gates"], 1)

            def tt(out_, a, b, op):
                dve.tensor_tensor(out_, a, b, op)

            def cmul(outr, outi, a, b, tmp, neg_i=False):
                tt(tmp[0], a[0], b[0], ALU.mult)
                tt(tmp[1], a[1], b[1], ALU.mult)
                tt(tmp[2], a[0], b[1], ALU.mult)
                tt(tmp[3], a[1], b[0], ALU.mult)
                dve.drain()
                tt(outr, tmp[0], tmp[1], ALU.subtract)
                if neg_i:
                    dve.scalar_tensor_tensor(outi, tmp[2], -1.0, tmp[3], ALU.mult, ALU.subtract)
                else:
                    tt(outi, tmp[2], tmp[3], ALU.add)
                dve.drain()

            def s5_parameters():
                dve.wait_ge(s5["dt"], 1)
                lr, li, dt, u, th = S5P(0), S5P(1), S5P(3), S5P(4), S5P(5)
                ta, tb, r = S5P(8), S5P(16), S5P(9)
                dve.tensor_scalar(lr, lr, -1e-4, None, ALU.min)
                tt(th, li, dt, ALU.mult)
                dve.drain()
                tt(u, lr, dt, ALU.mult)
                dve.tensor_scalar(ta, th, TURN_INV, ROUND, ALU.mult, ALU.add)
                dve.drain()
                dve.tensor_scalar(ta, ta, -ROUND, None, ALU.add)
                dve.drain()
                src = th
                for part in TURN:
                    dve.scalar_tensor_tensor(r, ta, -part, src, ALU.mult, ALU.add)
                    dve.drain()
                    src = r
                dve.tensor_scalar(r, r, PI, -PI, ALU.min, ALU.max)
                dve.drain().then_inc(s5["angle"], 1)
                tt(ta, lr, lr, ALU.mult)
                tt(tb, li, li, ALU.mult)
                dve.drain()
                tt(ta, ta, tb, ALU.add)
                dve.drain()
                dve.reciprocal(ta, ta)
                dve.wait_ge(s5["trig"], 1)
                mag, mag8, sn, cs, ar, ai, zr, zi = (S5P(k) for k in (6, 7, 10, 11, 12, 13, 14, 15))
                tt(cs, cs, cs, ALU.mult)
                dve.drain()
                dve.tensor_scalar(cs, cs, -2.0, 1.0, ALU.mult, ALU.add)
                dve.drain()
                tt(ar, mag, cs, ALU.mult)
                tt(ai, mag, sn, ALU.mult)
                dve.drain()
                t4 = [WK[:, 16, 256 * k:256 * k + 16] for k in range(4)]
                dve.tensor_scalar(tb, ar, -1.0, None, ALU.add)
                dve.drain()
                tt(t4[0], tb, lr, ALU.mult)
                tt(t4[1], ai, li, ALU.mult)
                tt(t4[2], ai, lr, ALU.mult)
                tt(t4[3], tb, li, ALU.mult)
                dve.drain()
                tt(zr, t4[0], t4[1], ALU.add)
                tt(zi, t4[2], t4[3], ALU.subtract)
                dve.drain()
                tt(zr, zr, ta, ALU.mult)
                tt(zi, zi, ta, ALU.mult)
                dve.drain()

                def pairs(at):
                    return WK[:, 15, at:at + 256].rearrange("p (j c) -> p j c", c=16)

                def over_c(x):
                    return x[:, :, None].to_broadcast([P, 16, 16])
                tb4 = [WK[:, 16, 256 * k:256 * k + 256].rearrange("p (j c) -> p j c", c=16) for k in range(4)]
                cmul(pairs(0), pairs(256), (pairs(0), pairs(256)), (over_c(zr), over_c(zi)), tb4)
                def table(k):
                    return WK[:, 14, 512 + 128 * k:640 + 128 * k].rearrange("p (j l) -> p j l", l=8)
                fr, fi, rr, ri_ = (table(k) for k in range(4))
                dve.memset(rr[:, :, 7:8], 1.0)
                dve.memset(ri_[:, :, 7:8], 0.0)
                dve.tensor_copy(fr[:, :, 0], ar)
                dve.tensor_copy(fi[:, :, 0], ai)
                dve.drain()
                for l in range(1, 8):
                    cmul(fr[:, :, l], fi[:, :, l], (fr[:, :, l - 1], fi[:, :, l - 1]), (ar, ai), t4)
                    dve.tensor_copy(rr[:, :, 7 - l], fr[:, :, l - 1])
                    dve.tensor_copy(ri_[:, :, 7 - l], fi[:, :, l - 1])
                e = [(S5P(18 + 2 * k), S5P(19 + 2 * k)) for k in range(7)]
                cmul(ta, tb, (cs, sn), (cs, sn), t4)
                cmul(ta, tb, (ta, tb), (ta, tb), t4)
                cmul(*e[0], (ta, tb), (ta, tb), t4)
                for k in range(1, 7):
                    cmul(*e[k], e[k - 1], e[k - 1], t4)

            def conv(xp, out_, j):
                dve.tensor_scalar(out_, xp[:, 3:3 + T], vec("ml_conv_w", 12 + j), vec("ml_conv_b", j),
                                  ALU.mult, ALU.add)
                for k in range(3):
                    dve.drain()
                    dve.scalar_tensor_tensor(out_, xp[:, k:k + T], vec("ml_conv_w", 4 * k + j), out_,
                                             ALU.mult, ALU.add)
                dve.drain().then_inc(m["conv"], 1)

            dec, den = WK[:, 19, ML_AT + 64:ML_AT + 72], WK[:, 19, ML_AT + 80:ML_AT + 88]
            for b in range(2):
                if b:
                    s5_parameters()
                for n, xp in enumerate((XQ, XK)):
                    dve.wait_ge(slot_free[n], UNIT0["ml_w"] // 2 + 3 * b + 1)
                    conv(xp, WK[:, 2 + n, :], 2 * n + b)
                if not b:
                    dve.wait_ge(m["turned_rows"], 1)
                    dve.tensor_copy(WK[:, 19, ML_AT:ML_AT + 64], PX[:, 0, 0:64]).then_inc(m["tok"], 1)
                    dve.memset(WK[:, 10, 0:P], 0.0)
                    dve.memset(WK[:, 19, ML_AT + 72:ML_AT + 73], 0.0)
                dve.wait_ge(m["silu"], 2 * b + 2)
                dve.wait_ge(m["spread"], b + 1)
                dve.tensor_tensor(WK[:, 8, :], WK[:, 2, :], aux(0), ALU.mult)
                dve.tensor_copy(dec, aux(0).rearrange("p (t c) -> p t c", c=P)[:, :, P - 1])
                dve.scalar_tensor_tensor(WK[:, 9, :], WK[:, 3, :], 0.125, aux(2), ALU.mult, ALU.mult)
                dve.drain()
                dve.tensor_scalar(WK[:, 3, :], WK[:, 3, :], 0.125, None, ALU.mult).then_inc(m["kw"], 1)
                dve.wait_ge(m["ds"], b + 1)
                for t in range(TT - 1):
                    dve.scalar_tensor_tensor(WK[:, 10, P * (t + 1):P * (t + 2)], WK[:, 10, P * t:P * (t + 1)],
                                             dec[:, t:t + 1], PX[:, 2 + t // 4, P * (t % 4):P * (t % 4) + P],
                                             ALU.mult, ALU.add)
                    dve.drain()
                dve.tensor_tensor_scan(WK[:, 19, ML_AT + 73:ML_AT + 80], dec[:, 0:7], PX[:, 0, 0:7], 0.0, ALU.mult, ALU.add)
                dve.drain().then_inc(m["state"], 1)
                for hh in range(2):
                    head = 2 * b + hh
                    dve.wait_ge(m["e"], head + 1)
                    dve.tensor_tensor(WK[:, 11, :], WK[:, 11, :], aux(2), ALU.mult).then_inc(m["p"], 1)
                    dve.wait_ge(m["num"], head + 1)
                    dve.tensor_scalar(den, PX[:, 2, 0:TT], -1.0, None, ALU.mult)
                    dve.drain()
                    dve.tensor_tensor(den, den, PX[:, 2, 0:TT], ALU.max)
                    dve.drain()
                    dve.tensor_tensor(den, den, WK[:, 19, ML_AT + 32:ML_AT + 64].rearrange("p (t h) -> p t h", h=4)[:, :, head],
                                      ALU.max)
                    dve.drain()
                    dve.reciprocal(den, den)
                    dve.drain()
                    dve.tensor_tensor(WK[:, 12, :].rearrange("p (t c) -> p t c", c=P),
                                      aux(0).rearrange("p (t c) -> p t c", c=P),
                                      den[:, :, None].to_broadcast([P, TT, P]), ALU.mult).then_inc(m["h"], 1)
                    dve.wait_ge(m["ht"], head + 1)
                    dve.tensor_tensor(H[:, 4 + head, :], aux(2), WK[:, 6 + hh, :], ALU.mult).then_inc(m["y"], 1)

            for n in range(2):
                dve.wait_ge(slot_free[n], UNIT0["s5_w"] // 2 + 2)

            def half(s_, h):
                return WK[:, s_, 512 * h:512 * h + 512].rearrange("p (j l c) -> p j l c", j=4, l=8)

            def seq(s_, h):
                return WK[:, s_, 512 * h:512 * h + 512].rearrange("p (j n) -> p j n", j=4)

            def bc(x):
                return x.rearrange("p (j c) -> p j c", c=16)[:, :, None, :].to_broadcast([P, 4, 8, 16])

            def pw(i, k):
                return WK[:, 14, ds(i * 32 + (512 + 128 * k), 32)].rearrange("p (j l) -> p j l", l=8)[
                    :, :, :, None].to_broadcast([P, 4, 8, 16])

            def coef(i, k):
                return WK[:, 15, ds(i * 64 + 256 * k, 64)]

            def padded(s_):
                return WK[:, s_, 0:960].rearrange("p (j l c) -> p j l c", j=4, l=15)[:, :, 0:8, :]

            t4_ = [half(9 + k // 2, k % 2) for k in range(4)]
            q4 = [seq(9 + k // 2, k % 2) for k in range(4)]
            ec, es = seq(7, 0), seq(7, 1)
            mt = WK[:, 13, 256:768]
            mtj = mt.rearrange("p (j n) -> p j n", j=4)

            def s5_tables(i):
                dve.tensor_copy(WK[:, 12, :], WK[:, ds(i + 16, 1), :].rearrange("p a t -> p (a t)"))
                for ri in range(2):
                    for g in range(2):
                        rows = slice(64 * g, 64 * g + 64)
                        dve.tensor_scalar(
                            WK[rows, 13, P * ri:P * ri + P].rearrange("p (j g c) -> p j g c", g=2, c=16)[:, :, g],
                            coef(i, 2 + ri)[rows].rearrange("p (j c) -> p j c", c=16), 1.0 - 2.0 * ri, None, ALU.mult)
                cmul(padded(0), padded(1), (bc(coef(i, 0)), bc(coef(i, 1))), (pw(i, 2), pw(i, 3)), t4_)
                dve.drain().then_inc(s5["g"], 1)
                for k in range(7):
                    w = 2 ** k

                    def ek(p):
                        return WK[:, 14, ds(i * 4 + 16 * (18 + 2 * k + p), 4)][:, :, None].to_broadcast([P, 4, w])
                    cmul(ec[:, :, w:2 * w], es[:, :, w:2 * w], (ec[:, :, 0:w], es[:, :, 0:w]), (ek(0), ek(1)),
                         [x[:, :, 0:w] for x in q4])
                dve.tensor_copy(mtj[:, :, 1:P], WK[:, 14, ds(i * 4 + 16 * 7, 4)][:, :, None].to_broadcast([P, 4, P - 1]))
                dve.drain()

            def s5_readout(i):
                cmul(half(2, 0), half(2, 1), (bc(coef(i, 2)), bc(coef(i, 3))), (pw(i, 0), pw(i, 1)), t4_)

            def s5_states(i):
                dve.wait_ge(s5["v"], i + 1)
                vr, vi = (PX[:, k, :].rearrange("p (j n) -> p j n", j=4)[:, :, 0:P - 1] for k in range(2))
                c1, s1 = ec[:, :, 1:P], es[:, :, 1:P]
                q1 = [x[:, :, 1:P] for x in q4]
                tt(q1[0], c1, vr, ALU.mult)
                tt(q1[1], s1, vi, ALU.mult)
                tt(q1[2], c1, vi, ALU.mult)
                tt(q1[3], s1, vr, ALU.mult)
                dve.drain()
                W = [seq(11, 0), seq(11, 1)]
                tt(W[0][:, :, 1:P], q1[0], q1[1], ALU.add)
                tt(W[1][:, :, 1:P], q1[2], q1[3], ALU.subtract)
                dve.memset(WK[:, 11, :].rearrange("p (j n) -> p j n", j=8)[:, :, 0:1], 0.0)
                dve.drain()
                for k in range(2):
                    w_ = WK[:, 11, 512 * k:512 * k + 512]
                    dve.tensor_tensor_scan(w_, mt, w_, 0.0, ALU.mult, ALU.add)
                dve.drain()
                cmul(seq(8, 0), seq(8, 1), (ec, es), (W[0], W[1]), q4, neg_i=True)
                dve.drain().then_inc(s5["x"], 1)

            def s5_output(i):
                dve.wait_ge(s5["back"], i + 1)
                y = WK[:, ds(i + 16, 1), :].rearrange("p a (n l) -> p (a l) n", l=8)
                dve.scalar_tensor_tensor(y, y, vec_at("s5_d", i), aux(0).rearrange("p (l n) -> p l n", l=8),
                                         ALU.mult, ALU.add).then_inc(s5["pre_gelu"], 1)

            dve.drain()
            dve.memset(WK[:, 0:2, :], 0.0)
            dve.memset(WK[:, 13, 0:768], 0.0)
            dve.memset(ec[:, :, 0:1], 1.0)
            dve.memset(es[:, :, 0:1], 0.0)
            dve.drain()
            s5_tables(0)
            s5_readout(0)
            with dve.Fori(0, 3) as i:
                s5_states(i)
                s5_tables(i + 1)
                s5_output(i)
                s5_readout(i + 1)
            s5_states(3)
            s5_output(3)
            for j in range(4):
                dve.wait_ge(glu_hi, j + 1)
                dve.tensor_tensor(GLO[:, j, :], WK[:, 16 + j, :], GH[:, j, :].bitcast(F32), ALU.subtract
                                  ).then_inc(glu_lo, 1)
            for n in range(4):
                dve.wait_ge(slot_free[n % 2], UNIT0["glu_w"] // 2 + n // 2 + 1)
                dve.tensor_tensor(WK[:, 16 + n, :], WK[:, 16 + n, :], WK[:, 8 + n, :], ALU.mult).then_inc(glu_y, 1)

            dve.drain()
            for hf in range(2):
                tok = slice(512 * hf, 512 * hf + 512)
                for k in range(12):
                    dve.wait_ge(mix_hi, 12 * hf + k + 1)
                    raw = H[:, k, tok] if k < 8 else WK[:, 8 + k, tok]
                    dve.tensor_tensor(YL[:, k, :], raw, YH[:, k, :].bitcast(F32), ALU.subtract).then_inc(mix_lo, 1)
                with dve.Fori(0, 4) as i:
                    for n in range(6):
                        s_ = n % 2
                        g = WK[:, 13, 512 * s_:512 * s_ + 512]
                        tmp_ = WK[:, 14, 512 * s_:512 * s_ + 512]
                        M_ = H[:, ds(i * 2 + n // 3, 1), tok].rearrange("p a t -> p (a t)")
                        dve.wait_ge(mix_sig, i * 6 + (24 * hf + n + 1))
                        dve.wait_ge(tile_done, i * 12 + (TILE0[f"mix{hf}"] + 2 * n + 2))
                        dve.tensor_tensor(tmp_ if n % 3 else M_, g, PG[:, 2 * s_ + 1, :], ALU.mult
                                          ).then_inc(slot_free[s_], 1)
                        dve.drain()
                        if n % 3:
                            ins = dve.tensor_tensor(M_, M_, tmp_, ALU.add)
                            if n % 3 == 2:
                                ins.then_inc(m_ready, 1)
                            dve.drain()
            for j in range(KB):
                dve.wait_ge(sp_hi, 8 + j + 1)
                dve.tensor_tensor(UL[:, j, :], H[:, j, :], UH[:, j, :].bitcast(F32),
                                  ALU.subtract).then_inc(sp_lo, 1)
            norm_sum_blocks(4, 8)
            dve.wait_ge(h_reloaded, 16 * 2 * KB)
            norm_residual(4, lambda j: [(slice(0, T), WK[:, j, :])], lambda j: vec("post1_g", j), H, 8)
            norm_sum_blocks(5)
            norm_split(5, 3, H, lambda j: vec("pre2_g", j), lambda j: MOD[:, 24 + j:25 + j])

            dve.wait_ge(h_saved, 16 * 2 * KB)
            for hf in range(2):
                for HL, i0, i1 in ((HL1, 0, 8), (HL2, 8, 11)):
                    with dve.Fori(i0, i1) as i:
                        for n in range(2):
                            g = WK[:, 18, 512 * n:512 * n + 512]
                            t_ = WK[:, 19, 512 * n:512 * n + 512]
                            dve.wait_ge(ffn_silu, i * 2 + (22 * hf + n + 1))
                            dve.wait_ge(tile_done, i * 4 + (TILE0[f"up{hf}"] + 2 * n + 2))
                            dve.tensor_tensor(t_, g, PG[:, 2 * n + 1, :], ALU.mult).then_inc(slot_free[n], 1)
                            dve.drain().then_inc(ffn_t, 1)
                            dve.wait_ge(ffn_hi, i * 2 + (22 * hf + n + 1))
                            dve.tensor_tensor(HL[:, ds(i * 2 + (n - 2 * i0), 1), :].rearrange("p a t -> p (a t)"), t_,
                                              HH[:, ds(i * 2 + n, 1), :].rearrange("p a t -> p (a t)").bitcast(F32),
                                              ALU.subtract).then_inc(ffn_lo, 1)
                            dve.drain()
            norm_sum_blocks(6)
            dve.wait_ge(x_reloaded, 16 * KB)
            norm_residual(6, lambda j: [(slice(512 * h, 512 * h + 512), YF[h][:, j, :]) for h in range(2)],
                          lambda j: vec("post2_g", j), XR, 0)



def pack_weight(w, kbs=8):
    import numpy as np
    k, n = w.shape
    return np.ascontiguousarray(w.reshape(k // P, P, n // P, P).transpose(2, 1, 0, 3).reshape(n // P, P, k))


def pack_vectors(v):
    import numpy as np
    cols = []
    for name, n in VEC_SPEC:
        a = np.asarray(v[name]).reshape(-1)
        cols.append(a.reshape(n, P).T)
    return np.ascontiguousarray(np.concatenate(cols, axis=1))


def layout(inp):
    import numpy as np
    f = {k: np.asarray(v) for k, v in inp.items()}
    w_in = f["w_in"][0]
    blk = {n: w_in[:, 512 * j:512 * (j + 1)] for j, n in enumerate(("xa", "ga", "q", "f", "i", "g"))}

    def cols(name, j):
        return blk[name][:, P * j:P * (j + 1)]
    rg = np.concatenate([cols(n, j) for j in range(4) for n in ("xa", "ga")], axis=1)
    hg = np.concatenate([cols(n, j) for j in range(4) for n in ("f", "q", "i", "g")], axis=1)
    bd = np.zeros((P, 4, 2, P), np.float32)
    for j in range(4):
        for k, w in enumerate((f["rg_wa"][0], f["rg_wx"][0])):
            for g in range(2):
                bd[64 * g:64 * g + 64, j, k, 64 * g:64 * g + 64] = w[2 * j + g]
    names = (("gq", 256), ("gk", 256), ("gv", 512), ("ga", 16), ("gr", 512), ("mq", 256), ("mk", 256), ("mv", 512),
             ("mi", 4), ("mf", 4), ("mo", 512), ("su", 512), ("zg", 3072))
    at, w2 = 0, {}
    for n, k in names:
        w2[n] = f["w_in_2"][0][:, at:at + k]
        at += k

    def c2(name, j):
        return w2[name][:, P * j:P * (j + 1)]
    misc = np.zeros((D, P), np.float32)
    for n, o in (("ga", 0), ("mi", 32), ("mf", 64)):
        misc[:, o:o + w2[n].shape[1]] = w2[n]
    misc = pack_weight(misc)[0].reshape(P, 2, 4 * P).transpose(1, 0, 2)
    gla = np.concatenate([c2(n, j) for b in range(2) for n, j in (
        ("gk", b), ("gq", b), ("gv", 2 * b), ("gv", 2 * b + 1), ("gr", 2 * b), ("gr", 2 * b + 1))], axis=1)
    ml = np.concatenate([c2(n, j) for b in range(2) for n, j in (
        ("mq", b), ("mk", b), ("mv", 2 * b), ("mv", 2 * b + 1), ("mo", 2 * b), ("mo", 2 * b + 1))], axis=1)
    zg = np.concatenate([c2("zg", 8 * br + j) for j in range(8) for br in range(3)], axis=1)
    pr = [f["proj_gla_2"][0], f["proj_ml_2"][0], f["proj_s5_2"][0]]
    proj = np.concatenate([pr[br][:, P * j:P * (j + 1)] for j in range(8) for br in range(3)], axis=1)
    hidden = f["ffn_w_out_2"].shape[1]
    up = f["ffn_w_in_2"][0]
    up = np.concatenate([up[:, o + P * j:o + P * (j + 1)] for j in range(hidden // P) for o in (0, hidden)], axis=1)
    down = np.zeros((3 * D, D), np.float32)
    down[:hidden] = f["ffn_w_out_2"][0]
    down = pack_weight(down).reshape(KB, P, 3, D).transpose(0, 2, 1, 3).reshape(3 * KB, P, D)
    if_b = np.zeros((P,), np.float32)
    if_b[32:36], if_b[64:68] = f["ml_i_b_2"][0], f["ml_f_b_2"][0]
    sel = np.zeros((P, 6 * P), np.float32)
    for h in range(4):
        sel[h, P * h:P * (h + 1)] = 1.0
        for r in (32, 64):
            sel[r + h, 4 * P + 64 * h:4 * P + 64 * (h + 1)] = 1.0

    def states(a):
        return a.reshape(16, P, -1).transpose(1, 0, 2).reshape(P, -1)
    bc = [states(f[k][0]) for k in ("s5_b_re_2", "s5_b_im_2")]
    bc += [states(f[k][0].transpose(0, 2, 1)) for k in ("s5_c_re_2", "s5_c_im_2")]
    lam = [states(f[k][0]) for k in ("s5_lam_re_2", "s5_lam_im_2")]
    lam += [states(np.repeat(f["s5_log_step_2"][0], 64))]
    v = {**f, "ml_if_b": if_b, "glu_b": f["s5_glu_b_2"], "branch_b": f["branch_gate_b_2"]}
    for n in ("ada_b", "pre1_w", "post1_w", "pre2_w", "post2_w", "gla_a_b", "gla_norm_w", "ml_conv_w", "ml_conv_b",
              "s5_d"):
        v[n] = f[n + "_2"]
    arrays = {
        "x": f["x"][0].T, "p": f["p"][0, 0].T, "vec": pack_vectors(v), "rg_bd": bd.reshape(P, 8 * P),
        "rg_w": pack_weight(rg), "hg_w": pack_weight(hg), "out1_w": pack_weight(f["w_out"][0]),
        "ple_w": pack_weight(f["w_ple_proj"][0]), "gate_w": pack_weight(f["w_ple_gate"][0]),
        "ada_w": f["ada_w_2"][0].T.reshape(6 * KB, P, D), "c_row": np.repeat(f["c_2"], P, axis=0),
        "misc_w": misc, "gla_w": pack_weight(gla), "ml_w": pack_weight(ml), "s5_w": pack_weight(w2["su"]),
        "glu_w": pack_weight(f["s5_glu_w_2"][0]), "zg_w": pack_weight(zg), "proj_w": pack_weight(proj),
        "out2_w": pack_weight(f["w_out_2"][0]), "up_w": pack_weight(up), "down_w": down,
        "gla_a2": f["gla_a2_2"][0], "sel": sel, "s5_bc": np.concatenate(bc, axis=1),
        "s5_lam": np.concatenate(lam, axis=1),
    }
    return {k: np.ascontiguousarray(a) for k, a in arrays.items()}


def build(nc, names, *aps):
    program(nc, dict(zip(names, aps)), aps[-1])


def kernel(**inputs):
    import numpy as np
    import concourse.bacc as bacc
    from concourse.bass_utils import run_bass_kernel_spmd

    nc = bacc.Bacc("TRN2", target_bir_lowering=False, num_devices=1)
    arrays = layout(inputs)
    aps = [nc.dram_tensor(name, a.shape, mybir.dt.from_np(a.dtype), kind="ExternalInput").ap()
           for name, a in arrays.items()]
    out = nc.dram_tensor("out", (D, T), F32, kind="ExternalOutput").ap()
    build(nc, list(arrays), *aps, out)
    r = run_bass_kernel_spmd(nc, [arrays], core_ids=[0])
    return np.ascontiguousarray(r.results[0]["out"].T)[None]
```

```python
import concourse.bass as bass
from concourse import mybir

F32 = mybir.dt.float32
F32R = mybir.dt.float32r
ALU = mybir.AluOpType
ACT = mybir.ActivationFunctionType
ds = bass.ds

P = 128
D = 1024
T = 1024
KB = D // P
EPS = 1e-6
SBUF_BASE = 16512
BLOCK = T * 4
CH = 64
NCH = T // CH
TT = T // P
PI = 3.1415925
TURN_INV = 0.15915494309189535
ROUND = 1.5 * 2 ** 23
TURN = (6.28125, 0.0019350051879882812, 3.019916050e-07)

VEC_SPEC = [
    ("norm_mix_w", 8), ("conv_w", 16), ("conv_b", 4), ("rg_ba", 4), ("rg_bx", 4), ("rg_lambda", 4),
    ("hg_lb", 8), ("hg_norm_w", 1), ("ple_norm_w", 8), ("b_ple_gate", 8), ("final_norm_w", 8),
    ("ada_b", 48), ("pre1_w", 8), ("post1_w", 8), ("pre2_w", 8), ("post2_w", 8), ("gla_a_b", 2),
    ("gla_norm_w", 4), ("ml_conv_w", 16), ("ml_conv_b", 4), ("ml_if_b", 1), ("s5_d", 4), ("glu_b", 4),
    ("branch_b", 24),
]
VEC_MADE = [
    ("zero", 8), ("eps", 1), ("one", 1), ("rg_s8", 4), ("neg_rg_s8", 4), ("lb", 4), ("one_minus_lb", 4), ("tmp", 24),
    ("pre1_g", 8), ("post1_g", 8), ("pre2_g", 8), ("post2_g", 8),
]


def columns(spec, at=0):
    found = {}
    for name, n in spec:
        found[name] = at
        at += n
    return found, at


VEC, N_VEC = columns(VEC_SPEC)
VEC_ON_CHIP, N_VEC_ALL = columns(VEC_MADE, N_VEC)
VEC.update(VEC_ON_CHIP)

STREAM = [
    ("rg_w", 8, (8, 8)), ("hg_w", 16, (8, 8)), ("out1_w", 8, (8, 8)), ("ple_w", 8, (2, 2)),
    ("gate_w", 8, (8, 8)), ("misc_w", 2, (4, 4)), ("gla_w", 12, (8, 8)), ("ml_w", 12, (8, 8)),
    ("s5_w", 4, (8, 8)), ("glu_w", 4, (4, 4)), ("mix0", 48, (6, 6)), ("mix1", 48, (6, 6)),
    ("out2_w", 8, (8, 8)), ("up0", 44, (8, 8)), ("down0", 24, (8, 8)), ("up1", 44, (8, 8)),
    ("down1", 24, (8, 8)),
]
SOURCE = {"mix0": "mix_w", "mix1": "mix_w", "up0": "up_w",
          "up1": "up_w", "down0": "down_w", "down1": "down_w"}
TILE0, N_TILES = columns([(name, n) for name, n, _ in STREAM])
UNIT0, N_UNITS = columns([
    ("rg_w", 8), ("hg_w", 16), ("out1_w", 8), ("ple_w", 8), ("gate_w", 8), ("misc_w", 2), ("gla_w", 12),
    ("ml_w", 12), ("s5_w", 4), ("glu_w", 4), ("mix0", 24), ("mix1", 24), ("out2_w", 8), ("up0", 22),
    ("down0", 4), ("up1", 22), ("down1", 4)])


DVE_NORMS = (0, 1, 2, 4, 6, 7)
PE_NORMS = (3, 5)


def program(nc, dram, out):
    def sb(name, blocks, shape, dt=F32):
        return nc.alloc_sbuf_tensor_at(name, [P, *shape], dt, offset=SBUF_BASE + int(blocks * BLOCK))

    def sem(name):
        return nc.alloc_semaphore(name)

    H = sb("H", 0, [8, T])
    UH = sb("UH", 8, [8, T], F32R)
    UL = sb("UL", 16, [8, T], F32R)
    WRAW = sb("WRAW", 24, [2, T])
    WH = sb("WH", 26, [2, T], F32R)
    WL = sb("WL", 28, [2, T], F32R)
    WK = sb("WK", 30, [20, T])
    ADA = sb("ADA", 47, [3, T])
    consts = [SBUF_BASE + 50 * BLOCK]

    def const(name, shape, dt=F32):
        t = nc.alloc_sbuf_tensor_at(name, [P, *shape], dt, offset=consts[0])
        n = 4
        for k in shape:
            n *= k
        consts[0] += n
        return t

    ONES = const("ONES", [P])
    IDENT = const("IDENT", [P])
    IDENT_R = const("IDENT_R", [P], F32R)
    NEGMASK = const("NEGMASK", [P], F32R)
    MASK = const("MASK", [CH])
    RESET = const("RESET", [T])
    C_ROW = WK[:, 16, :]
    ML_AT = 768
    A2W = WK[0:16, 19, 768:1024]
    SEL = WK[:, 19, 0:768]
    YH = sb("YH", 30, [12, 512], F32R)
    YL = sb("YL", 36, [12, 512], F32R)
    RESP = 768
    GH = sb("GH", 30, [4, T], F32R)
    GLO = sb("GLO", 34, [4, T], F32R)
    HH = sb("HH", 30, [22, 512], F32R)
    HL1 = sb("HL1", 0, [16, 512], F32R)
    HL2 = sb("HL2", 41, [6, 512], F32R)
    YF = [sb("YF0", 44, [8, 512]), sb("YF1", 16, [8, 512])]
    XR = sb("XR", 8, [8, T])
    h_save = nc.dram_tensor("h_save", [D, T], F32, kind="Internal").ap()
    TOUCH = const("TOUCH", [8])
    MOD = const("MOD", [48])
    CONST_V = const("CONST_V", [N_VEC_ALL])
    PH = sb("PH", 45, [2, T], F32R)
    PL = sb("PL", 47, [2, T], F32R)
    PG = nc.alloc_psum_tensor("PG", [P, 4, 512], F32)
    PX = nc.alloc_psum_tensor("PX", [P, 4, 512], F32)

    def vec(name, j=0):
        return CONST_V[:, VEC[name] + j:VEC[name] + j + 1]

    def vec_at(name, i):
        return CONST_V[:, ds(i + VEC[name], 1)]

    def vecs(name, n):
        return CONST_V[:, VEC[name]:VEC[name] + n]

    def wk(s, n=1):
        return WK[:, s:s + n, :].rearrange("p a t -> p (a t)")

    vec_loaded = sem("vec_loaded")
    x_loaded = [sem(f"x_loaded{j}") for j in range(4)]
    c_loaded = sem("c_loaded")
    bd_loaded = sem("bd_loaded")
    w_loaded = [sem(f"w_loaded{r}") for r in range(2)]
    ada_loaded = [sem(f"ada_loaded{r}") for r in range(3)]
    w_split = sem("w_split")
    tile_done = sem("tile_done")
    slot_free = [sem(f"slot_free{s}") for s in range(2)]
    ada_done = sem("ada_done")
    consts_made = sem("consts_made")
    pre_dve = sem("pre_dve")
    pre_act = sem("pre_act")
    norm_sq = sem("norm_sq")
    norm_acc = sem("norm_acc")
    norm_used = sem("norm_used")
    norm_ms = sem("norm_ms")
    norm_rs = sem("norm_rs")
    norm_t = sem("norm_t")
    norm_hi = sem("norm_hi")
    norm_lo = sem("norm_lo")
    rg_conv = sem("rg_conv")
    rg_gates = sem("rg_gates")
    rg_sig = sem("rg_sig")
    rg_decay = sem("rg_decay")
    rg_q = sem("rg_q")
    rg_mult = sem("rg_mult")
    rg_done = sem("rg_done")
    out_saved = sem("out_saved")
    la_names = (
        "sig", "logf", "gaps", "exps", "kd", "keys", "turned", "turned_copied", "scores", "attn", "ds", "state",
        "o", "sq", "ms", "rs", "y", "free")
    hg = {n: sem(f"hg_{n}") for n in la_names}
    gl = {n: sem(f"gla_{n}") for n in la_names}
    sp_hi = sem("sp_hi")
    sp_lo = sem("sp_lo")
    ple_hi = sem("ple_hi")
    ple_ready = sem("ple_ready")
    rg_ogate = sem("rg_ogate")
    gate_added = sem("gate_added")
    h_reloaded = sem("h_reloaded")
    p_loaded = [sem(f"p_loaded{j}") for j in range(2)]
    h_saved = sem("h_saved")
    small_loaded = sem("small_loaded")
    gains_made = sem("gains_made")
    misc_out = sem("misc_out")
    gla_a2 = sem("gla_a2")
    gla_x = sem("gla_x")
    gla_ln = sem("gla_ln")
    m = {n: sem(f"ml_{n}") for n in (
        "rows", "ln", "gates", "exps", "turned_rows", "tok", "conv", "silu", "spread", "kw", "turned",
        "turned_copied", "ds", "state", "scores", "e", "p", "num", "h", "ht", "y")}
    s5 = {n: sem(f"s5_{n}") for n in (
        "loaded", "dt", "angle", "trig", "parameters", "phasors", "phasors_used", "g", "resp", "resp_copied", "kt",
        "kt_copied", "gt", "gt_copied", "tok", "tok_copied", "u", "u_copied", "v", "x", "y", "y_copied", "back",
        "pre_gelu")}
    glu_hi = sem("glu_hi")
    glu_lo = sem("glu_lo")
    glu_y = sem("glu_y")
    mix_hi = sem("mix_hi")
    mix_lo = sem("mix_lo")
    mix_sig = sem("mix_sig")
    m_ready = sem("m_ready")
    x_reloaded = sem("x_reloaded")
    ffn_silu = sem("ffn_silu")
    ffn_t = sem("ffn_t")
    ffn_hi = sem("ffn_hi")
    ffn_lo = sem("ffn_lo")

    def S5P(k):
        return WK[:, 14, 16 * k:16 * k + 16]

    def slot(s):
        return PG[:, 2 * s:2 * s + 2, :].rearrange("p b t -> p (b t)")

    def aux(b, n=2):
        return PX[:, b:b + n, :].rearrange("p b t -> p (b t)")

    block = nc.Block()
    with block:
        @block.sync
        def _(sp):
            def weight_pair(name, pair):
                _, n, kbs = next(s for s in STREAM if s[0] == name)
                t0 = TILE0[name]
                for j in range(2):
                    if t0 or not isinstance(pair, int) or pair:
                        sp.wait_ge(w_split, pair * 2 + (t0 + j - 1))
                    src = dram[SOURCE.get(name, name)][ds(pair * 2 + j, 1)]
                    sp.dma_start(WRAW[:, j, 0:kbs[j] * P], src.rearrange("a p c -> (a p) c")
                                 ).then_inc(w_loaded[j], 16)

            def ada_tiles(first, n):
                for j in range(n):
                    if not isinstance(first, int) or first + j >= 3:
                        sp.wait_ge(ada_done, first + (j - 3 + 1))
                    sp.dma_start(ADA[:, j % 3, :], dram["ada_w"][ds(first + j, 1)].rearrange("a p c -> (a p) c")
                                 ).then_inc(ada_loaded[j % 3], 16)

            sp.dma_start(CONST_V[:, 0:N_VEC], dram["vec"]).then_inc(vec_loaded, 16)
            for j in range(KB):
                sp.dma_start(H[:, j, :], dram["x"][j * P:(j + 1) * P, :]).then_inc(x_loaded[j // 2], 16)
            weight_pair("rg_w", 0)
            sp.dma_start(WK[:, 14, :], dram["rg_bd"]).then_inc(bd_loaded, 16)
            sp.dma_start(C_ROW, dram["c_row"]).then_inc(c_loaded, 16)
            ada_tiles(0, 3)
            with sp.Fori(1, 4) as i:
                weight_pair("rg_w", i)
                ada_tiles(i * 3, 3)
            with sp.Fori(0, 4) as i:
                weight_pair("hg_w", i * 2)
                weight_pair("hg_w", i * 2 + 1)
                ada_tiles(i * 9 + 12, 9)
            weight_pair("out1_w", 0)
            sp.wait_ge(ada_done, 6 * KB)
            for j in range(2):
                sp.dma_start(WK[:, 19 - j, :], dram["p"][j * P:(j + 1) * P, :]).then_inc(p_loaded[j], 16)
            for j in range(KB):
                sp.wait_ge(sp_lo, j + 1)
                sp.dma_start(H[:, j, :], dram["x"][j * P:(j + 1) * P, :]).then_inc(x_loaded[j // 2], 16)
                if j in (5, 6, 7):
                    weight_pair("out1_w", j - 4)
            with sp.Fori(0, 4) as i:
                weight_pair("ple_w", i)
            with sp.Fori(0, 4) as i:
                weight_pair("gate_w", i)

            weight_pair("misc_w", 0)
            sp.wait_ge(norm_lo, 8 * 3)
            sp.dma_start(A2W, dram["gla_a2"]).then_inc(small_loaded, 16)
            sp.dma_start(SEL, dram["sel"]).then_inc(small_loaded, 16)
            for j in range(KB):
                sp.dma_start(h_save[j * P:(j + 1) * P, :], H[:, j, :]).then_inc(h_saved, 16)
            with sp.Fori(0, 6) as i:
                weight_pair("gla_w", i)
            with sp.Fori(0, 3) as i:
                weight_pair("ml_w", i)
            sp.wait_ge(m["gates"], 1)
            sp.dma_start(WK[:, 15, :], dram["s5_bc"]).then_inc(s5["loaded"], 16)
            sp.dma_start(WK[:, 14, 0:48], dram["s5_lam"]).then_inc(s5["loaded"], 16)
            with sp.Fori(3, 6) as i:
                weight_pair("ml_w", i)
            weight_pair("s5_w", 0)
            weight_pair("s5_w", 1)
            weight_pair("glu_w", 0)
            weight_pair("glu_w", 1)
            for name in ("mix0", "mix1"):
                with sp.Fori(0, 24) as i:
                    weight_pair(name, i)
            weight_pair("out2_w", 0)
            sp.wait_ge(sp_lo, 16)
            for j in range(KB):
                if j in (0, 2, 4):
                    weight_pair("out2_w", j // 2 + 1)
                sp.dma_start(H[:, j, :], h_save[j * P:(j + 1) * P, :]).then_inc(h_reloaded, 16)
            weight_pair("up0", 0)
            sp.wait_ge(norm_lo, 8 * 5)
            for j in range(KB):
                sp.dma_start(h_save[j * P:(j + 1) * P, :], H[:, j, :]).then_inc(h_saved, 16)
            with sp.Fori(1, 22) as i:
                weight_pair("up0", i)
            with sp.Fori(0, 12) as i:
                weight_pair("down0", i)
            with sp.Fori(0, 22) as i:
                weight_pair("up1", i)
            weight_pair("down1", 0)
            sp.wait_ge(tile_done, TILE0["down1"])
            with sp.Fori(1, 9) as i:
                weight_pair("down1", i)
                sp.dma_start(XR[:, ds(i - 1, 1), :].rearrange("p a t -> p (a t)"), h_save[ds(i * P - P, P), :]
                             ).then_inc(x_reloaded, 16)
            with sp.Fori(9, 12) as i:
                weight_pair("down1", i)
            for h in range(2):
                tok = slice(512 * h, 512 * h + 512)
                for j in range(KB):
                    sp.wait_ge(norm_lo, 8 * (7 + h) + j + 1)
                    sp.dma_start(out[j * P:(j + 1) * P, tok], XR[:, j, tok]).then_inc(out_saved, 16)
            sp.wait_ge(out_saved, 16 * 2 * KB)

        @block.gpsimd
        def _(pool):
            pool.memset(ONES[:], 0.0)
            pool.memset(IDENT[:], 0.0)
            pool.memset(MASK[:], 1.0)
            pool.memset(RESET[:], 1.0)
            pool.drain()
            pool.affine_select(out=IDENT[:], in_=IDENT[:], compare_op=ALU.not_equal, fill=1.0, base=0,
                               pattern=[[-1, P]], channel_multiplier=1)
            pool.affine_select(out=ONES[:], in_=ONES[:], compare_op=ALU.is_ge, fill=-1e30, base=0,
                               pattern=[[1, P]], channel_multiplier=-1)
            for c in range(2):
                pool.drain()
                rows = MASK[CH * c:CH * c + CH, :]
                pool.affine_select(out=rows, in_=rows, compare_op=ALU.is_ge, fill=0.0, base=0,
                                   pattern=[[1, CH]], channel_multiplier=-1)
            pool.drain()
            pool.tensor_scalar(IDENT_R[:], IDENT[:], 1.0, 0.0, ALU.mult, ALU.add)
            pool.tensor_scalar(NEGMASK[:], ONES[:], 1.0, 0.0, ALU.mult, ALU.add)
            pool.drain()
            pool.memset(ONES[:], 1.0)
            pool.memset(TOUCH[:], 0.0)
            pool.memset(RESET[:].rearrange("p (n c) -> p n c", c=CH)[:, :, 0:1], 0.0)
            pool.drain().then_inc(consts_made, 1)

            def split_tile(t, r, n, first=False):
                pool.wait_ge(w_loaded[r], (t // 2) * 16 + 16 if isinstance(t, int) else t * 8 + (16 - 8 * r))
                if not first:
                    pool.wait_ge(tile_done, t - 1)
                pool.tensor_tensor(TOUCH[:, 0:2], TOUCH[:, 2:4], TOUCH[:, 4:6], ALU.add)
                pool.tensor_scalar(WH[:, r, 0:n], WRAW[:, r, 0:n], 1.0, 0.0, ALU.mult, ALU.add)
                pool.drain()
                pool.tensor_tensor(WL[:, r, 0:n], WRAW[:, r, 0:n], WH[:, r, 0:n].bitcast(F32),
                                   ALU.subtract).then_inc(w_split, 1)

            def s5_phasors(i, first):
                ec, es = (WK[:, 9, 512 * k:512 * k + 512].rearrange("p (j n) -> p j n", j=4) for k in range(2))
                if first:
                    pool.wait_ge(s5["parameters"], 1)
                    pool.wait_ge(m["y"], 4)
                    pool.memset(ec[:, :, 0:1], 1.0)
                    pool.memset(es[:, :, 0:1], 0.0)
                else:
                    pool.wait_ge(s5["phasors_used"], i)
                    pool.tensor_tensor(TOUCH[:, 0:2], TOUCH[:, 2:4], TOUCH[:, 4:6], ALU.add)
                for k in range(7):
                    w = 2 ** k
                    er, ei = (WK[:, 14, ds(i * 4 + 16 * (18 + 2 * k + q), 4)][:, :, None].to_broadcast([P, 4, w])
                              for q in range(2))
                    tmp = [WK[:, 10, 256 * q:256 * q + 256].rearrange("p (j n) -> p j n", j=4)[:, :, 0:w]
                           for q in range(4)]
                    lo_r, lo_i = ec[:, :, 0:w], es[:, :, 0:w]
                    pool.drain()
                    pool.tensor_tensor(tmp[0], lo_r, er, ALU.mult)
                    pool.tensor_tensor(tmp[1], lo_i, ei, ALU.mult)
                    pool.tensor_tensor(tmp[2], lo_r, ei, ALU.mult)
                    pool.tensor_tensor(tmp[3], lo_i, er, ALU.mult)
                    pool.drain()
                    pool.tensor_tensor(ec[:, :, w:2 * w], tmp[0], tmp[1], ALU.subtract)
                    pool.tensor_tensor(es[:, :, w:2 * w], tmp[2], tmp[3], ALU.add)
                pool.drain().then_inc(s5["phasors"], 1)

            for name, n, kbs in STREAM:
                if name == "glu_w":
                    s5_phasors(0, True)
                    with pool.Fori(1, 4) as i:
                        s5_phasors(i, False)
                t0 = TILE0[name]
                start = 0
                if t0 == 0:
                    split_tile(0, 0, kbs[0] * P, first=True)
                    split_tile(1, 1, kbs[1] * P, first=True)
                    start = 1
                with pool.Fori(start, n // 2) as i:
                    for r in range(2):
                        split_tile(i * 2 + (t0 + r), r, kbs[r] * P)

        @block.tensor
        def _(pe):
            def norm_sum(n, wb=0):
                if n in PE_NORMS:
                    for j in range(KB):
                        pe.wait_ge(norm_sq, 8 * n + j + 1)
                        for half in range(2):
                            mm = pe.matmul(PX[:, half, :], ONES[:], WK[:, wb + j % 3, 512 * half:512 * half + 512],
                                           start=j == 0, stop=j == KB - 1)
                        mm.then_inc(norm_used if j < KB - 1 else norm_ms, 1)
                    return
                pe.wait_ge(norm_acc, 7 * (DVE_NORMS.index(n) + 1))
                for half in range(2):
                    mm = pe.matmul(PX[:, half, :], ONES[:], WK[:, wb + 3, 512 * half:512 * half + 512],
                                   start=True, stop=True)
                mm.then_inc(norm_ms, 1)

            def product(t, r, s, kbs, xh, xl, first=True, last=True):
                pe.wait_ge(w_split, t + 1)
                for half in range(2):
                    tok = slice(512 * half, 512 * half + 512)
                    for k in range(kbs):
                        for n, (w, x) in enumerate(((WH, xh), (WH, xl), (WL, xh))):
                            mm = pe.matmul(PG[:, 2 * s + half, :], w[:, r, P * k:P * k + P], x[:, k, tok],
                                           start=first and k == 0 and n == 0,
                                           stop=last and k == kbs - 1 and n == 2)
                mm.then_inc(tile_done, 1)

            def products_by_block(t, kbs, xh, xl, ready, count, u):
                blocks = list(range(kbs))

                def run(n_blocks):
                    for _ in range(n_blocks):
                        k = blocks.pop(0)
                        for r in range(2):
                            if k == 0:
                                pe.wait_ge(w_split, t + r + 1)
                                if u:
                                    pe.wait_ge(slot_free[r], u)
                        pe.wait_ge(ready, count + k + 1)
                        for r in range(2):
                            for half in range(2):
                                tok = slice(512 * half, 512 * half + 512)
                                for n, (w, x) in enumerate(((WH, xh), (WH, xl), (WL, xh))):
                                    mm = pe.matmul(PG[:, 2 * r + half, :], w[:, r, P * k:P * k + P], x[:, k, tok],
                                                   start=k == 0 and n == 0, stop=k == kbs - 1 and n == 2)
                            if k == kbs - 1:
                                mm.then_inc(tile_done, 1)
                return run

            def first_products(t, kbs, *args):
                products_by_block(t, kbs, *args)(kbs)

            def next_units(t, u):
                parts = [(n, half, quarter) for n in range(2) for half in range(2) for quarter in range(2)]

                def fill(count):
                    for _ in range(count):
                        n, half, quarter = parts.pop(0)
                        if half == 0 and quarter == 0:
                            pe.wait_ge(w_split, t + n + 1)
                            pe.wait_ge(slot_free[n], u)
                        tok = slice(512 * half, 512 * half + 512)
                        for k in range(4 * quarter, 4 * quarter + 4):
                            for m_, (w, x) in enumerate(((WH, UH), (WH, UL), (WL, UH))):
                                mm = pe.matmul(PG[:, 2 * n + half, :], w[:, n, P * k:P * k + P], x[:, k, tok],
                                               start=k == 0 and m_ == 0, stop=k == KB - 1 and m_ == 2)
                        if half == 1 and quarter == 1:
                            mm.then_inc(tile_done, 1)
                return fill

            pe.wait_ge(consts_made, 1)
            norm_sum(0)

            def rg_block(i, i0):
                t = TILE0["rg_w"] + i * 2
                if i0:
                    first_products(t, KB, UH, UL, norm_lo, 0, 0)
                else:
                    for n in range(2):
                        pe.wait_ge(slot_free[n], i)
                        product(t + n, n, n, KB, UH, UL)
                pe.wait_ge(rg_conv, i + 1)
                if not i0:
                    pe.wait_ge(rg_sig, i * 2)
                for g in range(2):
                    for half in range(2):
                        mm = pe.matmul(PX[:, 2 * g + half, :], WK[:, 15, P * g:P * g + P],
                                       WK[:, 2, 512 * half:512 * half + 512], start=True, stop=True)
                mm.then_inc(rg_gates, 1)

            rg_block(0, True)
            with pe.Fori(1, 4) as i:
                rg_block(i, False)

            def la_core(la, i, nh, dk, kdt, vt, att, qe0, ke, qe1, S, v, kd, sqo, n_turn, fill):
                one = nh == 1
                pe.wait_ge(la["kd"], i + 1)
                for n, src in enumerate([*v, kd]):
                    b = 2 * (n % 2)
                    if n >= 2:
                        pe.wait_ge(la["turned_copied"], i * n_turn + n - 1)
                    for t in range(TT):
                        mm = pe.transpose(PX[:, b + t // 4, P * (t % 4):P * (t % 4) + P],
                                          WK[:, src, P * t:P * t + P], IDENT[:])
                    mm.then_inc(la["turned"], 1)
                fill(2)
                pe.wait_ge(la["turned_copied"], i * n_turn + n_turn)
                pe.wait_ge(la["keys"], i + 1)
                for hh in range(nh):
                    rows = slice(dk * hh, dk * hh + dk)
                    for t in range(TT):
                        for c in range(2):
                            at = P * t + CH * c
                            mm = pe.matmul(PX[CH * c:CH * c + 32, hh, CH * t:CH * t + CH],
                                           WK[rows, ke, at:at + 32], WK[rows, qe0, at:at + CH],
                                           start=True, stop=True)
                            q = 32 * (2 * t + c)
                            mm = pe.matmul(PX[CH * c + 32:CH * c + CH, hh, CH * t + 32:CH * t + CH],
                                           WK[rows, ke, at + 32:at + CH], WK[rows, qe1, q:q + 32],
                                           start=True, stop=True)
                mm.then_inc(la["scores"], 1)
                for g in range(2):
                    if g:
                        fill(2 if one else 1)
                        pe.wait_ge(la["state"], i * 2 + 1)
                    for t in range(4 * g, 4 * g + 4):
                        for c in range(2):
                            for hh in range(nh):
                                tok = slice(CH * c, CH * c + CH)
                                mm = pe.matmul(PX[dk * hh:dk * hh + dk, 2 + c, P * (t % 4):P * (t % 4) + P],
                                               WK[tok, kdt, P * t + dk * hh:P * t + dk * hh + dk],
                                               WK[tok, vt[hh], P * t:P * t + P], start=True, stop=True)
                    mm.then_inc(la["ds"], 1)
                fill(2 if one else 1)
                pe.wait_ge(la["attn"], i + 1)
                pe.wait_ge(la["state"], i * 2 + 2)
                for hh in range(nh):
                    if hh:
                        fill(1)
                        pe.wait_ge(la["y"], i * nh + hh)
                    for t in range(TT):
                        o = PX[:, t // 4, P * (t % 4):P * (t % 4) + P]
                        pe.matmul(o, WK[:, vt[hh], P * t:P * t + P], WK[:, att[hh], P * t:P * t + P],
                                  start=True, stop=False)
                        for c in range(2):
                            rows = slice(dk * hh, dk * hh + dk)
                            mm = pe.matmul(o[:, CH * c:CH * c + CH], WK[rows, S:S + 2, :].rearrange(
                                "p a t -> p (a t)")[:, P * (2 * t + c):P * (2 * t + c) + P],
                                WK[rows, qe0, P * t + CH * c:P * t + CH * c + CH], start=False, stop=c == 1)
                    mm.then_inc(la["o"], 1)
                    fill(0 if one else 1)
                    pe.wait_ge(la["sq"], i * nh + hh + 1)
                    for half in range(2):
                        mm = pe.matmul(PX[:, 2 + half, :], ONES[:], WK[:, sqo, 512 * half:512 * half + 512],
                                       start=True, stop=True)
                    mm.then_inc(la["ms"], 1)
                fill(2 if one else 1)

            def hg_head(i, last):
                t = TILE0["hg_w"] + i * 4
                for n in range(2, 4):
                    pe.wait_ge(slot_free[n % 2], i * 2 + (UNIT0["hg_w"] // 2 + n // 2))
                    product(t + n, n % 2, n % 2, KB, UH, UL)
                pe.wait_ge(slot_free[0], i * 2 + (UNIT0["hg_w"] // 2 + 2))
                la_core(hg, i, 1, 128, 12, [11], [13], 8, 10, 6, 14, [4], 7, 4, 2,
                        next_units(t + 4, i * 2 + (UNIT0["hg_w"] // 2 + 2)) if not last else
                        products_by_block(TILE0["out1_w"], KB, UH, UL, sp_lo, 0, UNIT0["out1_w"] // 2))

            for n in range(2):
                pe.wait_ge(slot_free[n], UNIT0["hg_w"] // 2)
                product(TILE0["hg_w"] + n, n, n, KB, UH, UL)
            with pe.Fori(0, 3) as i:
                hg_head(i, False)
            hg_head(3, True)

            with pe.Fori(1, 4) as i:
                for n in range(2):
                    pe.wait_ge(slot_free[n], UNIT0["out1_w"] // 2 + i)
                    product(TILE0["out1_w"] + i * 2 + n, n, n, KB, UH, UL)
            norm_sum(1)
            pe.wait_ge(ple_ready, 2)
            with pe.Fori(0, 4) as i:
                for n in range(2):
                    pe.wait_ge(slot_free[n], UNIT0["ple_w"] // 2 + i)
                    product(TILE0["ple_w"] + i * 2 + n, n, n, 2, PH, PL)
            first_products(TILE0["gate_w"], KB, UH, UL, norm_lo, 8, UNIT0["gate_w"] // 2)
            with pe.Fori(1, 4) as i:
                for n in range(2):
                    pe.wait_ge(slot_free[n], UNIT0["gate_w"] // 2 + i)
                    product(TILE0["gate_w"] + i * 2 + n, n, n, KB, UH, UL)
            norm_sum(2, 15)

            def partial(t, r, bank, kbs, x, first=True, last=True, w0=0):
                pe.wait_ge(w_split, t + 1)
                for k in range(kbs):
                    xh, xl = x(k)
                    for n, (w, v) in enumerate(((WH, xh), (WH, xl), (WL, xh))):
                        mm = pe.matmul(PG[:, bank, :], w[:, r, P * k:P * k + P], v,
                                       start=first and k == 0 and n == 0, stop=last and k == kbs - 1 and n == 2)
                return mm

            def u_half(h):
                return lambda k: (UH[:, k, 512 * h:512 * h + 512], UL[:, k, 512 * h:512 * h + 512])

            norm_sum(3)
            for h in range(2):
                pe.wait_ge(slot_free[h], UNIT0["misc_w"] // 2)
            for k in range(KB):
                if k % 4 == 0:
                    pe.wait_ge(w_split, TILE0["misc_w"] + k // 4 + 1)
                pe.wait_ge(norm_lo, 24 + k + 1)
                for h in range(2):
                    tok = slice(512 * h, 512 * h + 512)
                    for n, (w, x) in enumerate(((WH, UH), (WH, UL), (WL, UH))):
                        mm = pe.matmul(PG[:, 2 * h, :], w[:, k // 4, P * (k % 4):P * (k % 4) + P], x[:, k, tok],
                                       start=k == 0 and n == 0, stop=k == KB - 1 and n == 2)
                if k % 4 == 3:
                    mm.then_inc(tile_done, 1)
            pe.wait_ge(misc_out, 1)
            pe.wait_ge(small_loaded, 32)
            for b in range(2):
                for half in range(2):
                    mm = pe.matmul(PX[:, 2 * b + half, :], A2W[:, P * b:P * b + P],
                                   WK[0:16, 15, 512 * half:512 * half + 512], start=True, stop=True)
            mm.then_inc(gla_a2, 1)

            for i in range(2):
                u = UNIT0["gla_w"] // 2 + 3 * i
                t = TILE0["gla_w"] + 6 * i
                for n in range(0 if i == 0 else 2, 6):
                    pe.wait_ge(slot_free[n % 2], u + n // 2)
                    product(t + n, n % 2, n % 2, KB, UH, UL)
                la_core(gl, i, 2, 64, 10, [5, 6], [14, 16], 11, 13, 9, 17, [5, 6], 10, 4, 3, next_units(t + 6, u + 3))

            for b in range(2):
                for n in range(2, 6):
                    pe.wait_ge(slot_free[n % 2], UNIT0["ml_w"] // 2 + 3 * b + n // 2)
                    product(TILE0["ml_w"] + 6 * b + n, n % 2, n % 2, KB, UH, UL)
                if not b:
                    pe.wait_ge(m["exps"], 1)
                    for n, s_ in enumerate((12, 11)):
                        for t in range(TT):
                            mm = pe.transpose(PX[:, 0, 32 * n + 4 * t:32 * n + 4 * t + 4],
                                              WK[0:4, s_, P * t:P * t + P], IDENT[0:4, 0:4])
                    mm.then_inc(m["turned_rows"], 1)
                    pe.wait_ge(m["tok"], 1)
                if b:
                    pe.wait_ge(m["y"], 2 * b)
                for g in range(2):
                    rows = slice(32 + 32 * g, 36 + 32 * g)
                    for half in range(2):
                        mm = pe.matmul(PX[:, 2 * g + half, :], SEL[rows, 512 + P * b:512 + P * b + P],
                                       WK[rows, 13, 512 * half:512 * half + 512], start=True, stop=True)
                mm.then_inc(m["spread"], 1)
                fill = next_units(TILE0["ml_w"] + 6 * b + 6, UNIT0["ml_w"] // 2 + 3 * b + 3)
                fill(1)
                pe.wait_ge(m["kw"], b + 1)
                for n, src in enumerate((4, 5, 9)):
                    bk = 2 * (n % 2)
                    if n >= 2:
                        pe.wait_ge(m["turned_copied"], 3 * b + n - 1)
                    for t in range(TT):
                        mm = pe.transpose(PX[:, bk + t // 4, P * (t % 4):P * (t % 4) + P],
                                          WK[:, src, P * t:P * t + P], IDENT[:])
                    mm.then_inc(m["turned"], 1)
                fill(1)
                pe.wait_ge(m["turned_copied"], 3 * b + 3)
                for t in range(TT):
                    for hh in range(2):
                        kw = WK[:, 9, P * t + 64 * hh:P * t + 64 * hh + 64]
                        pe.matmul(PX[64 * hh:64 * hh + 64, 2 + t // 4, P * (t % 4):P * (t % 4) + P], kw,
                                  WK[:, 4 + hh, P * t:P * t + P], start=True, stop=True)
                        mm = pe.matmul(PX[64 * hh:64 * hh + 64, 0, t:t + 1], kw, ONES[:, 0:1],
                                       start=True, stop=True)
                mm.then_inc(m["ds"], 1)
                fill(1)
                pe.wait_ge(m["state"], b + 1)
                for hh in range(2):
                    head = 2 * b + hh
                    rows = slice(64 * hh, 64 * hh + 64)
                    if hh:
                        fill(1)
                        pe.wait_ge(m["y"], head)
                    for half in range(2):
                        pe.matmul(PX[:, half, :], SEL[0:4, P * head:P * head + P],
                                  WK[0:4, 13, 512 * half:512 * half + 512], start=True, stop=False)
                        pe.matmul(PX[:, half, :].rearrange("p (t c) -> p t c", c=P), IDENT_R[:],
                                  NEGMASK[:, None, :].to_broadcast([P, 4, P]), start=False, stop=True)
                    for t in range(TT):
                        mm = pe.matmul(PX[:, 2 + t // 4, P * (t % 4):P * (t % 4) + P],
                                       WK[rows, 3, P * t:P * t + P], WK[rows, 2, P * t:P * t + P],
                                       start=True, stop=True)
                    mm.then_inc(m["scores"], 1)
                    fill(1 if hh else 2)
                    pe.wait_ge(m["p"], head + 1)
                    for t in range(TT):
                        qw = WK[rows, 8, P * t:P * t + P]
                        o = PX[:, t // 4, P * (t % 4):P * (t % 4) + P]
                        pe.matmul(o, WK[:, 11, P * t:P * t + P], WK[:, 4 + hh, P * t:P * t + P],
                                  start=True, stop=False)
                        pe.matmul(o, qw, WK[rows, 10, P * t:P * t + P], start=False, stop=True)
                        d_ = PX[:, 2, t:t + 1]
                        pe.matmul(d_, WK[:, 11, P * t:P * t + P], ONES[:, 0:1], start=True, stop=False)
                        mm = pe.matmul(d_, qw, WK[rows, 19, ML_AT + 72 + t:ML_AT + 73 + t], start=False, stop=True)
                    mm.then_inc(m["num"], 1)
                    if not hh:
                        fill(1)
                    pe.wait_ge(m["h"], head + 1)
                    for t in range(TT):
                        mm = pe.transpose(PX[:, 2 + t // 4, P * (t % 4):P * (t % 4) + P],
                                          WK[:, 12, P * t:P * t + P], IDENT[:])
                    mm.then_inc(m["ht"], 1)

            for n in range(2, 4):
                pe.wait_ge(slot_free[n % 2], UNIT0["s5_w"] // 2 + n // 2)
                product(TILE0["s5_w"] + n, n % 2, n % 2, KB, UH, UL)

            def s5_block(i, first):
                pe.wait_ge(s5["g"], i + 1)
                if not first:
                    pe.wait_ge(s5["pre_gelu"], i)
                for l in range(8):
                    mm = pe.transpose(PX[:, l // 4, P * (l % 4):P * (l % 4) + P],
                                      WK[:, 12, :].rearrange("p (n l) -> p l n", l=8)[:, l, :], IDENT[:])
                mm.then_inc(s5["tok"], 1)
                for j in range(4):
                    for ri in range(2):
                        mm = pe.matmul(PX[32 * j:32 * j + 32, 2, 0:240],
                                       WK[:, 13, P * ri + 32 * j:P * ri + 32 * j + 32],
                                       WK[:, ri, 240 * j:240 * j + 240], start=ri == 0, stop=ri == 1)
                mm.then_inc(s5["resp"], 1)
                pe.wait_ge(s5["tok_copied"], i + 1)
                for g in range(8):
                    mm = pe.transpose(PX[:, g // 4, P * (g % 4):P * (g % 4) + P],
                                      WK[:, 5, P * g:P * g + P], IDENT[:])
                mm.then_inc(s5["u"], 1)
                pe.wait_ge(s5["resp_copied"], i + 1)
                for j in range(4):
                    for ri in range(2):
                        n = 2 * j + ri
                        mm = pe.transpose(PX[:, 2 + n // 4, P * (n % 4):P * (n % 4) + P],
                                          WK[:, ri, 240 * j:240 * j + P], IDENT[:])
                mm.then_inc(s5["gt"], 1)
                pe.wait_ge(s5["u_copied"], i + 1)
                pe.wait_ge(s5["gt_copied"], i + 1)
                for g in range(8):
                    j, rows = g // 2, slice(64 * (g % 2), 64 * (g % 2) + 64)
                    for ri in range(2):
                        n = 2 * j + ri
                        mm = pe.matmul(PX[rows, ri, P * j:P * j + P],
                                       WK[:, 4, P * n + 64 * (g % 2):P * n + 64 * (g % 2) + 64],
                                       WK[:, 6, P * g:P * g + P], start=True, stop=True)
                mm.then_inc(s5["v"], 1)
                for l in range(8):
                    mm = pe.transpose(PX[:, 2 + l // 4, P * (l % 4):P * (l % 4) + P],
                                      WK[:, 13, RESP + 16 * (7 - l):RESP + 16 * (7 - l) + P], IDENT[:])
                mm.then_inc(s5["kt"], 1)
                pe.wait_ge(s5["kt_copied"], i + 1)
                pe.wait_ge(s5["x"], i + 1)
                for g in range(8):
                    j, rows = g // 2, slice(64 * (g % 2), 64 * (g % 2) + 64)
                    o = PX[:, 2 + g % 2, P * j:P * j + P]
                    pe.matmul(o, WK[:, 6, P * g:P * g + P], WK[:, 3, P * g:P * g + P], start=True, stop=False)
                    for ri in range(2):
                        mm = pe.matmul(o, WK[rows, 8, 512 * ri + P * j:512 * ri + P * j + P],
                                       WK[rows, 2, 512 * ri + P * j:512 * ri + P * j + P],
                                       start=False, stop=ri == 1)
                mm.then_inc(s5["y"], 1)
                pe.wait_ge(s5["y_copied"], i + 1)
                for l in range(8):
                    mm = pe.transpose(PX[:, l // 4, P * (l % 4):P * (l % 4) + P],
                                      WK[:, 5, P * l:P * l + P], IDENT[:])
                mm.then_inc(s5["back"], 1)

            s5_block(0, True)
            with pe.Fori(1, 4) as i:
                s5_block(i, False)
            first_products(TILE0["glu_w"], 4, GH, GLO, glu_lo, 0, UNIT0["glu_w"] // 2)
            for n in range(2, 4):
                pe.wait_ge(slot_free[n % 2], UNIT0["glu_w"] // 2 + n // 2)
                product(TILE0["glu_w"] + n, n % 2, n % 2, 4, GH, GLO)

            for hf, name in enumerate(("mix0", "mix1")):
                with pe.Fori(0, 4) as i:
                    for n in range(6):
                        s_ = n % 2
                        t = i * 12 + (TILE0[name] + 2 * n)
                        pe.wait_ge(slot_free[s_], i * 3 + (UNIT0[name] // 2 + n // 2))
                        gate, proj = PG[:, 2 * s_, :], PG[:, 2 * s_ + 1, :]
                        tok = slice(512 * hf, 512 * hf + 512)
                        for k in range(12):
                            if k % 6 == 0:
                                pe.wait_ge(w_split, t + k // 6 + 1)
                            if k < 8:
                                o, xh, xl = gate, UH[:, k, tok], UL[:, k, tok]
                            else:
                                y = 4 * (n % 3) + k - 8
                                o, xh, xl = proj, YH[:, y, :], YL[:, y, :]
                            if k == 8:
                                pe.wait_ge(mix_lo, 12 * hf + 4 * (n % 3) + 4)
                            w = slice(P * (k % 6), P * (k % 6) + P)
                            for m_, (w_, x_) in enumerate(((WH, xh), (WH, xl), (WL, xh))):
                                mm = pe.matmul(o, w_[:, k // 6, w], x_, start=k in (0, 8) and m_ == 0,
                                               stop=k in (7, 11) and m_ == 2)
                            if k % 6 == 5:
                                mm.then_inc(tile_done, 1)
            first_products(TILE0["out2_w"], KB, UH, UL, sp_lo, 8, UNIT0["out2_w"] // 2)
            with pe.Fori(1, 4) as i:
                for n in range(2):
                    pe.wait_ge(slot_free[n], UNIT0["out2_w"] // 2 + i)
                    product(TILE0["out2_w"] + i * 2 + n, n, n, KB, UH, UL)
            norm_sum(4, 8)
            norm_sum(5)
            def hl(k):
                return HL1[:, k, :] if k < 16 else HL2[:, k - 16, :]

            for hf in range(2):
                up, down = f"up{hf}", f"down{hf}"
                if hf == 0:
                    for k in range(KB):
                        for g in range(2):
                            if k == 0:
                                pe.wait_ge(slot_free[0], UNIT0[up] // 2)
                                pe.wait_ge(w_split, TILE0[up] + g + 1)
                            pe.wait_ge(norm_lo, 40 + k + 1)
                            for m_, (w, x) in enumerate(((WH, UH), (WH, UL), (WL, UH))):
                                mm = pe.matmul(PG[:, g, :], w[:, g, P * k:P * k + P], x[:, k, 0:512],
                                               start=k == 0 and m_ == 0, stop=k == KB - 1 and m_ == 2)
                            if k == KB - 1:
                                mm.then_inc(tile_done, 1)
                    t = TILE0[up] + 2
                    pe.wait_ge(slot_free[1], UNIT0[up] // 2)
                    for g in range(2):
                        partial(t + g, g, 2 + g, 8, u_half(0)).then_inc(tile_done, 1)
                else:
                    pe.wait_ge(norm_lo, 56)
                with pe.Fori(1 - hf, 11) as i:
                    for n in range(2):
                        t = i * 4 + (TILE0[up] + 2 * n)
                        pe.wait_ge(slot_free[n], i + UNIT0[up] // 2)
                        for g in range(2):
                            partial(t + g, g, 2 * n + g, 8, u_half(hf)).then_inc(tile_done, 1)

                def down_pair(i):
                    for n in range(2):
                        pe.wait_ge(slot_free[n], i + UNIT0[down] // 2)
                        for b in range(2):
                            for q in range(3):
                                o = 6 * n + 3 * b + q
                                pe.wait_ge(ffn_lo, 22 * hf + min(8 * q + 8, 22))
                                partial(i * 12 + (TILE0[down] + o), o % 2, 2 * n + b, (8, 8, 6)[q],
                                        lambda k: (HH[:, 8 * q + k, :], hl(8 * q + k)),
                                        q == 0, q == 2).then_inc(tile_done, 1)

                if hf == 0:
                    with pe.Fori(0, 2) as i:
                        down_pair(i)
                else:
                    for i in range(2):
                        down_pair(i)
                        pe.wait_ge(norm_acc, 7 * (DVE_NORMS.index(6 + i) + 1))
                        pe.matmul(PX[:, i, :], ONES[:], WK[:, 19, 0:512], start=True, stop=True).then_inc(norm_ms, 1)

        @block.scalar
        def _(act):
            def square(n, j, pieces, wb=0):
                if j >= 3:
                    if n in PE_NORMS:
                        act.wait_ge(norm_used, 7 * PE_NORMS.index(n) + j - 2)
                    else:
                        act.wait_ge(norm_acc, 7 * DVE_NORMS.index(n) + max(1, j - 3))
                for tok, x in pieces:
                    ins = act.activation(WK[:, wb + j % 3, tok], x, ACT.Square)
                ins.then_inc(norm_sq, 1)

            def norm_root(n, wb=0):
                act.wait_ge(norm_ms, n + 1)
                act.activation(WK[:, wb + 4, :], aux(0), ACT.Ln, bias=vec("eps"), scale=1.0 / D)
                act.drain()
                act.activation(WK[:, wb + 4, :], WK[:, wb + 4, :], ACT.Exp, scale=-0.5).then_inc(norm_rs, 1)

            def norm_squares(n, src, wb=0, made=None):
                for j in range(KB):
                    if made is not None:
                        act.wait_ge(*made(j))
                    square(n, j, src(j), wb)
                norm_root(n, wb)

            def whole(x):
                return lambda j: [(slice(0, T), x[:, j, :])]

            def norm_split(m, shift=None, halves=1):
                for q in range(halves * KB):
                    j, tok = q % KB, slice(512 * (q // KB), 512 * (q // KB) + T // halves)
                    act.wait_ge(norm_t, 8 * m + q + 1)
                    act.activation(UH[:, j, tok], WK[:, 5 + q % 2, tok], ACT.Identity,
                                   bias=0.0 if shift is None else shift(j)).then_inc(norm_hi, 1)

            act.wait_ge(vec_loaded, 16)
            act.wait_ge(pre_dve, 1)
            tmp = VEC["tmp"]
            act.activation(CONST_V[:, tmp + 12:tmp + 24], CONST_V[:, tmp:tmp + 12], ACT.Exp).then_inc(pre_act, 1)
            norm_squares(0, whole(H), made=lambda j: (x_loaded[j // 2], 32))
            norm_split(0)
            act.wait_ge(c_loaded, 16)
            act.activation(C_ROW, C_ROW, ACT.Silu).then_inc(pre_act, 1)

            XP = wk(0, 2)
            with act.Fori(0, 4) as i:
                t = TILE0["rg_w"] + i * 2
                act.wait_ge(tile_done, t + 1)
                act.wait_ge(pre_dve, i + 2)
                act.activation(XP[:, 3:3 + T], slot(0), ACT.Copy).then_inc(slot_free[0], 1)
                act.wait_ge(tile_done, t + 2)
                act.activation(WK[:, 5, :], slot(1), ACT.Sigmoid).then_inc(rg_ogate, 1)
                act.wait_ge(rg_gates, i + 1)
                act.activation(WK[:, 3, :], aux(0), ACT.Sigmoid, bias=vec_at("rg_ba", i)).then_inc(rg_sig, 1)
                act.activation(WK[:, 4, :], aux(2), ACT.Sigmoid, bias=vec_at("rg_bx", i)).then_inc(rg_sig, 1)
                act.drain()
                act.activation(WK[:, 6, :], WK[:, 3, :], ACT.Tanh, scale=vec_at("rg_s8", i))
                act.activation(WK[:, 7, :], WK[:, 3, :], ACT.Exp, scale=vec_at("neg_rg_s8", i))
                act.drain()
                act.activation(WK[:, 8, :], WK[:, 7, :], ACT.Square).then_inc(rg_decay, 1)
                act.wait_ge(rg_q, i + 1)
                act.activation(WK[:, 8, :], WK[:, 8, :], ACT.Sqrt).then_inc(rg_mult, 1)

            def halves(s, lo):
                v = WK[:, s, :].rearrange("p (n c) -> p n c", c=CH)
                return v[:, :, 0:32] if lo else v[:, :, 32:CH]

            def half_row(s, k):
                return WK[:, s, 512 * k:512 * k + 512].rearrange("p (n c) -> p n c", c=32)

            def la_exps(la, i, b, bm, eb, ek, ed):
                act.wait_ge(la["gaps"], i + 1)
                act.activation(WK[:, ed, :], WK[:, ed, :], ACT.Exp)
                act.activation(WK[:, eb, :], WK[:, b, :], ACT.Exp)
                act.activation(half_row(bm, 1), half_row(bm, 0), ACT.Exp)
                act.activation(halves(ek, True), halves(b, True), ACT.Exp, scale=-1.0)
                act.activation(halves(ek, False), half_row(bm, 0), ACT.Exp, scale=-1.0).then_inc(la["exps"], 1)

            def la_rest(la, i, nh, n_turn, dst, sqo, rs):
                for n, s in enumerate(dst):
                    act.wait_ge(la["turned"], i * n_turn + n + 1)
                    act.activation(WK[:, s, :], aux(2 * (n % 2)), ACT.Copy).then_inc(la["turned_copied"], 1)
                for hh in range(nh):
                    act.wait_ge(la["o"], i * nh + hh + 1)
                    act.activation(WK[:, sqo, :], aux(0), ACT.Square).then_inc(la["sq"], 1)
                    act.wait_ge(la["ms"], i * nh + hh + 1)
                    act.activation(WK[:, rs, :], aux(2), ACT.Ln, bias=vec("eps"), scale=1.0 / P)
                    act.drain()
                    act.activation(WK[:, rs, :], WK[:, rs, :], ACT.Exp, scale=-0.5).then_inc(la["rs"], 1)

            act.wait_ge(rg_done, 4)
            def hg_head(i, last):
                t = TILE0["hg_w"] + i * 4
                act.wait_ge(tile_done, t + 1)
                act.activation(WK[:, 0, :], slot(0), ACT.Sigmoid)
                act.activation(WK[:, 2, :], slot(0), ACT.Sigmoid, scale=-1.0).then_inc(slot_free[0], 1)
                act.wait_ge(tile_done, t + 2)
                act.activation(WK[:, 3, :], slot(1), ACT.Sigmoid).then_inc(hg["sig"], 1)
                act.drain()
                act.activation(WK[:, 0, :], WK[:, 0, :], ACT.Ln, bias=vec_at("lb", i),
                               scale=vec_at("one_minus_lb", i)).then_inc(hg["logf"], 1)
                la_exps(hg, i, 1, 0, 9, 10, 7)
                act.wait_ge(tile_done, t + 3)
                act.activation(WK[:, 4, :], slot(0), ACT.Copy).then_inc(slot_free[0], 1)
                act.wait_ge(hg["free"], i + 1)
                act.wait_ge(tile_done, t + 4)
                act.activation(WK[:, 5, :], slot(1), ACT.Sigmoid).then_inc(hg["sig"], 1)
                if last:
                    act.wait_ge(hg["y"], 3)
                    for j in range(KB - 1):
                        act.activation(UH[:, j, :], H[:, j, :], ACT.Copy).then_inc(sp_hi, 1)
                la_rest(hg, i, 1, 2, [11, 12], 4, 1)

            with act.Fori(0, 3) as i:
                hg_head(i, False)
            hg_head(3, True)

            act.wait_ge(hg["y"], 4)
            act.activation(UH[:, KB - 1, :], H[:, KB - 1, :], ACT.Copy).then_inc(sp_hi, 1)
            for j in range(2):
                act.wait_ge(p_loaded[j], 16)
                act.activation(PH[:, j, :], WK[:, 19 - j, :], ACT.Copy).then_inc(ple_hi, 1)
            norm_squares(1, whole(H), made=lambda j: (slot_free[j % 2], UNIT0["out1_w"] // 2 + j // 2 + 1))
            with act.Fori(0, 4) as i:
                for n in range(2):
                    act.wait_ge(tile_done, i * 2 + (TILE0["ple_w"] + n + 1))
                    act.activation(WK[:, ds(i * 2 + (7 + n), 1), :].rearrange("p a t -> p (a t)"), slot(n),
                                   ACT.Copy).then_inc(slot_free[n], 1)
            norm_split(1)
            for j in range(KB):
                n = j % 2
                act.wait_ge(tile_done, TILE0["gate_w"] + j + 1)
                if j >= 2:
                    act.wait_ge(gate_added, j - 1)
                act.activation(WK[:, n, :], slot(n), ACT.Sigmoid, bias=vec("b_ple_gate", j)
                               ).then_inc(slot_free[n], 1)
                if j:
                    act.wait_ge(gate_added, j)
                    square(2, j - 1, whole(H)(j - 1), 15)
            act.wait_ge(gate_added, 8)
            square(2, 7, whole(H)(7), 15)
            norm_root(2, 15)

            act.wait_ge(gains_made, 1)
            norm_squares(3, whole(H), made=lambda j: (norm_lo, 16 + j + 1))
            norm_split(2, lambda j: MOD[:, j:j + 1])
            act.wait_ge(tile_done, TILE0["misc_w"] + 2)
            for half in range(2):
                act.activation(WK[:, 15, 512 * half:512 * half + 512], PG[:, 2 * half, :],
                               ACT.Copy).then_inc(slot_free[half], 1)
            act.drain().then_inc(misc_out, 1)
            act.wait_ge(gla_x, 1)
            for b in range(2):
                act.activation(WK[:, 2 + b, :], WK[:, 2 + b, :], ACT.Exp)
            act.drain()
            for b in range(2):
                act.activation(WK[:, 2 + b, :], WK[:, 2 + b, :], ACT.Ln, bias=vec("one")).then_inc(gla_ln, 1)

            with act.Fori(0, 2) as i:
                t = TILE0["gla_w"] + i * 6
                act.wait_ge(tile_done, t + 1)
                act.activation(WK[:, 4, :], slot(0), ACT.Copy).then_inc(slot_free[0], 1)
                act.wait_ge(gl["free"], i + 1)
                la_exps(gl, i, 2, 9, 12, 13, 10)
                for n in range(2):
                    act.wait_ge(tile_done, t + 3 + n)
                    act.activation(WK[:, 5 + n, :], slot(n), ACT.Copy).then_inc(slot_free[n], 1)
                for n in range(2):
                    act.wait_ge(tile_done, t + 5 + n)
                    act.activation(WK[:, 7 + n, :], slot(n), ACT.Silu).then_inc(slot_free[n], 1)
                la_rest(gl, i, 2, 3, [5, 6, 10], 4, 2)

            XQ, XK = wk(17, 2), wk(0, 2)
            for b in range(2):
                t = TILE0["ml_w"] + 6 * b
                if b:
                    act.wait_ge(s5["loaded"], 32)
                    act.activation(S5P(3), S5P(2), ACT.Exp).then_inc(s5["dt"], 1)
                    act.wait_ge(s5["angle"], 1)
                    act.activation(S5P(6), S5P(4), ACT.Exp)
                    act.activation(S5P(7), S5P(4), ACT.Exp, scale=8.0)
                    act.activation(S5P(10), S5P(9), ACT.Sin)
                    act.activation(S5P(11), S5P(9), ACT.Sin, scale=0.5)
                    act.drain().then_inc(s5["trig"], 1)
                for n, x in enumerate((XQ, XK)):
                    act.wait_ge(tile_done, t + 1 + n)
                    if b:
                        act.wait_ge(m["conv"], 2 * b)
                    act.activation(x[:, 3:3 + T], slot(n), ACT.Copy).then_inc(slot_free[n], 1)
                if not b:
                    act.wait_ge(m["rows"], 1)
                    act.activation(WK[0:4, 2, :], WK[0:4, 2, :], ACT.Exp)
                    act.drain()
                    act.activation(WK[0:4, 2, :], WK[0:4, 2, :], ACT.Ln, bias=CONST_V[0:4, VEC["one"]:VEC["one"] + 1]
                                   ).then_inc(m["ln"], 1)
                    act.wait_ge(m["gates"], 1)
                    act.activation(WK[32:36, 13, :], WK[0:4, 9, :], ACT.Exp)
                    act.activation(WK[64:68, 13, :], WK[0:4, 16, :], ACT.Exp)
                    act.activation(WK[0:4, 11, :], WK[0:4, 3, :], ACT.Exp, scale=-1.0).then_inc(m["exps"], 1)
                for n in range(2):
                    act.wait_ge(tile_done, t + 3 + n)
                    act.activation(WK[:, 4 + n, :], slot(n), ACT.Copy).then_inc(slot_free[n], 1)
                for n in range(2):
                    act.wait_ge(m["conv"], 2 * b + n + 1)
                    act.activation(WK[:, 2 + n, :], WK[:, 2 + n, :], ACT.Silu).then_inc(m["silu"], 1)
                for n in range(2):
                    act.wait_ge(tile_done, t + 5 + n)
                    act.activation(WK[:, 6 + n, :], slot(n), ACT.Sigmoid).then_inc(slot_free[n], 1)
                for n, s_ in enumerate((4, 5, 9)):
                    act.wait_ge(m["turned"], 3 * b + n + 1)
                    act.activation(WK[:, s_, :], aux(2 * (n % 2)), ACT.Copy).then_inc(m["turned_copied"], 1)
                for hh in range(2):
                    head = 2 * b + hh
                    act.wait_ge(m["scores"], head + 1)
                    for t in range(TT):
                        ins = act.activation(WK[:, 11, P * t:P * t + P], PX[:, t // 4, P * (t % 4):P * (t % 4) + P],
                                             ACT.Exp, bias=WK[:, 19, ML_AT + 4 * t + head:ML_AT + 4 * t + head + 1])
                    ins.then_inc(m["e"], 1)

            for n in range(4):
                act.wait_ge(tile_done, TILE0["s5_w"] + n + 1)
                act.activation(WK[:, 16 + n, :], slot(n % 2), ACT.Copy).then_inc(slot_free[n % 2], 1)
            with act.Fori(0, 4) as i:
                act.wait_ge(s5["tok"], i + 1)
                act.activation(WK[:, 5, :].rearrange("p (g l c) -> p l g c", g=8, l=8),
                               aux(0).rearrange("p (l g c) -> p l g c", g=8, l=8), ACT.Copy
                               ).then_inc(s5["tok_copied"], 1)
                act.wait_ge(s5["resp"], i + 1)
                act.activation(WK[:, 13, RESP:RESP + 240], PX[:, 2, 0:240], ACT.Copy).then_inc(s5["resp_copied"], 1)
                act.wait_ge(s5["u"], i + 1)
                act.activation(WK[:, 6, :], aux(0), ACT.Copy).then_inc(s5["u_copied"], 1)
                act.wait_ge(s5["gt"], i + 1)
                act.activation(WK[:, 4, :], aux(2), ACT.Copy).then_inc(s5["gt_copied"], 1)
                act.wait_ge(s5["kt"], i + 1)
                act.activation(WK[:, 3, :].rearrange("p (g l c) -> p l g c", g=8, l=8),
                               aux(2).rearrange("p (l g c) -> p l g c", g=8, l=8), ACT.Copy
                               ).then_inc(s5["kt_copied"], 1)
                act.wait_ge(s5["y"], i + 1)
                for b in range(2):
                    ins = act.activation(WK[:, 5, :].rearrange("p (l j g c) -> p g j l c", g=2, j=4, l=8)[:, b],
                                         PX[:, 2 + b, :].rearrange("p (j l c) -> p j l c", j=4, l=8), ACT.Copy)
                ins.then_inc(s5["y_copied"], 1)
                act.wait_ge(s5["pre_gelu"], i + 1)
                y = WK[:, ds(i + 16, 1), :].rearrange("p a t -> p (a t)")
                act.activation(y, y, ACT.Gelu_apprx_tanh)
            act.drain()
            for j in range(4):
                act.activation(GH[:, j, :], WK[:, 16 + j, :], ACT.Copy).then_inc(glu_hi, 1)
            for n in range(4):
                act.wait_ge(tile_done, TILE0["glu_w"] + n + 1)
                act.activation(WK[:, 8 + n, :], slot(n % 2), ACT.Sigmoid, bias=vec("glu_b", n)
                               ).then_inc(slot_free[n % 2], 1)

            for hf in range(2):
                tok = slice(512 * hf, 512 * hf + 512)
                if hf:
                    act.wait_ge(tile_done, TILE0["mix1"])
                for k in range(12):
                    if k == 8 and not hf:
                        act.wait_ge(glu_y, 4)
                    raw = H[:, k, tok] if k < 8 else WK[:, 8 + k, tok]
                    act.activation(YH[:, k, :], raw, ACT.Copy).then_inc(mix_hi, 1)
                with act.Fori(0, 4) as i:
                    for n in range(6):
                        s_ = n % 2
                        act.wait_ge(tile_done, i * 12 + (TILE0[f"mix{hf}"] + 2 * n + 2))
                        act.activation(WK[:, 13, 512 * s_:512 * s_ + 512], PG[:, 2 * s_, :], ACT.Sigmoid,
                                       bias=vec_at("branch_b", i * 2 + (8 * (n % 3) + n // 3))).then_inc(mix_sig, 1)

            act.wait_ge(m_ready, 16)
            for j in range(KB):
                act.activation(UH[:, j, :], H[:, j, :], ACT.Copy).then_inc(sp_hi, 1)
            for j in range(KB):
                act.wait_ge(tile_done, TILE0["out2_w"] + j + 1)
                act.activation(WK[:, j, :], slot(j % 2), ACT.Copy)
                if j >= 3:
                    act.wait_ge(norm_acc, 7 * DVE_NORMS.index(4) + max(1, j - 3))
                act.activation(WK[:, 8 + j % 3, :], slot(j % 2), ACT.Square).then_inc(slot_free[j % 2], 1)
                act.drain().then_inc(norm_sq, 1)
            norm_root(4, 8)
            norm_squares(5, whole(H), made=lambda j: (norm_lo, 32 + j + 1))
            norm_split(3, lambda j: MOD[:, 24 + j:25 + j], 2)

            for hf in range(2):
                with act.Fori(0, 11) as i:
                    for n in range(2):
                        act.wait_ge(tile_done, i * 4 + (TILE0[f"up{hf}"] + 2 * n + 1))
                        act.activation(WK[:, 18, 512 * n:512 * n + 512], PG[:, 2 * n, :], ACT.Silu
                                       ).then_inc(ffn_silu, 1)
                        act.wait_ge(ffn_t, i * 2 + (22 * hf + n + 1))
                        act.activation(HH[:, ds(i * 2 + n, 1), :].rearrange("p a t -> p (a t)"),
                                       WK[:, 19, 512 * n:512 * n + 512], ACT.Copy).then_inc(ffn_hi, 1)

                def down_copy(i, n):
                    act.wait_ge(tile_done, i * 12 + (TILE0[f"down{hf}"] + 6 * n + 6))
                    act.activation(YF[hf][:, ds(i * 4 + 2 * n, 2), :], PG[:, 2 * n:2 * n + 2, :], ACT.Copy
                                   ).then_inc(slot_free[n], 1)

                if hf == 0:
                    with act.Fori(0, 2) as i:
                        for n in range(2):
                            down_copy(i, n)

            def half_squares(h, j):
                if j >= 2:
                    act.wait_ge(norm_acc, 7 * DVE_NORMS.index(6 + h) + max(1, j - 2))
                act.activation(WK[:, 18, 512 * (j % 2):512 * (j % 2) + 512], YF[h][:, j, :], ACT.Square
                               ).then_inc(norm_sq, 1)

            def half_root(h):
                act.wait_ge(norm_ms, 6 + h + 1)
                rs = WK[:, 19, 512:1024]
                act.activation(rs, PX[:, h, :], ACT.Ln, bias=vec("eps"), scale=1.0 / D)
                act.drain()
                act.activation(rs, rs, ACT.Exp, scale=-0.5).then_inc(norm_rs, 1)

            act.drain()
            for j in range(KB):
                half_squares(0, j)
            for n in range(2):
                down_copy(0, n)
            half_root(0)
            for j in range(4):
                half_squares(1, j)
            for n in range(2):
                down_copy(1, n)
                act.drain()
                for j in range(2):
                    half_squares(1, 4 + 2 * n + j)
            half_root(1)

        @block.vector
        def _(dve):
            def norm_add(n, j, wb=0):
                dve.wait_ge(norm_sq, 8 * n + j + 1)
                a = WK[:, wb, :] if j == 1 else WK[:, wb + 3, :]
                dve.tensor_tensor(WK[:, wb + 3, :], a, WK[:, wb + j % 3, :], ALU.add).then_inc(norm_acc, 1)
                dve.drain()

            def norm_sum_blocks(n, wb=0):
                for j in range(1, KB):
                    norm_add(n, j, wb)

            def norm_residual(n, pieces, gain, res, wb):
                dve.wait_ge(norm_rs, n + 1)
                for j in range(KB):
                    for tok, x in pieces(j):
                        dve.scalar_tensor_tensor(WK[:, wb + 5 + j % 2, tok], x, gain(j), WK[:, wb + 4, tok],
                                                 ALU.mult, ALU.mult)
                    dve.drain()
                    dve.tensor_tensor(res[:, j, :], res[:, j, :], WK[:, wb + 5 + j % 2, :], ALU.add
                                      ).then_inc(norm_lo, 1)
                    dve.drain()

            def norm_split(n, m, src, gain, shift=None, halves=1):
                dve.wait_ge(norm_rs, n + 1)

                def where(q):
                    return q % KB, slice(512 * (q // KB), 512 * (q // KB) + T // halves)

                def low(q):
                    j, tok = where(q)
                    dve.wait_ge(norm_hi, 8 * m + q + 1)
                    dve.scalar_tensor_tensor(UL[:, j, tok], WK[:, 5 + q % 2, tok],
                                             vec("zero") if shift is None else shift(j),
                                             UH[:, j, tok].bitcast(F32), ALU.add, ALU.subtract).then_inc(norm_lo, 1)
                for q in range(halves * KB):
                    j, tok = where(q)
                    if q >= 2:
                        dve.drain()
                    dve.scalar_tensor_tensor(WK[:, 5 + q % 2, tok], src[:, j, tok], gain(j), WK[:, 4, tok],
                                             ALU.mult, ALU.mult).then_inc(norm_t, 1)
                    if q:
                        low(q - 1)
                low(halves * KB - 1)

            def horner(q, c, z2):
                dve.drain()
                dve.scalar_tensor_tensor(q, q, c, z2, ALU.add, ALU.mult)

            dve.memset(vecs("zero", 8), 0.0)
            dve.memset(vecs("eps", 1), EPS)
            dve.memset(vecs("one", 1), 1.0)
            dve.wait_ge(vec_loaded, 16)
            tmp = VEC["tmp"]
            q = [CONST_V[:, tmp + 4 * j:tmp + 4 * j + 4] for j in range(6)]
            lb0, lb1 = CONST_V[:, VEC["hg_lb"]:VEC["hg_lb"] + 4], CONST_V[:, VEC["hg_lb"] + 4:VEC["hg_lb"] + 8]
            lam = vecs("rg_lambda", 4)
            dve.tensor_tensor(q[3], lb0, lb1, ALU.max)
            dve.drain()
            dve.tensor_tensor(q[0], lb0, q[3], ALU.subtract)
            dve.tensor_tensor(q[1], lb1, q[3], ALU.subtract)
            dve.scalar_tensor_tensor(q[2], lam, -1.0, lam, ALU.mult, ALU.min)
            dve.drain().then_inc(pre_dve, 1)
            dve.wait_ge(pre_act, 1)
            dve.tensor_tensor(q[0], q[3], q[4], ALU.add)
            dve.drain()
            dve.reciprocal(q[0], q[0])
            dve.drain()
            dve.tensor_tensor(vecs("lb", 4), q[3], q[0], ALU.mult)
            dve.drain()
            dve.tensor_scalar(vecs("one_minus_lb", 4), vecs("lb", 4), -1.0, 1.0, ALU.mult, ALU.add)
            dve.tensor_scalar(q[1], q[5], 2.0, None, ALU.add)
            dve.drain()
            dve.reciprocal(q[1], q[1])
            dve.drain()
            dve.tensor_tensor(q[2], q[5], q[1], ALU.mult)
            dve.drain()
            dve.tensor_tensor(q[0], q[2], q[2], ALU.mult)
            dve.drain()
            dve.tensor_scalar(q[1], q[0], 1.0 / 15, None, ALU.mult)
            for k in (13, 11, 9, 7, 5, 3):
                horner(q[1], 1.0 / k, q[0])
            dve.drain()
            dve.scalar_tensor_tensor(q[2], q[1], 1.0, q[2], ALU.add, ALU.mult)
            dve.tensor_scalar(q[3], lam, -1.0, 0.0, ALU.mult, ALU.max)
            dve.drain()
            dve.scalar_tensor_tensor(q[1], q[2], 2.0, q[3], ALU.mult, ALU.add)
            dve.drain()
            dve.tensor_scalar(vecs("rg_s8", 4), q[1], 8.0, None, ALU.mult)
            dve.tensor_scalar(vecs("neg_rg_s8", 4), q[1], -8.0, None, ALU.mult)
            dve.drain()
            norm_sum_blocks(0)
            norm_split(0, 0, H, lambda j: vec("norm_mix_w", j))

            XP = wk(0, 2)
            XC = WK[:, 2, :]
            bd = wk(14)
            dve.drain()
            dve.memset(XP[:, 0:3], 0.0).then_inc(pre_dve, 1)
            dve.wait_ge(bd_loaded, 16)
            dve.wait_ge(pre_act, 2)

            def rg_conv_block(i, first):
                if not first:
                    dve.wait_ge(rg_gates, i)
                dve.tensor_copy(WK[:, 15, 0:2 * P], bd[:, ds(i * (2 * P), 2 * P)])
                dve.wait_ge(slot_free[0], i + 1)
                dve.tensor_scalar(XC, XP[:, 3:3 + T], vec_at("conv_w", i + 12), vec_at("conv_b", i),
                                  ALU.mult, ALU.add)
                for k in range(3):
                    dve.drain()
                    dve.scalar_tensor_tensor(XC, XP[:, k:k + T], vec_at("conv_w", i + 4 * k), XC,
                                             ALU.mult, ALU.add)
                dve.drain().then_inc(rg_conv, 1)

            def ada(i, in_rg, n):
                for j in range(n):
                    q = j % 3
                    dve.wait_ge(ada_loaded[q], (i * 16 if in_rg else i * 48 + 64) + 16 * (j // 3 + 1))
                    dve.scalar_tensor_tensor(ADA[:, q, :], ADA[:, q, :], 1.0, C_ROW, ALU.mult, ALU.mult,
                                             accum_out=MOD[:, ds((i * 3 if in_rg else i * 9 + 12) + j, 1)]
                                             ).then_inc(ada_done, 1)

            def rg_rest(i):
                dve.wait_ge(rg_ogate, i + 1)
                dve.tensor_tensor(WK[:, 5, :], slot(1), WK[:, 5, :], ALU.mult).then_inc(slot_free[1], 1)
                ada(i, True, 3)
                dve.wait_ge(rg_sig, i * 2 + 2)
                dve.tensor_tensor(WK[:, 9, :], WK[:, 4, :], XC, ALU.mult)
                dve.wait_ge(rg_decay, i + 1)
                dve.scalar_tensor_tensor(WK[:, 8, :], WK[:, 8, :], 1.0, WK[:, 6, :], ALU.add,
                                         ALU.mult).then_inc(rg_q, 1)
                dve.wait_ge(rg_mult, i + 1)
                dve.memset(WK[:, 8, 0:1], 1.0)
                dve.drain()
                dve.tensor_tensor(WK[:, 9, :], WK[:, 9, :], WK[:, 8, :], ALU.mult)
                dve.drain()
                dve.tensor_tensor_scan(WK[:, 10, :], WK[:, 7, :], WK[:, 9, :], 0.0, ALU.mult, ALU.add)
                dve.drain()
                dve.tensor_tensor(H[:, ds(i, 1), :].rearrange("p a t -> p (a t)"), WK[:, 10, :], WK[:, 5, :],
                                  ALU.mult).then_inc(rg_done, 1)
                dve.drain().then_inc(pre_dve, 1)

            rg_conv_block(0, True)
            rg_rest(0)
            with dve.Fori(1, 4) as i:
                rg_conv_block(i, False)
                rg_rest(i)

            def chunks(s, w=CH):
                return WK[:, s, :].rearrange("p (n c) -> p n c", c=w)

            def half_row(s, k):
                return WK[:, s, 512 * k:512 * k + 512].rearrange("p (n c) -> p n c", c=32)

            def la_gaps(la, b, bm, bd_, logf):
                dve.tensor_tensor_scan(WK[:, b, :], RESET[:], logf, 0.0, ALU.mult, ALU.add)
                dve.drain()
                B = chunks(b)
                dve.tensor_tensor(half_row(bm, 0), B[:, :, 32:CH], B[:, :, 31:32].to_broadcast([P, NCH, 32]),
                                  ALU.subtract)
                dve.tensor_tensor(chunks(bd_), B[:, :, CH - 1:CH].to_broadcast([P, NCH, CH]), B,
                                  ALU.subtract).then_inc(la["gaps"], 1)

            def la_core(la, i, nh, dk, att, S, eb):
                for hh in range(nh):
                    if hh == 0:
                        dve.wait_ge(la["scores"], i + 1)
                    for c in range(2):
                        rows = slice(CH * c, CH * c + CH)
                        out_ = WK[rows, att[hh], :].rearrange("p (t c) -> p t c", c=P)[:, :, CH * c:CH * c + CH]
                        ins = dve.tensor_tensor(out_, PX[rows, hh, :].rearrange("p (t c) -> p t c", c=CH),
                                                MASK[rows, None, :].to_broadcast([CH, TT, CH]), ALU.mult)
                ins.then_inc(la["attn"], 1)
                st = WK[:, S:S + 2, :].rearrange("p a t -> p (a t)")
                for n in range(NCH):
                    if n % 8 == 0:
                        dve.wait_ge(la["ds"], i * 2 + (n // 8 + 1))
                    if n < NCH - 1:
                        ins = dve.scalar_tensor_tensor(
                            st[:, P * (n + 1):P * (n + 2)], st[:, P * n:P * (n + 1)],
                            WK[:, eb, CH * n + CH - 1:CH * n + CH],
                            PX[:, 2 + n % 2, P * (n // 2 % 4):P * (n // 2 % 4) + P], ALU.mult, ALU.add)
                    if n % 8 == 7:
                        dve.drain().then_inc(la["state"], 1)
                    else:
                        dve.drain()

            dve.drain()
            dve.memset(WK[:, 14, 0:P], 0.0)
            dve.memset(WK[:, 13, :], 0.0)
            dve.drain().then_inc(hg["free"], 1)
            def out1_low(j):
                dve.wait_ge(sp_hi, j + 1)
                dve.tensor_tensor(UL[:, j, :], H[:, j, :], UH[:, j, :].bitcast(F32),
                                  ALU.subtract).then_inc(sp_lo, 1)

            def hg_head(i, last):
                dve.wait_ge(hg["sig"], i * 2 + 1)
                dve.scalar_tensor_tensor(WK[:, 3, :], slot(1), 128 ** -0.5, WK[:, 3, :], ALU.mult,
                                         ALU.mult).then_inc(slot_free[1], 1)
                dve.wait_ge(hg["logf"], i + 1)
                la_gaps(hg, 1, 0, 7, WK[:, 0, :])
                ada(i, False, 9)
                dve.wait_ge(hg["exps"], i + 1)
                k = vec_at("one_minus_lb", i)
                dve.scalar_tensor_tensor(WK[:, 7, :], WK[:, 2, :], k, WK[:, 7, :], ALU.mult,
                                         ALU.mult).then_inc(hg["kd"], 1)
                dve.tensor_tensor(WK[:, 8, :], WK[:, 3, :], WK[:, 9, :], ALU.mult)
                dve.tensor_tensor(half_row(6, 0), chunks(3)[:, :, 32:CH], half_row(0, 1), ALU.mult)
                dve.scalar_tensor_tensor(WK[:, 10, :], WK[:, 2, :], k, WK[:, 10, :], ALU.mult,
                                         ALU.mult).then_inc(hg["keys"], 1)
                dve.wait_ge(hg["sig"], i * 2 + 2)
                dve.tensor_tensor(WK[:, 5, :], slot(1), WK[:, 5, :], ALU.mult).then_inc(slot_free[1], 1)
                if last:
                    for j in range(KB - 1):
                        out1_low(j)
                la_core(hg, i, 1, 128, [13], 14, 9)
                dve.wait_ge(hg["rs"], i + 1)
                dve.scalar_tensor_tensor(WK[:, 9, :], aux(0), vec("hg_norm_w"), WK[:, 1, :], ALU.mult, ALU.mult)
                dve.drain()
                dve.tensor_tensor(H[:, ds(i + 4, 1), :].rearrange("p a t -> p (a t)"), WK[:, 9, :],
                                  WK[:, 5, :], ALU.mult).then_inc(hg["y"], 1)
                dve.drain().then_inc(hg["free"], 1)

            with dve.Fori(0, 3) as i:
                hg_head(i, False)
            hg_head(3, True)

            out1_low(KB - 1)

            def h_at(j):
                return H[:, ds(j, 1), :].rearrange("p a t -> p (a t)")

            for j in range(2):
                dve.wait_ge(ple_hi, j + 1)
                dve.tensor_tensor(PL[:, j, :], WK[:, 19 - j, :], PH[:, j, :].bitcast(F32),
                                  ALU.subtract).then_inc(ple_ready, 1)
            for j in range(KB):
                dve.wait_ge(tile_done, TILE0["out1_w"] + j + 1)
                dve.wait_ge(x_loaded[j // 2], 2 * 32)
                dve.tensor_tensor(H[:, j, :], H[:, j, :], slot(j % 2), ALU.add).then_inc(slot_free[j % 2], 1)
                if j >= 2:
                    norm_add(1, j - 1)
            norm_add(1, KB - 1)
            norm_split(1, 1, H, lambda j: vec("ple_norm_w", j))
            for j in range(KB):
                n = j % 2
                dve.wait_ge(slot_free[n], UNIT0["gate_w"] // 2 + j // 2 + 1)
                dve.tensor_tensor(WK[:, n, :], WK[:, n, :], WK[:, 7 + j, :], ALU.mult)
                dve.drain()
                dve.tensor_tensor(H[:, j, :], H[:, j, :], WK[:, n, :], ALU.add).then_inc(gate_added, 1)
                if j >= 2:
                    norm_add(2, j - 1, 15)
            norm_add(2, KB - 1, 15)
            dve.tensor_tensor(MOD[:], MOD[:], vecs("ada_b", 48), ALU.add)
            dve.drain()
            for g, at, w in (("pre1", 8, "pre1"), ("post1", 16, "post1"), ("pre2", 32, "pre2"), ("post2", 40, "post2")):
                dve.scalar_tensor_tensor(vecs(g + "_g", 8), MOD[:, at:at + 8], 1.0, vecs(w + "_w", 8),
                                         ALU.add, ALU.mult)
            dve.drain().then_inc(gains_made, 1)
            dve.wait_ge(norm_rs, 3)
            for j in range(KB):
                dve.scalar_tensor_tensor(H[:, j, :], H[:, j, :], vec("final_norm_w", j), WK[:, 19, :],
                                         ALU.mult, ALU.mult).then_inc(norm_lo, 1)

            norm_split(3, 2, H, lambda j: vec("pre1_g", j), lambda j: MOD[:, j:j + 1])
            dve.wait_ge(gla_a2, 1)
            for b in range(2):
                dve.tensor_scalar(WK[:, b, :], aux(2 * b), vec("gla_a_b", b), None, ALU.add)
            dve.drain()
            for b in range(2):
                dve.scalar_tensor_tensor(WK[:, 2 + b, :], WK[:, b, :], -1.0, WK[:, b, :], ALU.mult, ALU.min)
            dve.drain().then_inc(gla_x, 1)
            dve.memset(WK[:, 14, :], 0.0)
            dve.memset(WK[:, 16, :], 0.0)
            dve.memset(WK[:, 17, 0:P], 0.0)
            for b in range(2):
                dve.wait_ge(gla_ln, b + 1)
                dve.scalar_tensor_tensor(WK[:, b, :], WK[:, b, :], 0.0, WK[:, 2 + b, :], ALU.min, ALU.subtract)
            dve.drain()
            for b in range(2):
                dve.tensor_scalar(WK[:, b, :], WK[:, b, :], 1.0 / 16, None, ALU.mult)
            dve.wait_ge(h_saved, 16 * KB)
            dve.drain().then_inc(gl["free"], 1)
            with dve.Fori(0, 2) as i:
                dve.wait_ge(gl["free"], i + 1)
                dve.wait_ge(tile_done, i * 6 + (TILE0["gla_w"] + 2))
                dve.tensor_scalar(WK[:, 3, :], slot(1), 0.125, None, ALU.mult).then_inc(slot_free[1], 1)
                la_gaps(gl, 2, 9, 10, WK[:, ds(i, 1), :].rearrange("p a t -> p (a t)"))
                dve.drain()
                dve.wait_ge(gl["exps"], i + 1)
                dve.tensor_tensor(WK[:, 11, :], WK[:, 3, :], WK[:, 12, :], ALU.mult)
                dve.tensor_tensor(half_row(9, 0), chunks(3)[:, :, 32:CH], half_row(9, 1), ALU.mult)
                dve.wait_ge(slot_free[1], i * 3 + (UNIT0["gla_w"] // 2 + 2))
                dve.tensor_tensor(WK[:, 10, :], WK[:, 4, :], WK[:, 10, :], ALU.mult).then_inc(gl["kd"], 1)
                dve.tensor_tensor(WK[:, 13, :], WK[:, 4, :], WK[:, 13, :], ALU.mult).then_inc(gl["keys"], 1)
                la_core(gl, i, 2, 64, [14, 16], 17, 12)
                for hh in range(2):
                    dve.wait_ge(gl["rs"], i * 2 + hh + 1)
                    dve.scalar_tensor_tensor(WK[:, 3, :], aux(0), vec_at("gla_norm_w", i * 2 + hh), WK[:, 2, :],
                                             ALU.mult, ALU.mult)
                    dve.drain()
                    dve.tensor_tensor(h_at(i * 2 + hh), WK[:, 3, :], WK[:, 7 + hh, :], ALU.mult
                                      ).then_inc(gl["y"], 1)
                    dve.drain()
                dve.drain().then_inc(gl["free"], 1)

            def row(s):
                return WK[0:4, s, :]

            def tiles(s):
                return row(s).rearrange("p (t c) -> p t c", c=P)

            ip, x, ln, M, Bc, reset, A, mprev, ib = 10, 7, 2, 3, 4, 5, 6, 8, 12
            bias = VEC["ml_if_b"]
            dve.tensor_scalar(row(ip), WK[32:36, 15, :], CONST_V[32:36, bias:bias + 1], None, ALU.add)
            dve.tensor_scalar(row(x), WK[64:68, 15, :], CONST_V[64:68, bias:bias + 1], None, ALU.add)
            dve.drain()
            dve.scalar_tensor_tensor(row(ln), row(x), -1.0, row(x), ALU.mult, ALU.min)
            dve.drain().then_inc(m["rows"], 1)
            dve.memset(row(reset), 1.0)
            dve.memset(row(mprev)[:, 0:TT], 0.0)
            dve.drain()
            dve.memset(tiles(reset)[:, :, 0:1], 0.0)
            dve.wait_ge(m["ln"], 1)
            dve.scalar_tensor_tensor(row(x), row(x), 0.0, row(ln), ALU.min, ALU.subtract)
            dve.drain()
            dve.tensor_tensor_scan(row(M), row(x), row(ip), 0.0, ALU.add, ALU.max)
            dve.tensor_tensor_scan(row(Bc), row(reset), row(x), 0.0, ALU.mult, ALU.add)
            dve.drain()
            dve.tensor_tensor(row(A), row(Bc), row(M), ALU.subtract)
            dve.tensor_tensor(row(ib), row(ip), row(Bc), ALU.subtract)
            dve.tensor_copy(row(mprev)[:, 1:TT], tiles(M)[:, 0:TT - 1, P - 1])
            dve.drain()
            dve.tensor_tensor(tiles(9), tiles(A), row(mprev)[:, 0:TT, None].to_broadcast([4, TT, P]), ALU.add)
            dve.tensor_tensor(tiles(16), tiles(ib), tiles(A)[:, :, P - 1:P].to_broadcast([4, TT, P]), ALU.add)
            dve.tensor_copy(row(13), row(A))
            dve.drain()
            XQ, XK = wk(17, 2), wk(0, 2)
            dve.memset(XQ[:, 0:3], 0.0)
            dve.memset(XK[:, 0:3], 0.0)
            dve.drain().then_inc(m["gates"], 1)

            def tt(out_, a, b, op):
                dve.tensor_tensor(out_, a, b, op)

            def cmul(outr, outi, a, b, tmp, neg_i=False):
                tt(tmp[0], a[0], b[0], ALU.mult)
                tt(tmp[1], a[1], b[1], ALU.mult)
                tt(tmp[2], a[0], b[1], ALU.mult)
                tt(tmp[3], a[1], b[0], ALU.mult)
                dve.drain()
                tt(outr, tmp[0], tmp[1], ALU.subtract)
                if neg_i:
                    dve.scalar_tensor_tensor(outi, tmp[2], -1.0, tmp[3], ALU.mult, ALU.subtract)
                else:
                    tt(outi, tmp[2], tmp[3], ALU.add)
                dve.drain()

            def s5_parameters():
                dve.wait_ge(s5["dt"], 1)
                lr, li, dt, u, th = S5P(0), S5P(1), S5P(3), S5P(4), S5P(5)
                ta, tb, r = S5P(8), S5P(16), S5P(9)
                dve.tensor_scalar(lr, lr, -1e-4, None, ALU.min)
                tt(th, li, dt, ALU.mult)
                dve.drain()
                tt(u, lr, dt, ALU.mult)
                dve.tensor_scalar(ta, th, TURN_INV, ROUND, ALU.mult, ALU.add)
                dve.drain()
                dve.tensor_scalar(ta, ta, -ROUND, None, ALU.add)
                dve.drain()
                src = th
                for part in TURN:
                    dve.scalar_tensor_tensor(r, ta, -part, src, ALU.mult, ALU.add)
                    dve.drain()
                    src = r
                dve.tensor_scalar(r, r, PI, -PI, ALU.min, ALU.max)
                dve.drain().then_inc(s5["angle"], 1)
                tt(ta, lr, lr, ALU.mult)
                tt(tb, li, li, ALU.mult)
                dve.drain()
                tt(ta, ta, tb, ALU.add)
                dve.drain()
                dve.reciprocal(ta, ta)
                dve.wait_ge(s5["trig"], 1)
                mag, mag8, sn, cs, ar, ai, zr, zi = (S5P(k) for k in (6, 7, 10, 11, 12, 13, 14, 15))
                tt(cs, cs, cs, ALU.mult)
                dve.drain()
                dve.tensor_scalar(cs, cs, -2.0, 1.0, ALU.mult, ALU.add)
                dve.drain()
                tt(ar, mag, cs, ALU.mult)
                tt(ai, mag, sn, ALU.mult)
                dve.drain()
                t4 = [WK[:, 16, 256 * k:256 * k + 16] for k in range(4)]
                dve.tensor_scalar(tb, ar, -1.0, None, ALU.add)
                dve.drain()
                tt(t4[0], tb, lr, ALU.mult)
                tt(t4[1], ai, li, ALU.mult)
                tt(t4[2], ai, lr, ALU.mult)
                tt(t4[3], tb, li, ALU.mult)
                dve.drain()
                tt(zr, t4[0], t4[1], ALU.add)
                tt(zi, t4[2], t4[3], ALU.subtract)
                dve.drain()
                tt(zr, zr, ta, ALU.mult)
                tt(zi, zi, ta, ALU.mult)
                dve.drain()

                def pairs(at):
                    return WK[:, 15, at:at + 256].rearrange("p (j c) -> p j c", c=16)

                def over_c(x):
                    return x[:, :, None].to_broadcast([P, 16, 16])
                tb4 = [WK[:, 16, 256 * k:256 * k + 256].rearrange("p (j c) -> p j c", c=16) for k in range(4)]
                cmul(pairs(0), pairs(256), (pairs(0), pairs(256)), (over_c(zr), over_c(zi)), tb4)
                def table(k):
                    return WK[:, 14, 512 + 128 * k:640 + 128 * k].rearrange("p (j l) -> p j l", l=8)
                fr, fi, rr, ri_ = (table(k) for k in range(4))
                dve.memset(rr[:, :, 7:8], 1.0)
                dve.memset(ri_[:, :, 7:8], 0.0)
                dve.tensor_copy(fr[:, :, 0], ar)
                dve.tensor_copy(fi[:, :, 0], ai)
                dve.drain()
                for l in range(1, 8):
                    cmul(fr[:, :, l], fi[:, :, l], (fr[:, :, l - 1], fi[:, :, l - 1]), (ar, ai), t4)
                    dve.tensor_copy(rr[:, :, 7 - l], fr[:, :, l - 1])
                    dve.tensor_copy(ri_[:, :, 7 - l], fi[:, :, l - 1])
                e = [(S5P(18 + 2 * k), S5P(19 + 2 * k)) for k in range(7)]
                cmul(ta, tb, (cs, sn), (cs, sn), t4)
                cmul(ta, tb, (ta, tb), (ta, tb), t4)
                cmul(*e[0], (ta, tb), (ta, tb), t4)
                for k in range(1, 7):
                    cmul(*e[k], e[k - 1], e[k - 1], t4)
                dve.drain().then_inc(s5["parameters"], 1)

            def conv(xp, out_, j):
                dve.tensor_scalar(out_, xp[:, 3:3 + T], vec("ml_conv_w", 12 + j), vec("ml_conv_b", j),
                                  ALU.mult, ALU.add)
                for k in range(3):
                    dve.drain()
                    dve.scalar_tensor_tensor(out_, xp[:, k:k + T], vec("ml_conv_w", 4 * k + j), out_,
                                             ALU.mult, ALU.add)
                dve.drain().then_inc(m["conv"], 1)

            dec, den = WK[:, 19, ML_AT + 64:ML_AT + 72], WK[:, 19, ML_AT + 80:ML_AT + 88]
            for b in range(2):
                if b:
                    s5_parameters()
                for n, xp in enumerate((XQ, XK)):
                    dve.wait_ge(slot_free[n], UNIT0["ml_w"] // 2 + 3 * b + 1)
                    if not b:
                        dve.wait_ge(m["exps"], 1)
                    conv(xp, WK[:, 2 + n, :], 2 * n + b)
                if not b:
                    dve.wait_ge(m["turned_rows"], 1)
                    dve.tensor_copy(WK[:, 19, ML_AT:ML_AT + 64], PX[:, 0, 0:64]).then_inc(m["tok"], 1)
                    dve.memset(WK[:, 10, 0:P], 0.0)
                    dve.memset(WK[:, 19, ML_AT + 72:ML_AT + 73], 0.0)
                dve.wait_ge(m["silu"], 2 * b + 2)
                dve.wait_ge(m["spread"], b + 1)
                dve.tensor_tensor(WK[:, 8, :], WK[:, 2, :], aux(0), ALU.mult)
                dve.tensor_copy(dec, aux(0).rearrange("p (t c) -> p t c", c=P)[:, :, P - 1])
                dve.scalar_tensor_tensor(WK[:, 9, :], WK[:, 3, :], 0.125, aux(2), ALU.mult, ALU.mult)
                dve.drain()
                dve.tensor_scalar(WK[:, 3, :], WK[:, 3, :], 0.125, None, ALU.mult).then_inc(m["kw"], 1)
                dve.wait_ge(m["ds"], b + 1)
                for t in range(TT - 1):
                    dve.scalar_tensor_tensor(WK[:, 10, P * (t + 1):P * (t + 2)], WK[:, 10, P * t:P * (t + 1)],
                                             dec[:, t:t + 1], PX[:, 2 + t // 4, P * (t % 4):P * (t % 4) + P],
                                             ALU.mult, ALU.add)
                    dve.drain()
                dve.tensor_tensor_scan(WK[:, 19, ML_AT + 73:ML_AT + 80], dec[:, 0:7], PX[:, 0, 0:7], 0.0,
                                       ALU.mult, ALU.add)
                dve.drain().then_inc(m["state"], 1)
                for hh in range(2):
                    head = 2 * b + hh
                    dve.wait_ge(m["e"], head + 1)
                    dve.tensor_tensor(WK[:, 11, :], WK[:, 11, :], aux(2), ALU.mult).then_inc(m["p"], 1)
                    dve.wait_ge(m["num"], head + 1)
                    dve.tensor_scalar(den, PX[:, 2, 0:TT], -1.0, None, ALU.mult)
                    dve.drain()
                    dve.tensor_tensor(den, den, PX[:, 2, 0:TT], ALU.max)
                    dve.drain()
                    em = WK[:, 19, ML_AT + 32:ML_AT + 64].rearrange("p (t h) -> p t h", h=4)[:, :, head]
                    dve.tensor_tensor(den, den, em,
                                      ALU.max)
                    dve.drain()
                    dve.reciprocal(den, den)
                    dve.drain()
                    dve.tensor_tensor(WK[:, 12, :].rearrange("p (t c) -> p t c", c=P),
                                      aux(0).rearrange("p (t c) -> p t c", c=P),
                                      den[:, :, None].to_broadcast([P, TT, P]), ALU.mult).then_inc(m["h"], 1)
                    dve.wait_ge(m["ht"], head + 1)
                    dve.tensor_tensor(H[:, 4 + head, :], aux(2), WK[:, 6 + hh, :], ALU.mult).then_inc(m["y"], 1)


            def half(s_, h):
                return WK[:, s_, 512 * h:512 * h + 512].rearrange("p (j l c) -> p j l c", j=4, l=8)

            def seq(s_, h):
                return WK[:, s_, 512 * h:512 * h + 512].rearrange("p (j n) -> p j n", j=4)

            def bc(x):
                return x.rearrange("p (j c) -> p j c", c=16)[:, :, None, :].to_broadcast([P, 4, 8, 16])

            def pw(i, k):
                return WK[:, 14, ds(i * 32 + (512 + 128 * k), 32)].rearrange("p (j l) -> p j l", l=8)[
                    :, :, :, None].to_broadcast([P, 4, 8, 16])

            def coef(i, k):
                return WK[:, 15, ds(i * 64 + 256 * k, 64)]

            def padded(s_):
                return WK[:, s_, 0:960].rearrange("p (j l c) -> p j l c", j=4, l=15)[:, :, 0:8, :]

            tmp4 = [PG[:, 0, :], WK[:, 11, 0:512], PG[:, 2, :], WK[:, 11, 512:1024]]
            t4_ = [x.rearrange("p (j l c) -> p j l c", j=4, l=8) for x in tmp4]
            q4 = [x.rearrange("p (j n) -> p j n", j=4) for x in tmp4]
            ec, es = seq(7, 0), seq(7, 1)
            mt = WK[:, 13, 256:768]
            mtj = mt.rearrange("p (j n) -> p j n", j=4)

            def s5_tables(i):
                for ri in range(2):
                    for g in range(2):
                        rows = slice(64 * g, 64 * g + 64)
                        dve.tensor_scalar(
                            WK[rows, 13, P * ri:P * ri + P].rearrange("p (j g c) -> p j g c", g=2, c=16)[:, :, g],
                            coef(i, 2 + ri)[rows].rearrange("p (j c) -> p j c", c=16), 1.0 - 2.0 * ri, None, ALU.mult)
                cmul(padded(0), padded(1), (bc(coef(i, 0)), bc(coef(i, 1))), (pw(i, 2), pw(i, 3)), t4_)

            def s5_input(i):
                dve.tensor_copy(WK[:, 12, :], WK[:, ds(i + 16, 1), :].rearrange("p a t -> p (a t)")
                                ).then_inc(s5["g"], 1)
                dve.tensor_copy(mtj[:, :, 1:P],
                                WK[:, 14, ds(i * 4 + 16 * 7, 4)][:, :, None].to_broadcast([P, 4, P - 1]))

            def s5_phasors(i):
                dve.wait_ge(s5["phasors"], i + 1)
                dve.tensor_copy(WK[:, 7, :], WK[:, 9, :]).then_inc(s5["phasors_used"], 1)
                dve.drain()

            def s5_readout(i):
                cmul(half(2, 0), half(2, 1), (bc(coef(i, 2)), bc(coef(i, 3))), (pw(i, 0), pw(i, 1)), t4_)

            def s5_states(i):
                dve.wait_ge(s5["v"], i + 1)
                vr, vi = (PX[:, k, :].rearrange("p (j n) -> p j n", j=4)[:, :, 0:P - 1] for k in range(2))
                c1, s1 = ec[:, :, 1:P], es[:, :, 1:P]
                q1 = [x[:, :, 1:P] for x in q4]
                tt(q1[0], c1, vr, ALU.mult)
                tt(q1[1], s1, vi, ALU.mult)
                tt(q1[2], c1, vi, ALU.mult)
                tt(q1[3], s1, vr, ALU.mult)
                dve.drain()
                W = [PG[:, k, :].rearrange("p (j n) -> p j n", j=4) for k in (1, 3)]
                tt(W[0][:, :, 1:P], q1[0], q1[1], ALU.add)
                tt(W[1][:, :, 1:P], q1[2], q1[3], ALU.subtract)
                for k in range(2):
                    dve.memset(W[k][:, :, 0:1], 0.0)
                dve.drain()
                for k in (1, 3):
                    w_ = PG[:, k, :]
                    dve.tensor_tensor_scan(w_, mt, w_, 0.0, ALU.mult, ALU.add)
                dve.drain()
                cmul(seq(8, 0), seq(8, 1), (ec, es), (W[0], W[1]), q4, neg_i=True)
                dve.drain().then_inc(s5["x"], 1)

            def s5_output(i):
                dve.wait_ge(s5["back"], i + 1)
                y = WK[:, ds(i + 16, 1), :].rearrange("p a (n l) -> p (a l) n", l=8)
                dve.scalar_tensor_tensor(y, y, vec_at("s5_d", i), aux(0).rearrange("p (l n) -> p l n", l=8),
                                         ALU.mult, ALU.add).then_inc(s5["pre_gelu"], 1)

            dve.drain()
            dve.memset(WK[:, 0:2, :], 0.0)
            dve.memset(WK[:, 13, 0:768], 0.0)
            dve.drain()
            for n in range(2):
                dve.wait_ge(slot_free[n], UNIT0["s5_w"] // 2 + 2)
            s5_tables(0)
            s5_input(0)
            s5_readout(0)
            with dve.Fori(0, 3) as i:
                s5_phasors(i)
                s5_states(i)
                s5_tables(i + 1)
                s5_input(i + 1)
                s5_output(i)
                s5_readout(i + 1)
            s5_phasors(3)
            s5_states(3)
            s5_output(3)
            for j in range(4):
                dve.wait_ge(glu_hi, j + 1)
                dve.tensor_tensor(GLO[:, j, :], WK[:, 16 + j, :], GH[:, j, :].bitcast(F32), ALU.subtract
                                  ).then_inc(glu_lo, 1)
            for n in range(4):
                dve.wait_ge(slot_free[n % 2], UNIT0["glu_w"] // 2 + n // 2 + 1)
                dve.tensor_tensor(WK[:, 16 + n, :], WK[:, 16 + n, :], WK[:, 8 + n, :], ALU.mult).then_inc(glu_y, 1)

            dve.drain()
            for hf in range(2):
                tok = slice(512 * hf, 512 * hf + 512)
                for k in range(12):
                    dve.wait_ge(mix_hi, 12 * hf + k + 1)
                    raw = H[:, k, tok] if k < 8 else WK[:, 8 + k, tok]
                    dve.tensor_tensor(YL[:, k, :], raw, YH[:, k, :].bitcast(F32), ALU.subtract).then_inc(mix_lo, 1)
                with dve.Fori(0, 4) as i:
                    for n in range(6):
                        s_ = n % 2
                        g = WK[:, 13, 512 * s_:512 * s_ + 512]
                        tmp_ = WK[:, 14, 512 * s_:512 * s_ + 512]
                        M_ = H[:, ds(i * 2 + n // 3, 1), tok].rearrange("p a t -> p (a t)")
                        dve.wait_ge(mix_sig, i * 6 + (24 * hf + n + 1))
                        dve.wait_ge(tile_done, i * 12 + (TILE0[f"mix{hf}"] + 2 * n + 2))
                        dve.tensor_tensor(tmp_ if n % 3 else M_, g, PG[:, 2 * s_ + 1, :], ALU.mult
                                          ).then_inc(slot_free[s_], 1)
                        dve.drain()
                        if n % 3:
                            ins = dve.tensor_tensor(M_, M_, tmp_, ALU.add)
                            if n % 3 == 2:
                                ins.then_inc(m_ready, 1)
                            dve.drain()
            for j in range(KB):
                dve.wait_ge(sp_hi, 8 + j + 1)
                dve.tensor_tensor(UL[:, j, :], H[:, j, :], UH[:, j, :].bitcast(F32),
                                  ALU.subtract).then_inc(sp_lo, 1)
            norm_sum_blocks(4, 8)
            dve.wait_ge(h_reloaded, 16 * KB)
            norm_residual(4, lambda j: [(slice(0, T), WK[:, j, :])], lambda j: vec("post1_g", j), H, 8)
            norm_split(5, 3, H, lambda j: vec("pre2_g", j), lambda j: MOD[:, 24 + j:25 + j], 2)

            dve.wait_ge(h_saved, 16 * 2 * KB)
            for hf in range(2):
                for HL, i0, i1 in ((HL1, 0, 8), (HL2, 8, 11)):
                    with dve.Fori(i0, i1) as i:
                        for n in range(2):
                            g = WK[:, 18, 512 * n:512 * n + 512]
                            t_ = WK[:, 19, 512 * n:512 * n + 512]
                            dve.wait_ge(ffn_silu, i * 2 + (22 * hf + n + 1))
                            dve.wait_ge(tile_done, i * 4 + (TILE0[f"up{hf}"] + 2 * n + 2))
                            dve.tensor_tensor(t_, g, PG[:, 2 * n + 1, :], ALU.mult).then_inc(slot_free[n], 1)
                            dve.drain().then_inc(ffn_t, 1)
                            dve.wait_ge(ffn_hi, i * 2 + (22 * hf + n + 1))
                            dve.tensor_tensor(HL[:, ds(i * 2 + (n - 2 * i0), 1), :].rearrange("p a t -> p (a t)"), t_,
                                              HH[:, ds(i * 2 + n, 1), :].rearrange("p a t -> p (a t)").bitcast(F32),
                                              ALU.subtract).then_inc(ffn_lo, 1)
                            dve.drain()
            for h in range(2):
                tok = slice(512 * h, 512 * h + 512)
                acc, rs = WK[:, 19, 0:512], WK[:, 19, 512:1024]
                for j in range(1, KB):
                    dve.wait_ge(norm_sq, 8 * (6 + h) + j + 1)
                    dve.tensor_tensor(acc, WK[:, 18, 0:512] if j == 1 else acc,
                                      WK[:, 18, 512 * (j % 2):512 * (j % 2) + 512], ALU.add).then_inc(norm_acc, 1)
                    dve.drain()
                if h == 0:
                    dve.wait_ge(x_reloaded, 16 * KB)
                dve.wait_ge(norm_rs, 6 + h + 1)
                for j in range(KB):
                    y = YF[h][:, j, :]
                    dve.scalar_tensor_tensor(y, y, vec("post2_g", j), rs, ALU.mult, ALU.mult)
                    dve.drain()
                    dve.tensor_tensor(XR[:, j, tok], XR[:, j, tok], y, ALU.add).then_inc(norm_lo, 1)


def pack_weight(w, kbs=8):
    import numpy as np
    k, n = w.shape
    return np.ascontiguousarray(w.reshape(k // P, P, n // P, P).transpose(2, 1, 0, 3).reshape(n // P, P, k))


def pack_vectors(v):
    import numpy as np
    cols = []
    for name, n in VEC_SPEC:
        a = np.asarray(v[name]).reshape(-1)
        cols.append(a.reshape(n, P).T)
    return np.ascontiguousarray(np.concatenate(cols, axis=1))


def layout(inp):
    import numpy as np
    f = {k: np.asarray(v) for k, v in inp.items()}
    w_in = f["w_in"][0]
    blk = {n: w_in[:, 512 * j:512 * (j + 1)] for j, n in enumerate(("xa", "ga", "q", "f", "i", "g"))}

    def cols(name, j):
        return blk[name][:, P * j:P * (j + 1)]
    rg = np.concatenate([cols(n, j) for j in range(4) for n in ("xa", "ga")], axis=1)
    hg = np.concatenate([cols(n, j) for j in range(4) for n in ("f", "q", "i", "g")], axis=1)
    bd = np.zeros((P, 4, 2, P), np.float32)
    for j in range(4):
        for k, w in enumerate((f["rg_wa"][0], f["rg_wx"][0])):
            for g in range(2):
                bd[64 * g:64 * g + 64, j, k, 64 * g:64 * g + 64] = w[2 * j + g]
    names = (("gq", 256), ("gk", 256), ("gv", 512), ("ga", 16), ("gr", 512), ("mq", 256), ("mk", 256), ("mv", 512),
             ("mi", 4), ("mf", 4), ("mo", 512), ("su", 512), ("zg", 3072))
    at, w2 = 0, {}
    for n, k in names:
        w2[n] = f["w_in_2"][0][:, at:at + k]
        at += k

    def c2(name, j):
        return w2[name][:, P * j:P * (j + 1)]
    misc = np.zeros((D, P), np.float32)
    for n, o in (("ga", 0), ("mi", 32), ("mf", 64)):
        misc[:, o:o + w2[n].shape[1]] = w2[n]
    misc = pack_weight(misc)[0].reshape(P, 2, 4 * P).transpose(1, 0, 2)
    gla = np.concatenate([c2(n, j) for b in range(2) for n, j in (
        ("gk", b), ("gq", b), ("gv", 2 * b), ("gv", 2 * b + 1), ("gr", 2 * b), ("gr", 2 * b + 1))], axis=1)
    ml = np.concatenate([c2(n, j) for b in range(2) for n, j in (
        ("mq", b), ("mk", b), ("mv", 2 * b), ("mv", 2 * b + 1), ("mo", 2 * b), ("mo", 2 * b + 1))], axis=1)
    pr = [f["proj_gla_2"][0], f["proj_ml_2"][0], f["proj_s5_2"][0]]
    mix = np.concatenate([np.concatenate([c2("zg", 8 * br + j), pr[br][:, P * j:P * (j + 1)]])
                          for j in range(8) for br in range(3)], axis=1)
    mix = pack_weight(mix).reshape(24, P, 2, 6 * P).transpose(0, 2, 1, 3).reshape(48, P, 6 * P)
    hidden = f["ffn_w_out_2"].shape[1]
    up = f["ffn_w_in_2"][0]
    up = np.concatenate([up[:, o + P * j:o + P * (j + 1)] for j in range(hidden // P) for o in (0, hidden)], axis=1)
    down = np.zeros((3 * D, D), np.float32)
    down[:hidden] = f["ffn_w_out_2"][0]
    down = pack_weight(down).reshape(KB, P, 3, D).transpose(0, 2, 1, 3).reshape(3 * KB, P, D)
    if_b = np.zeros((P,), np.float32)
    if_b[32:36], if_b[64:68] = f["ml_i_b_2"][0], f["ml_f_b_2"][0]
    sel = np.zeros((P, 6 * P), np.float32)
    for h in range(4):
        sel[h, P * h:P * (h + 1)] = 1.0
        for r in (32, 64):
            sel[r + h, 4 * P + 64 * h:4 * P + 64 * (h + 1)] = 1.0

    def states(a):
        return a.reshape(16, P, -1).transpose(1, 0, 2).reshape(P, -1)
    bc = [states(f[k][0]) for k in ("s5_b_re_2", "s5_b_im_2")]
    bc += [states(f[k][0].transpose(0, 2, 1)) for k in ("s5_c_re_2", "s5_c_im_2")]
    lam = [states(f[k][0]) for k in ("s5_lam_re_2", "s5_lam_im_2")]
    lam += [states(np.repeat(f["s5_log_step_2"][0], 64))]
    v = {**f, "ml_if_b": if_b, "glu_b": f["s5_glu_b_2"], "branch_b": f["branch_gate_b_2"]}
    for n in ("ada_b", "pre1_w", "post1_w", "pre2_w", "post2_w", "gla_a_b", "gla_norm_w", "ml_conv_w", "ml_conv_b",
              "s5_d"):
        v[n] = f[n + "_2"]
    arrays = {
        "x": f["x"][0].T, "p": f["p"][0, 0].T, "vec": pack_vectors(v), "rg_bd": bd.reshape(P, 8 * P),
        "rg_w": pack_weight(rg), "hg_w": pack_weight(hg), "out1_w": pack_weight(f["w_out"][0]),
        "ple_w": pack_weight(f["w_ple_proj"][0]), "gate_w": pack_weight(f["w_ple_gate"][0]),
        "ada_w": f["ada_w_2"][0].T.reshape(6 * KB, P, D), "c_row": np.repeat(f["c_2"], P, axis=0),
        "misc_w": misc, "gla_w": pack_weight(gla), "ml_w": pack_weight(ml), "s5_w": pack_weight(w2["su"]),
        "glu_w": pack_weight(f["s5_glu_w_2"][0]), "mix_w": mix,
        "out2_w": pack_weight(f["w_out_2"][0]), "up_w": pack_weight(up), "down_w": down,
        "gla_a2": f["gla_a2_2"][0], "sel": sel, "s5_bc": np.concatenate(bc, axis=1),
        "s5_lam": np.concatenate(lam, axis=1),
    }
    return {k: np.ascontiguousarray(a) for k, a in arrays.items()}


def build(nc, names, *aps):
    program(nc, dict(zip(names, aps)), aps[-1])


def kernel(**inputs):
    import numpy as np
    import concourse.bacc as bacc
    from concourse.bass_utils import run_bass_kernel_spmd

    nc = bacc.Bacc("TRN2", target_bir_lowering=False, num_devices=1)
    arrays = layout(inputs)
    aps = [nc.dram_tensor(name, a.shape, mybir.dt.from_np(a.dtype), kind="ExternalInput").ap()
           for name, a in arrays.items()]
    out = nc.dram_tensor("out", (D, T), F32, kind="ExternalOutput").ap()
    build(nc, list(arrays), *aps, out)
    r = run_bass_kernel_spmd(nc, [arrays], core_ids=[0])
    return np.ascontiguousarray(r.results[0]["out"].T)[None]
```
